# Optimizing a Trainium2 kernel written in Bass

```python
import math, functools
import jax, jax.numpy as jnp
from jax import lax
import numpy as np

D_MODEL = 1024
BATCH = 1
SEQ = 1024
DEPTH = 1
DEC_BATCH = 8
DEC_SEQ = 8
PAST_LEN = 2048
PAGE_SIZE = 128

ATT_HEADS = 8
KV_HEADS = 4
HEAD_DIM = 64
ATT_WIDTH = ATT_HEADS * HEAD_DIM
ROT_DIM = HEAD_DIM // 4
ROPE_THETA = 500000.0
IDX_HEADS = 8
IDX_DIM = 64
IDX_ROT_DIM = IDX_DIM // 4
TOPK_MAX = 256
Q_BLOCK = 128
HG_HEADS = 4
HG_DK = 128
HG_DV = 128
HG_WIDTH = HG_HEADS * HG_DV
HG_CHUNK = 64
MIX_WIDTH = ATT_WIDTH + HG_WIDTH
PROJ_SIZES = (ATT_WIDTH,
              KV_HEADS * HEAD_DIM,
              KV_HEADS * HEAD_DIM,
              IDX_HEADS * IDX_DIM,
              IDX_DIM,
              IDX_HEADS,
              HG_HEADS * HG_DK,
              HG_HEADS * HG_DK,
              HG_WIDTH,
              HG_WIDTH)
N_IN = (ATT_WIDTH + 2 * KV_HEADS * HEAD_DIM + IDX_HEADS * IDX_DIM + IDX_DIM + IDX_HEADS
        + 2 * HG_HEADS * HG_DK + 2 * HG_WIDTH)
N_GROUPS = 4
EXPERTS_PER_GROUP = 4
N_EXPERTS = N_GROUPS * EXPERTS_PER_GROUP
TOP_K_INNER = 2
D_EXPERT = 512
MOE_BLOCK = 256
EPS = 1e-6

kernel_name = "hymba_dsa_hgrn2_hmoe_adaln_step"

def _rmsnorm(x, g):
    xf = x.astype(jnp.float32)
    y = xf * lax.rsqrt(jnp.mean(xf * xf, axis=-1, keepdims=True) + EPS)
    return (y * g.astype(jnp.float32)).astype(x.dtype)

def _ada(c, w, b, n):
    m = jnp.einsum('bd,de->be', jax.nn.silu(c), w) + b
    return jnp.split(m[:, None, :], n, axis=-1)

def _rope_partial(x, pos, rot_dim):
    half = rot_dim // 2
    inv_freq = ROPE_THETA ** (-jnp.arange(half, dtype=jnp.float32) * (2.0 / rot_dim))
    ang = pos.astype(jnp.float32)[:, None] * inv_freq[None, :]
    cos, sin = jnp.cos(ang)[:, None, :], jnp.sin(ang)[:, None, :]
    xr = x[..., :rot_dim].astype(jnp.float32)
    x1, x2 = xr[..., :half], xr[..., half:]
    rot = jnp.concatenate([x1 * cos - x2 * sin, x2 * cos + x1 * sin], axis=-1).astype(x.dtype)
    return jnp.concatenate([rot, x[..., rot_dim:]], axis=-1)

def _project(h, w_in, idx_k_g, pos):
    B, T, _ = h.shape
    z = jnp.einsum('btd,de->bte', h, w_in)
    pts, acc = [], 0
    for s in PROJ_SIZES[:-1]:
        acc += s
        pts.append(acc)
    q, k, v, qi, ki, wi, hq, hf, hi, hg = jnp.split(z, pts, axis=-1)
    q = _rope_partial(q.reshape(B, T, ATT_HEADS, HEAD_DIM), pos, ROT_DIM)
    k = _rope_partial(k.reshape(B, T, KV_HEADS, HEAD_DIM), pos, ROT_DIM)
    v = v.reshape(B, T, KV_HEADS, HEAD_DIM)
    qi = _rope_partial(qi.reshape(B, T, IDX_HEADS, IDX_DIM), pos, IDX_ROT_DIM)
    ki = _rope_partial(_rmsnorm(ki, idx_k_g)[:, :, None, :], pos, IDX_ROT_DIM)[:, :, 0, :]
    wi = wi * (IDX_HEADS ** -0.5)
    return q, k, v, qi, ki, wi, hq, hf, hi, hg

def _select_attend(q, qi, wi, ki_all, q_pos, gather_kv):
    B, Tq = q.shape[:2]
    L = ki_all.shape[1]
    topk = min(TOPK_MAX, L // 4)
    s = jnp.einsum('bqhd,bsd->bqhs', qi.astype(jnp.float32), ki_all.astype(jnp.float32)) * (IDX_DIM ** -0.5)
    score = jnp.einsum('bqhs,bqh->bqs', jax.nn.relu(s), wi.astype(jnp.float32))
    admissible = jnp.arange(L)[None, :] <= q_pos[:, None]
    score = jnp.where(admissible[None], score, -jnp.inf)
    _, sel = lax.top_k(score, topk)
    valid = sel <= q_pos[None, :, None]
    k_sel, v_sel = gather_kv(sel)
    qg = q.reshape(B, Tq, KV_HEADS, ATT_HEADS // KV_HEADS, HEAD_DIM).astype(jnp.float32)
    logits = jnp.einsum('bqhgd,bqkhd->bqhgk', qg, k_sel.astype(jnp.float32)) * (HEAD_DIM ** -0.5)
    logits = jnp.where(valid[:, :, None, None, :], logits, -jnp.inf)
    p = jax.nn.softmax(logits, axis=-1)
    o = jnp.einsum('bqhgk,bqkhd->bqhgd', p, v_sel.astype(jnp.float32))
    return o.reshape(B, Tq, ATT_WIDTH).astype(q.dtype)

def _prompt_attention(q, k, v, qi, wi, ki):
    B, T = q.shape[:2]
    nb = T // Q_BLOCK
    b_idx = jnp.arange(B)[:, None, None]

    def gather(sel):
        return k[b_idx, sel], v[b_idx, sel]

    def split_blocks(a):
        return a.reshape(B, nb, Q_BLOCK, *a.shape[2:]).swapaxes(0, 1)

    def blk(args):
        qb, qib, wib, posb = args
        return _select_attend(qb, qib, wib, ki, posb, gather)

    out = lax.map(blk, (split_blocks(q), split_blocks(qi), split_blocks(wi),
                        jnp.arange(T).reshape(nb, Q_BLOCK)))
    return out.swapaxes(0, 1).reshape(B, T, ATT_WIDTH)

def _sample_attention(q, k_new, v_new, qi, wi, ki_new, cache_k_l, cache_v_l, cache_ki_l, page_table):
    DB, T = q.shape[:2]
    n_pages = PAST_LEN // PAGE_SIZE
    past = n_pages * PAGE_SIZE
    ki_past = cache_ki_l[page_table].reshape(DB, past, IDX_DIM).astype(ki_new.dtype)
    ki_all = jnp.concatenate([ki_past, ki_new], axis=1)
    q_pos = past + jnp.arange(T)
    b_idx = jnp.arange(DB)[:, None, None]

    def gather(sel):
        in_past = (sel < past)[..., None, None]
        ps = jnp.minimum(sel, past - 1)
        phys = page_table[b_idx, ps // PAGE_SIZE]
        off = ps % PAGE_SIZE
        ns = jnp.clip(sel - past, 0, T - 1)
        kk = jnp.where(in_past, cache_k_l[phys, off].astype(k_new.dtype), k_new[b_idx, ns])
        vv = jnp.where(in_past, cache_v_l[phys, off].astype(v_new.dtype), v_new[b_idx, ns])
        return kk, vv

    return _select_attend(q, qi, wi, ki_all, q_pos, gather)

def _gla_chunked(q, k, v, log_f, s0):
    B, T, H, DK = q.shape
    C = min(HG_CHUNK, T)
    pad = (-T) % C
    if pad:
        pw = ((0, 0), (0, pad), (0, 0), (0, 0))
        q, k, v, log_f = (jnp.pad(a, pw) for a in (q, k, v, log_f))
    n = (T + pad) // C

    def blocks(a):
        return a.reshape(B, n, C, H, a.shape[-1]).transpose(1, 0, 3, 2, 4)

    q, k, v, log_f = blocks(q), blocks(k), blocks(v), blocks(log_f)
    b = jnp.cumsum(log_f, axis=3)
    b_last = b[:, :, :, -1]
    q_in = q * jnp.exp(b)
    k_in = k * jnp.exp(-b)
    k_st = k * jnp.exp(b_last[:, :, :, None] - b)
    causal = jnp.tril(jnp.ones((C, C), dtype=bool))
    att = jnp.where(causal, jnp.einsum('nbhtd,nbhsd->nbhts', q_in, k_in), 0.0)
    intra = jnp.einsum('nbhts,nbhse->nbhte', att, v)

    def step(S, inp):
        qc, kc, vc, blc, ic = inp
        o = jnp.einsum('bhtd,bhde->bhte', qc, S) + ic
        S = jnp.exp(blc)[..., None] * S + jnp.einsum('bhsd,bhse->bhde', kc, vc)
        return S, o

    s_T, o = lax.scan(step, s0, (q_in, k_st, v, b_last, intra))
    o = o.transpose(1, 0, 3, 2, 4).reshape(B, n * C, H, HG_DV)[:, :T]
    return o, s_T

def _hgrn2(hq, hf, hi, hg, lb, out_g, s0):
    B, T, _ = hq.shape
    q = hq.astype(jnp.float32).reshape(B, T, HG_HEADS, HG_DK) * (HG_DK ** -0.5)
    f = lb + (1.0 - lb) * jax.nn.sigmoid(hf.astype(jnp.float32))
    f = f.reshape(B, T, HG_HEADS, HG_DK)
    k = 1.0 - f
    v = hi.astype(jnp.float32).reshape(B, T, HG_HEADS, HG_DV)
    o, s_T = _gla_chunked(q, k, v, jnp.log(f), s0.astype(jnp.float32))
    o = _rmsnorm(o, out_g.reshape(HG_HEADS, HG_DV)).reshape(B, T, HG_WIDTH)
    o = o * jax.nn.silu(hg.astype(jnp.float32))
    return o.astype(hq.dtype), s_T.astype(s0.dtype)

def _expert_dispatch(xf, experts, weights, w1, w3, w2):
    N, D = xf.shape
    K = experts.shape[1]
    A = N * K
    flat_e = experts.reshape(-1)
    order = jnp.argsort(flat_e)
    se = flat_e[order]
    counts = jnp.bincount(flat_e, length=N_EXPERTS)
    padded = (counts + MOE_BLOCK - 1) // MOE_BLOCK * MOE_BLOCK
    pad_end = jnp.cumsum(padded)
    pad_start = pad_end - padded
    start = jnp.cumsum(counts) - counts
    dest = pad_start[se] + jnp.arange(A) - start[se]
    n_blocks = -(-A // MOE_BLOCK) + N_EXPERTS
    rows = n_blocks * MOE_BLOCK
    tok_of_assign = (order // K).astype(jnp.int32)
    tok = jnp.full((rows,), N, dtype=jnp.int32).at[dest].set(tok_of_assign)
    xpad = jnp.concatenate([xf, jnp.zeros((1, D), xf.dtype)], axis=0)
    xin = xpad[tok].reshape(n_blocks, MOE_BLOCK, D)
    blk_e = jnp.minimum(jnp.searchsorted(pad_end, jnp.arange(n_blocks) * MOE_BLOCK, side='right'),
                        N_EXPERTS - 1)

    def run(args):
        xb, e = args
        return (jax.nn.silu(xb @ w1[e]) * (xb @ w3[e])) @ w2[e]

    yb = lax.map(run, (xin, blk_e)).reshape(rows, D)
    contrib = yb[dest] * weights.reshape(-1)[order][:, None].astype(yb.dtype)
    return jnp.zeros((N, D), yb.dtype).at[tok_of_assign].add(contrib)

def _moe(h, w_group, b_group, w_er, b_er, w1, w3, w2):
    B, T, D = h.shape
    xf = h.reshape(-1, D)
    N = xf.shape[0]
    gp = jax.nn.softmax((xf @ w_group + b_group).astype(jnp.float32), axis=-1)
    g_w, g_sel = lax.top_k(gp, 1)
    elog = (xf @ w_er + b_er).astype(jnp.float32).reshape(N, N_GROUPS, EXPERTS_PER_GROUP)
    elog_g = jnp.take_along_axis(elog, g_sel[:, :, None], axis=1)[:, 0]
    e_w, e_sel = lax.top_k(jax.nn.softmax(elog_g, axis=-1), TOP_K_INNER)
    e_w = e_w / jnp.sum(e_w, axis=-1, keepdims=True)
    weights = g_w * e_w
    experts = g_sel * EXPERTS_PER_GROUP + e_sel
    return _expert_dispatch(xf, experts, weights, w1, w3, w2).reshape(B, T, D)

def _block(x, c, pos, s0, attend, lb, ada_w, ada_b, norm1_g, norm2_g, w_in, idx_k_g, attn_out_g,
           hg_out_g, w_out, w_group, b_group, w_er, b_er, w1, w3, w2):
    sh1, sc1, gt1, sh2, sc2, gt2 = _ada(c, ada_w, ada_b, 6)
    h = _rmsnorm(x, norm1_g) * (1.0 + sc1) + sh1
    q, k, v, qi, ki, wi, hq, hf, hi, hg = _project(h, w_in, idx_k_g, pos)
    a = _rmsnorm(attend(q, k, v, qi, wi, ki), attn_out_g)
    r, s_T = _hgrn2(hq, hf, hi, hg, lb, hg_out_g, s0)
    mix = jnp.einsum('bte,ed->btd', jnp.concatenate([a, r], axis=-1), w_out)
    x = x + gt1 * mix
    h = _rmsnorm(x, norm2_g) * (1.0 + sc2) + sh2
    x = x + gt2 * _moe(h, w_group, b_group, w_er, b_er, w1, w3, w2)
    return x, k, v, ki, s_T

def _final(x, c, g, w, b):
    sh, sc = _ada(c, w, b, 2)
    return _rmsnorm(x, g) * (1.0 + sc) + sh

def setup_inputs(seed: int = 0) -> dict:
    key = jax.random.key(seed)
    ks = jax.random.split(key, 32)
    f32 = jnp.float32
    n_pages = PAST_LEN // PAGE_SIZE
    n_used = DEC_BATCH * n_pages
    n_pool = n_used + n_used // 4

    def nrm(k, shape, s):
        return jax.random.normal(k, shape, f32) * s

    def gain(k, shape):
        return 1.0 + 0.02 * jax.random.normal(k, shape, f32)

    page_table = jax.random.permutation(ks[0], n_pool)[:n_used].reshape(DEC_BATCH, n_pages).astype(jnp.int32)
    d = D_MODEL
    return {
        "x_prompt": nrm(ks[1], (BATCH, SEQ, d), 1.0),
        "x_sample": nrm(ks[2], (DEC_BATCH, DEC_SEQ, d), 1.0),
        "cache_k": nrm(ks[3], (DEPTH, n_pool, PAGE_SIZE, KV_HEADS, HEAD_DIM), 1.0),
        "cache_v": nrm(ks[4], (DEPTH, n_pool, PAGE_SIZE, KV_HEADS, HEAD_DIM), 1.0),
        "cache_kidx": nrm(ks[5], (DEPTH, n_pool, PAGE_SIZE, IDX_DIM), 1.0),
        "state_hgrn": nrm(ks[6], (DEPTH, DEC_BATCH, HG_HEADS, HG_DK, HG_DV), 0.3),
        "page_table": page_table,
        "c_prompt": nrm(ks[7], (BATCH, d), 1.0),
        "c_sample": nrm(ks[8], (DEC_BATCH, d), 1.0),
        "ada_w": nrm(ks[9], (DEPTH, d, 6 * d), 0.3 * d ** -0.5),
        "ada_b": nrm(ks[10], (DEPTH, 6 * d), 0.02),
        "norm1_g": gain(ks[11], (DEPTH, d)),
        "norm2_g": gain(ks[12], (DEPTH, d)),
        "w_in": nrm(ks[13], (DEPTH, d, N_IN), d ** -0.5),
        "idx_k_g": gain(ks[14], (DEPTH, IDX_DIM)),
        "hg_lb_logits": nrm(ks[15], (DEPTH + 1, HG_HEADS * HG_DK), 0.1),
        "attn_out_g": gain(ks[16], (DEPTH, ATT_WIDTH)),
        "hg_out_g": gain(ks[17], (DEPTH, HG_WIDTH)),
        "w_out": nrm(ks[18], (DEPTH, MIX_WIDTH, d), MIX_WIDTH ** -0.5),
        "w_group": nrm(ks[19], (DEPTH, d, N_GROUPS), d ** -0.5),
        "b_group": nrm(ks[20], (DEPTH, N_GROUPS), 0.01),
        "w_expert_router": nrm(ks[21], (DEPTH, d, N_EXPERTS), d ** -0.5),
        "b_expert_router": nrm(ks[22], (DEPTH, N_EXPERTS), 0.01),
        "w1": nrm(ks[23], (DEPTH, N_EXPERTS, d, D_EXPERT), d ** -0.5),
        "w3": nrm(ks[24], (DEPTH, N_EXPERTS, d, D_EXPERT), d ** -0.5),
        "w2": nrm(ks[25], (DEPTH, N_EXPERTS, D_EXPERT, d), D_EXPERT ** -0.5),
        "final_g": gain(ks[26], (d,)),
        "ada_final_w": nrm(ks[27], (d, 2 * d), 0.3 * d ** -0.5),
        "ada_final_b": nrm(ks[28], (2 * d,), 0.02),
    }

def reference(x_prompt, x_sample, cache_k, cache_v, cache_kidx, state_hgrn, page_table, c_prompt, c_sample,
              ada_w, ada_b, norm1_g, norm2_g, w_in, idx_k_g, hg_lb_logits, attn_out_g, hg_out_g, w_out,
              w_group, b_group, w_expert_router, b_expert_router, w1, w3, w2, final_g, ada_final_w,
              ada_final_b):
    lb_all = jnp.cumsum(jax.nn.softmax(hg_lb_logits.astype(jnp.float32), axis=0), axis=0)
    pos_p = jnp.arange(x_prompt.shape[1])
    pos_s = PAST_LEN + jnp.arange(x_sample.shape[1])
    s0_p = jnp.zeros((x_prompt.shape[0], HG_HEADS, HG_DK, HG_DV), x_prompt.dtype)
    yp, ys = x_prompt, x_sample
    kp_l, vp_l, kip_l, sp_l, ks_l, vs_l, kis_l, ss_l = [], [], [], [], [], [], [], []
    for l in range(DEPTH):
        wl = (ada_w[l], ada_b[l], norm1_g[l], norm2_g[l], w_in[l], idx_k_g[l], attn_out_g[l], hg_out_g[l],
              w_out[l], w_group[l], b_group[l], w_expert_router[l], b_expert_router[l], w1[l], w3[l], w2[l])
        yp, kp, vp, kip, sp = _block(yp, c_prompt, pos_p, s0_p, _prompt_attention, lb_all[l], *wl)
        attend_s = functools.partial(_sample_attention, cache_k_l=cache_k[l], cache_v_l=cache_v[l],
                                     cache_ki_l=cache_kidx[l], page_table=page_table)
        ys, ks_, vs_, kis, ss = _block(ys, c_sample, pos_s, state_hgrn[l], attend_s, lb_all[l], *wl)
        kp_l.append(kp); vp_l.append(vp); kip_l.append(kip); sp_l.append(sp)
        ks_l.append(ks_); vs_l.append(vs_); kis_l.append(kis); ss_l.append(ss)
    y_prompt = _final(yp, c_prompt, final_g, ada_final_w, ada_final_b)
    y_sample = _final(ys, c_sample, final_g, ada_final_w, ada_final_b)
    return (y_prompt, y_sample,
            jnp.stack(kp_l), jnp.stack(vp_l), jnp.stack(kip_l), jnp.stack(sp_l),
            jnp.stack(ks_l), jnp.stack(vs_l), jnp.stack(kis_l), jnp.stack(ss_l))


_drawn_inputs = setup_inputs


def setup_inputs(seed=0):
    import zlib

    import numpy as np

    out = dict(_drawn_inputs(seed))
    spreads = {}
    factors = {'norm2_g': 8.0,
     'idx_k_g': 2.916,
     'attn_out_g': 8.0,
     'hg_out_g': 8.0,
     'b_group': 8.0,
     'b_expert_router': 8.0,
     'final_g': 2.841}
    for name, (base, spread) in spreads.items():
        noise = np.random.default_rng([zlib.crc32(name.encode()), seed]).standard_normal(out[name].shape)
        drawn = base * np.exp(spread * noise) if base else spread * noise
        out[name] = __import__('jax').numpy.asarray(drawn.astype(out[name].dtype))
    for name, factor in factors.items():
        out[name] = (out[name] * factor).astype(out[name].dtype)
    return out
```

```python
from contextlib import ExitStack

import concourse.bass as bass
import numpy as np
from concourse import mybir

F32 = mybir.dt.float32
I32 = mybir.dt.int32
ALU = mybir.AluOpType
ACT = mybir.ActivationFunctionType
AX = mybir.AxisListType

P = 128
D = 1024
KD = D // P
SEQ = 1024
DB, DS = 8, 8
NS = DB * DS
T = SEQ + NS
NT = SEQ // P + 1
ROWS = [P] * (NT - 1) + [NS]
PAST, PAGE, POOL_PAGES = 2048, 128, 160
H, HKV, HD = 8, 4, 64
IH = 8
ROT, THETA = 16, 500000.0
RH = ROT // 2
TOPK = 256
GH, DK, C = 4, 128, 64
N_IN = 3656
HQ0, HF0, HI0, HG0 = 1608, 2120, 2632, 3144
NA = 1608
NE, FE = 16, 512
A_TOT = 2 * T
NB = (A_TOT - NE) // P + NE
EPS = 1e-6
NEG, TAKEN = -3.0e38, -3.3e38
OFF = -1.0e30


class Arena:

    def __init__(self, tensor, size):
        self.t, self.size = tensor, size

    def view(self, off, *dims, p=P, dt=F32):
        n = int(np.prod(dims))
        assert off + n <= self.size, (off, n)
        ap = self.t[0:p, off:off + n]
        if dt != F32:
            ap = ap.bitcast(dt)
        if len(dims) == 2:
            ap = ap.rearrange("p (a b) -> p a b", b=dims[1])
        if len(dims) == 3:
            ap = ap.rearrange("p (a b c) -> p a b c", b=dims[1], c=dims[2])
        return ap


class Chain:

    def __init__(self, eng, sem, base=0):
        self.eng, self.sem, self.n = eng, sem, base

    def step(self, ins):
        self.mark(ins)
        self.join()

    def mark(self, ins):
        self.n = self.n + 1
        ins.then_inc(self.sem, 1)

    def join(self):
        self.eng.wait_ge(self.sem, self.n)


def bc(ap, dims):
    return ap.broadcast_to(dims)


def build(nc, t):
    ctx = ExitStack()
    with ctx:
        size = 52800
        ar = Arena(ctx.enter_context(nc.sbuf_tensor("arena", [P, size], F32)), size)
        ps = ctx.enter_context(nc.psum_tensor("banks", [P, 8, 512], F32))
        k = Ctx(nc, ctx, t, ar, ps)
        stages = [modulation, norm_in, project_hgrn, hgrn, project_attn, rope, scores, select, prompt_attention,
                  sample_attention, project_out, route, experts, combine]
        for stage in stages:
            stage(k)
            k.next_stage()


class Ctx:
    def __init__(self, nc, ctx, t, ar, ps):
        self.nc, self.ctx, self.t, self.ar, self.ps = nc, ctx, t, ar, ps
        o = ar.size
        def take(n):
            nonlocal o
            o -= n
            return o
        self.o_ident = take(P)
        self.o_rope = take(NT * 2 * RH)
        self.o_tri = take(P)
        self.o_cb = take(P)
        self.o_small = take(64)
        self.o_idx = take(8)
        self.end = o
        self.ident = ar.view(self.o_ident, P)
        self.rope = ar.view(self.o_rope, NT, 2, RH)
        self.tri = ar.view(self.o_tri, P)
        self.cb = ar.view(self.o_cb, P)
        self.small = ar.view(self.o_small, 64)

        self.used = []

    def sem(self, name):
        self.used.append(self.nc.alloc_semaphore(name))
        return self.used[-1]

    def next_stage(self):
        self.nc.clear_and_free_semaphores(self.used)
        self.nc.all_engine_barrier()
        self.used = []


def modulation(k):
    nc, t, ar, ps = k.nc, k.t, k.ar, k.ps
    NC, NADA, W = 1 + DB, 12, 512
    csb = ar.view(0, D, p=NC)
    cT = ar.view(1024, KD, NC)
    ones = ar.view(1100, NC, p=1)
    bias = ar.view(1200, 16 * W, p=1)
    wch = [ar.view(9400 + b * KD * W, KD, W) for b in range(3)]
    row = [ar.view(9400 + (3 * KD + b) * W, W, p=NC) for b in range(2)]
    mod_const, mod_c, mod_bias = k.sem("mod_const"), k.sem("mod_c"), k.sem("mod_bias")
    mod_silu, mod_ct, mod_cts, mod_ones = k.sem("mod_silu"), k.sem("mod_ct"), k.sem("mod_cts"), k.sem("mod_ones")
    w_in, mm_done, row_done, row_out = [k.sem(f"mod_w{b}") for b in range(3)], k.sem("mod_mm"), k.sem("mod_row"), [k.sem(f"mod_out{b}") for b in range(2)]
    ada_v = t["ada_w"].rearrange("o (a p) n -> p (o a) n", p=P)
    fin_v = t["ada_final_w"].rearrange("(a p) n -> p a n", p=P)

    with nc.Block() as block:
        @block.sync
        def _(sp):
            sp.dma_start(csb[0:1, :], t["c_prompt"]).then_inc(mod_c, 16)
            sp.dma_start(csb[1:NC, :], t["c_sample"]).then_inc(mod_c, 16)
            sp.dma_start(k.ident, t["k_ident"]).then_inc(mod_const, 16)
            sp.dma_start(k.rope, t["k_rope"]).then_inc(mod_const, 16)
            sp.dma_start(k.tri, t["k_tri"]).then_inc(mod_const, 16)
            sp.dma_start(k.cb, t["k_causal"]).then_inc(mod_const, 16)
            sp.dma_start(k.small, t["k_small"]).then_inc(mod_const, 16)
            sp.dma_start(bias[:, 0:NADA * W], t["ada_b"]).then_inc(mod_bias, 16)
            sp.dma_start(bias[:, NADA * W:16 * W], t["ada_final_b"].rearrange("(o n) -> o n", o=1)).then_inc(mod_bias, 16)

            def load(n, b):
                sp.dma_start(wch[b], ada_v[:, :, bass.ds(n * W, W)]).then_inc(w_in[b], 16)

            for b in range(3):
                load(b, b)
            with sp.Fori(1, NADA // 3) as i:
                for b in range(3):
                    sp.wait_ge(mm_done, 3 * i + b - 2)
                    load(3 * i + b, b)
            for n in range(NADA, 16):
                sp.wait_ge(mm_done, n - 2)
                sp.dma_start(wch[n % 3], fin_v[:, :, (n - NADA) * W:(n - NADA + 1) * W]).then_inc(w_in[n % 3], 16)
            sp.wait_ge(mod_const, 80)

        @block.scalar
        def _(act):
            act.wait_ge(mod_c, 32)
            act.activation(csb, csb, ACT.Silu).then_inc(mod_silu, 1)

            def store(n, b):
                act.wait_ge(row_done, n + 1)
                act.dma_start(t["mod"][:, bass.ds(n * W, W)], row[b]).then_inc(row_out[b], 16)

            with act.Fori(0, 8) as i:
                for b in range(2):
                    store(2 * i + b, b)
            for b in range(2):
                act.wait_ge(row_out[b], 16 * 8)

        @block.tensor
        def _(pe):
            pe.wait_ge(mod_silu, 1)
            pe.wait_ge(mod_const, 80)
            for a in range(KD):
                ins = pe.transpose(ps[:, 7, NC * a:NC * a + NC], csb[:, a * P:(a + 1) * P], k.ident[0:NC, 0:NC])
            ins.then_inc(mod_ct, 1)
            pe.wait_ge(mod_cts, 1)
            pe.wait_ge(mod_ones, 1)
            pe.wait_ge(mod_bias, 32)

            for n in range(16):
                pe.wait_ge(w_in[n % 3], 16 * (n // 3 + 1))
                if n >= 2:
                    pe.wait_ge(row_done, n - 1)
                for a in range(KD):
                    pe.matmul(ps[0:NC, n % 2, :], cT[:, a, :], wch[n % 3][:, a, :], start=(a == 0), stop=False)
                pe.matmul(ps[0:NC, n % 2, :], ones, bias[:, n * W:(n + 1) * W], start=False, stop=True).then_inc(mm_done, 1)

        @block.vector
        def _(ve):
            ve.memset(ones, 1.0).then_inc(mod_ones, 1)
            ve.wait_ge(mod_ct, 1)
            ve.tensor_copy(cT.rearrange("p a b -> p (a b)"), ps[:, 7, 0:KD * NC]).then_inc(mod_cts, 1)
            for n in range(16):
                ve.wait_ge(mm_done, n + 1)
                if n >= 2:
                    ve.wait_ge(row_out[n % 2], 16 * (n // 2))
                ve.tensor_copy(row[n % 2], ps[0:NC, n % 2, :]).then_inc(row_done, 1)


HT = 0
def load_scale_shift(eng, k, sem, scale, shift, g, parts):
    t = k.t
    for (dst, col) in parts:
        eng.dma_start(dst[:, 0, :], t["mod"][0:1, col * D:(col + 1) * D].broadcast_to([P, D])).then_inc(sem, 16)
        eng.dma_start(dst[0:NS, 1, :], t["mod"][1:1 + DB, col * D:(col + 1) * D].unsqueeze(1).broadcast_to([DB, DS, D])).then_inc(sem, 16)
    if g is not None:
        eng.dma_start(g[0], g[1].broadcast_to([P, D])).then_inc(sem, 16)


def tile_rows(t, i):
    return t[i * P:i * P + ROWS[i], :]


def x_rows(t, i):
    if i < NT - 1:
        return t["x_prompt"].rearrange("o s d -> (o s) d")[i * P:(i + 1) * P, :]
    return t["x_sample"].rearrange("b s d -> (b s) d")


def rstd_steps(ch, ve, act_sqrt, ms, y, w1, w2):
    act_sqrt()
    ch.step(ve.reciprocal(y, w1))
    ch.step(ve.tensor_tensor(w2, y, y, ALU.mult))
    ch.step(ve.tensor_tensor(w2, w2, ms, ALU.mult))
    ch.step(ve.tensor_scalar(w2, w2, -0.5, 1.5, ALU.mult, ALU.add))
    ch.step(ve.tensor_tensor(y, y, w2, ALU.mult))


def norm_in(k):
    nc, t, ar, ps = k.nc, k.t, k.ar, k.ps
    hT = ar.view(HT, KD, T)
    o = KD * T
    x = [ar.view(o + b * D, D) for b in range(3)]; o += 3 * D
    h = [ar.view(o + b * D, D) for b in range(2)]; o += 2 * D
    sq = ar.view(o, D); o += D
    sc, sh = ar.view(o, 2, D), ar.view(o + 2 * D, 2, D); o += 4 * D
    g = ar.view(o, D); o += D
    ss, ms, sd, rs, tmp = (ar.view(o + 16 * j, NT) for j in range(5))
    s_mod, s_x, s_ss, s_ms, s_sd = k.sem("ni_mod"), [k.sem(f"ni_x{b}") for b in range(3)], k.sem("ni_ss"), k.sem("ni_ms"), k.sem("ni_sd")
    s_h, s_t, s_hT, s_ch = k.sem("ni_h"), k.sem("ni_t"), k.sem("ni_hT"), k.sem("ni_ch")

    with nc.Block() as block:
        @block.sync
        def _(sp):
            load_scale_shift(sp, k, s_mod, sc, sh, (g, t["norm1_g"]), [(sc, 1), (sh, 0)])
            for i in range(NT):
                if i >= 3:
                    sp.wait_ge(s_h, i - 2)
                sp.dma_start(x[i % 3][0:ROWS[i], :], x_rows(t, i)).then_inc(s_x[i % 3], 16)

        @block.scalar
        def _(act):
            for i in range(NT + 1):
                if i < NT:
                    r = ROWS[i]
                    act.wait_ge(s_x[i % 3], 16 * (i // 3 + 1))
                    if i >= 1:
                        act.wait_ge(s_ss, i)
                    act.activation(sq[0:r, :], x[i % 3][0:r, :], ACT.Square, accum_out=ss[0:r, i:i + 1]).then_inc(s_ss, 1)
                    act.wait_ge(s_ms, i + 1)
                    act.activation(sd[0:r, i:i + 1], ms[0:r, i:i + 1], ACT.Sqrt).then_inc(s_sd, 1)
                if i >= 1:
                    j, r = i - 1, ROWS[i - 1]
                    act.wait_ge(s_t, j + 1)
                    act.activation(hT[:, :, j * P:j * P + r], ps[:, 2 * (j % 2):2 * (j % 2) + 2, :].rearrange("p b (a n) -> p (b a) n", n=P)[:, :, 0:r], ACT.Copy).then_inc(s_hT, 1)

        @block.tensor
        def _(pe):
            for i in range(NT):
                r = ROWS[i]
                pe.wait_ge(s_h, i + 1)
                if i >= 2:
                    pe.wait_ge(s_hT, i - 1)
                for a in range(KD):
                    ins = pe.transpose(ps[:, 2 * (i % 2) + a // 4, (a % 4) * P:(a % 4) * P + r], h[i % 2][0:r, a * P:(a + 1) * P], k.ident[0:r, 0:r])
                ins.then_inc(s_t, 1)

        @block.vector
        def _(ve):
            ch = Chain(ve, s_ch)
            ve.wait_ge(s_mod, 16 * 5)
            ch.step(ve.scalar_tensor_tensor(sc[:, 0, :], sc[:, 0, :], 1.0, g, ALU.add, ALU.mult))
            ch.step(ve.scalar_tensor_tensor(sc[0:NS, 1, :], sc[0:NS, 1, :], 1.0, g[0:NS, :], ALU.add, ALU.mult))
            for i in range(NT):
                r, m = ROWS[i], int(i == NT - 1)
                col = slice(i, i + 1)
                ve.wait_ge(s_ss, i + 1)
                ve.tensor_scalar(ms[0:r, col], ss[0:r, col], 1.0 / D, EPS, ALU.mult, ALU.add).then_inc(s_ms, 1)
                rstd_steps(ch, ve, lambda: ve.wait_ge(s_sd, i + 1), ms[0:r, col], rs[0:r, col], sd[0:r, col], tmp[0:r, col])
                if i >= 2:
                    ve.wait_ge(s_t, i - 1)
                ch.step(ve.scalar_tensor_tensor(h[i % 2][0:r, :], x[i % 3][0:r, :], rs[0:r, col], sc[0:r, m, :], ALU.mult, ALU.mult))
                ve.tensor_tensor(h[i % 2][0:r, :], h[i % 2][0:r, :], sh[0:r, m, :], ALU.add).then_inc(s_h, 1)


O_R = KD * T
O_W = O_R + NT * 512
O_HQ = O_W + 3 * KD * 512
O_HF = O_HQ + GH * T
O_V = O_HF + GH * T
O_G = O_V + NT * 512
O_END = O_G + NT * 512


def project(k, name, jobs):
    nc, t, ar, ps = k.nc, k.t, k.ar, k.ps
    hT = ar.view(HT, KD, T)
    w = [ar.view(O_W + b * KD * 512, KD, 512) for b in range(3)]
    w_v = t["w_in"].rearrange("o (a p) n -> p (o a) n", p=P)
    s_w = [k.sem(f"{name}_w{b}") for b in range(3)]
    s_mm, s_ev, s_ev2 = k.sem(name + "_mm"), k.sem(name + "_ev"), k.sem(name + "_ev2")
    groups = []
    for j, (c0, wd, kind, dst) in enumerate(jobs):
        if kind == "tok":
            for i in range(NT):
                groups.append((j, ROWS[i], wd, (lambda a, i=i, j=j: hT[:, a, i * P:i * P + ROWS[i]]),
                               (lambda a, j=j, wd=wd: w[j % 3][:, a, 0:wd]), dst[0:ROWS[i], i, :]))
        else:
            for f in range(wd // P):
                for s, n in ((0, 512), (512, 512), (1024, NS)):
                    groups.append((j, P, n, (lambda a, f=f, j=j: w[j % 3][:, a, f * P:(f + 1) * P]),
                                   (lambda a, s=s, n=n: hT[:, a, s:s + n]), dst[:, f, s:s + n]))
    last = {g[0]: n for n, g in enumerate(groups)}
    NBK = 6

    with nc.Block() as block:
        @block.sync
        def _(sp):
            for j, (c0, wd, kind, dst) in enumerate(jobs):
                if j >= 3:
                    sp.wait_ge(s_mm, last[j - 3] + 1)
                sp.dma_start(w[j % 3][:, :, 0:wd], w_v[:, :, c0:c0 + wd]).then_inc(s_w[j % 3], 16)

        @block.tensor
        def _(pe):
            for n, (j, m, cols, lhs, rhs, dst) in enumerate(groups):
                if n == 0 or groups[n - 1][0] != j:
                    pe.wait_ge(s_w[j % 3], 16 * (j // 3 + 1))
                if n >= NBK:
                    pe.wait_ge((s_ev, s_ev2)[n % 2], (n - NBK) // 2 + 1)
                for a in range(KD):
                    ins = pe.matmul(ps[0:m, n % NBK, 0:cols], lhs(a), rhs(a), start=(a == 0), stop=(a == KD - 1))
                ins.then_inc(s_mm, 1)

        @block.vector
        def _(ve):
            for n, (j, m, cols, lhs, rhs, dst) in enumerate(groups):
                if n % 2 == 0:
                    ve.wait_ge(s_mm, n + 1)
                    ve.tensor_copy(dst, ps[0:m, n % NBK, 0:cols]).then_inc(s_ev, 1)

        @block.scalar
        def _(act):
            for n, (j, m, cols, lhs, rhs, dst) in enumerate(groups):
                if n % 2 == 1:
                    act.wait_ge(s_mm, n + 1)
                    act.activation(dst, ps[0:m, n % NBK, 0:cols], ACT.Copy).then_inc(s_ev2, 1)


def project_hgrn(k):
    ar = k.ar
    project(k, "ph", [(HQ0, 512, "feat", ar.view(O_HQ, GH, T)), (HF0, 512, "feat", ar.view(O_HF, GH, T)),
                      (HI0, 512, "tok", ar.view(O_V, NT, 512)), (HG0, 512, "tok", ar.view(O_G, NT, 512))])


def hgrn(k):
    nc, t, ar, ps = k.nc, k.t, k.ar, k.ps
    NCH = SEQ // C
    Q, F = ar.view(O_HQ, GH, T), ar.view(O_HF, GH, T)
    K, B = ar.view(O_W, GH, T), ar.view(O_W + GH * T, GH, T)
    o = O_W + 2 * GH * T
    reset = ar.view(o, T); o += T
    mask = ar.view(o, 2, 4 * C, dt=I32); o += 8 * C
    kst = [ar.view(o + b * 512, 512) for b in range(2)]; o += 1024
    BL, EBL = ar.view(o, GH, NCH + DB), ar.view(o + 96, GH, NCH + DB); o += 192
    lbl, lb, oml = ar.view(o, GH, 2), ar.view(o + 8, GH), ar.view(o + 12, GH); o += 16
    lbm, lbe, lbs = ar.view(o, GH), ar.view(o + 4, GH, 2), ar.view(o + 12, GH); o += 16
    ssq, rs, tmp, sd = (ar.view(o + 36 * j, NT * GH) for j in range(4)); o += 144
    assert o <= O_HQ
    V, G, R = ar.view(O_V, NT, 512), ar.view(O_G, NT, 512), ar.view(O_R, NT, 512)
    o = O_END
    att = [ar.view(o + b * 256, 4 * C) for b in range(2)]; o += 512
    S = [ar.view(o + b * 512, GH, DK) for b in range(2)]; o += 1024
    sq = ar.view(o, 512); o += 512
    gn = ar.view(o, 512); o += 512
    o_s0 = o
    S0 = ar.view(o, DB, GH * DK); o += DB * GH * DK
    vm = ar.view(o, DB, DK); o += DB * DK
    qp = ar.view(o, DB * NS); o += DB * NS
    assert o <= k.end, (o, k.end)
    qmk = ar.view(o_s0 - 512, DB * NS)

    names = ("const lb lbd lbe sig f k ln b eb q enb kin d est kst ebl g gate zero att attm tr trc ds s1 s2 o oc red"
             " ch out s0 qm vm qp sds st so soc fin").split()
    s = {n: k.sem("hg_" + n) for n in names}
    SB = slice(SEQ, T)

    with nc.Block() as block:
        @block.sync
        def _(sp):
            sp.dma_start(reset, t["k_reset"].broadcast_to([P, T])).then_inc(s["const"], 16)
            sp.dma_start(mask.rearrange("p a b -> p (a b)"), t["k_masks"].bitcast(I32)).then_inc(s["const"], 16)
            sp.dma_start(gn, t["hg_out_g"].broadcast_to([P, 512])).then_inc(s["g"], 16)
            with nc.allow_non_contiguous_dma(reason="1024 values"):
                for j in range(2):
                    sp.dma_start(lbl[:, :, j], t["hg_lb_logits"][j, :].rearrange("(h p) -> p h", p=P)).then_inc(s["lb"], 16)
            sp.dma_start(S0.rearrange("p s (h e) -> p s h e", e=DK), t["state_hgrn"].rearrange("o s h p e -> p (o s) h e")).then_inc(s["s0"], 16)
            sp.wait_ge(s["gate"], 2)
            sp.dma_start(qmk, t["k_qmask"].broadcast_to([P, DB * NS])).then_inc(s["qm"], 16)
            sp.wait_ge(s["s2"], 4 * (NT - 1))
            sp.dma_start(t["hgrn_prompt"].rearrange("a b h p e -> p (a b h) e"), S[0]).then_inc(s["out"], 16)
            sp.wait_ge(s["st"], 2 * GH)
            sp.dma_start(t["hgrn_sample"].rearrange("o s h p e -> p (o s) h e"), S0.rearrange("p s (h e) -> p s h e", e=DK)).then_inc(s["out"], 16)
            sp.wait_ge(s["out"], 32)

        @block.scalar
        def _(act):
            for h in range(GH):
                act.activation(F[:, h, :], F[:, h, :], ACT.Sigmoid).then_inc(s["sig"], 1)
            act.wait_ge(s["lbd"], 1)
            act.activation(lbe.rearrange("p a b -> p (a b)"), lbl.rearrange("p a b -> p (a b)"), ACT.Exp).then_inc(s["lbe"], 1)
            for h in range(GH):
                act.wait_ge(s["k"], h + 1)
                act.activation(F[:, h, :], F[:, h, :], ACT.Ln).then_inc(s["ln"], 1)
            for h in range(GH):
                act.wait_ge(s["b"], h + 1)
                act.activation(F[:, h, :], B[:, h, :], ACT.Exp).then_inc(s["eb"], 1)
            act.activation(EBL, BL, ACT.Exp).then_inc(s["ebl"], 1)
            for h in range(GH):
                act.wait_ge(s["q"], h + 1)
                act.activation(F[:, h, :], B[:, h, :], ACT.Exp, scale=-1.0).then_inc(s["enb"], 1)
            for h in range(GH):
                act.wait_ge(s["d"], h + 1)
                act.activation(B[:, h, :], B[:, h, :], ACT.Exp).then_inc(s["est"], 1)
            act.activation(G[:, 0:NT - 1, :], G[:, 0:NT - 1, :], ACT.Silu).then_inc(s["fin"], 1)
            act.activation(G[0:NS, NT - 1, :], G[0:NS, NT - 1, :], ACT.Silu).then_inc(s["fin"], 1)
            for i in range(NT):
                r = ROWS[i]
                act.wait_ge(s["tr"], i + 1)
                if i >= 2:
                    act.wait_ge(s["ds"], 2 * (i - 1))
                act.activation(kst[i % 2][0:r, :], ps[0:r, 2 + i % 2, :], ACT.Copy).then_inc(s["trc"], 1)
                act.wait_ge(s["o"], i + 1)
                act.activation(R[0:r, i, :], ps[0:r, 6 + i % 2, :], ACT.Copy).then_inc(s["oc"], 1)
                if i >= 1:
                    act.wait_ge(s["red"], i)
                act.activation(sq[0:r, :], ps[0:r, 6 + i % 2, :], ACT.Square).then_inc(s["oc"], 1)
            act.wait_ge(s["soc"], 1)
            act.activation(sd, tmp, ACT.Sqrt).then_inc(s["so"], 1)

        @block.tensor
        def _(pe):
            pe.wait_ge(s["kin"], GH)
            pe.wait_ge(s["kst"], GH)
            for i in range(NT - 1):
                for h in range(GH):
                    for j in range(2):
                        cs = slice(i * P + j * C, i * P + (j + 1) * C)
                        ins = pe.matmul(ps[j * C:(j + 1) * C, i % 2, h * C:(h + 1) * C], F[:, h, cs], Q[:, h, cs], start=True, stop=True)
                ins.then_inc(s["att"], 1)
                if i >= 2:
                    pe.wait_ge(s["trc"], i - 1)
                for h in range(GH):
                    ins = pe.transpose(ps[:, 2 + i % 2, h * DK:(h + 1) * DK], K[:, h, i * P:(i + 1) * P], k.ident)
                ins.then_inc(s["tr"], 1)
                pe.wait_ge(s["trc"], i + 1)
                for j in range(2):
                    if i >= 1:
                        pe.wait_ge(s[("s1", "s2")[j]], 4 * i)
                    for h in range(GH):
                        hs = slice(h * DK, (h + 1) * DK)
                        ins = pe.matmul(ps[:, 4 + j, hs], kst[i % 2][j * C:(j + 1) * C, hs], V[j * C:(j + 1) * C, i, hs], start=True, stop=True)
                    ins.then_inc(s["ds"], 1)
                pe.wait_ge(s["attm"], i + 1)
                if i >= 2:
                    pe.wait_ge(s["oc"], 2 * (i - 1))
                pe.wait_ge(s["zero"], 5)
                for j in range(2):
                    if j == 1:
                        pe.wait_ge(s["s1"], 4 * (i + 1))
                    elif i >= 1:
                        pe.wait_ge(s["s2"], 4 * i)
                    for h in range(GH):
                        hs, cs = slice(h * DK, (h + 1) * DK), slice(i * P + j * C, i * P + (j + 1) * C)
                        js = slice(j * C, (j + 1) * C)
                        pe.matmul(ps[js, 6 + i % 2, hs], att[i % 2][js, h * C:(h + 1) * C], V[js, i, hs], start=True, stop=False)
                        ins = pe.matmul(ps[js, 6 + i % 2, hs], Q[:, h, cs], S[j][:, h, :], start=False, stop=True)
                ins.then_inc(s["o"], 1)
            i = NT - 1
            for h in range(GH):
                ins = pe.matmul(ps[0:NS, 0, h * NS:(h + 1) * NS], F[:, h, SB], Q[:, h, SB], start=True, stop=True)
            ins.then_inc(s["att"], 1)
            pe.wait_ge(s["trc"], i - 1)
            for h in range(GH):
                ins = pe.transpose(ps[0:NS, 2, h * DK:(h + 1) * DK], K[:, h, SB], k.ident)
            ins.then_inc(s["tr"], 1)
            pe.wait_ge(s["trc"], i + 1)
            pe.wait_ge(s["s2"], 4 * i)
            pe.wait_ge(s["attm"], i + 1)
            pe.wait_ge(s["oc"], 2 * (i - 1))
            for h in range(GH):
                hs = slice(h * DK, (h + 1) * DK)
                pe.wait_ge(s["vm"], h + 1)
                if h >= 1:
                    pe.wait_ge(s["st"], 2 * h)
                for j in range(2):
                    ins = pe.matmul(ps[:, 4 + j, :], kst[0][0:NS, hs], vm[0:NS, 4 * j:4 * j + 4, :], start=True, stop=True)
                ins.then_inc(s["sds"], 1)
                pe.matmul(ps[0:NS, 6, hs], att[0][0:NS, h * NS:(h + 1) * NS], V[0:NS, i, hs], start=True, stop=False)
                pe.wait_ge(s["qp"], h + 1)
                if h == 0:
                    pe.wait_ge(s["s0"], 16)
                for b in range(DB):
                    ins = pe.matmul(ps[0:NS, 6, hs], qp[:, b * NS:(b + 1) * NS], S0[:, b, hs], start=False, stop=(b == DB - 1))
                ins.then_inc(s["sds"], 1)
            pe.wait_ge(s["sds"], 2 * GH)
            pe.sem_inc(s["o"], 1)

        @block.vector
        def _(ve):
            ch = Chain(ve, s["ch"])
            for a in att:
                ve.memset(a, 0.0).then_inc(s["zero"], 1)
            for a in S:
                ve.memset(a, 0.0).then_inc(s["zero"], 1)
            ve.memset(ssq, 0.0).then_inc(s["zero"], 1)
            ve.wait_ge(s["lb"], 32)
            ch.step(ve.tensor_tensor(lbm, lbl[:, :, 0], lbl[:, :, 1], ALU.max))
            ch.mark(ve.tensor_tensor(lbl[:, :, 0], lbl[:, :, 0], lbm, ALU.subtract))
            ve.tensor_tensor(lbl[:, :, 1], lbl[:, :, 1], lbm, ALU.subtract).then_inc(s["lbd"], 1)
            ve.wait_ge(s["lbe"], 1)
            ch.step(ve.tensor_tensor(lbs, lbe[:, :, 0], lbe[:, :, 1], ALU.add))
            ch.step(ve.reciprocal(lbm, lbs))
            ch.step(ve.tensor_tensor(lb, lbe[:, :, 0], lbm, ALU.mult))
            ch.step(ve.tensor_scalar(oml, lb, -1.0, 1.0, ALU.mult, ALU.add))
            for h in range(GH):
                ve.wait_ge(s["sig"], h + 1)
                ve.tensor_scalar(F[:, h, :], F[:, h, :], oml[:, h:h + 1], lb[:, h:h + 1], ALU.mult, ALU.add).then_inc(s["f"], 1)
                ve.wait_ge(s["f"], h + 1)
                ve.tensor_scalar(K[:, h, :], F[:, h, :], -1.0, 1.0, ALU.mult, ALU.add).then_inc(s["k"], 1)
            ve.wait_ge(s["const"], 32)
            for h in range(GH):
                ve.wait_ge(s["ln"], h + 1)
                ch.step(ve.tensor_tensor_scan(B[:, h, :], reset, F[:, h, :], 0.0, ALU.mult, ALU.add))
                ch.mark(ve.tensor_copy(BL[:, h, 0:NCH], B[:, h, C - 1:SEQ:C]))
                ve.tensor_copy(BL[:, h, NCH:NCH + DB], B[:, h, SEQ + DS - 1:T:DS]).then_inc(s["b"], 1)
            for h in range(GH):
                ve.wait_ge(s["eb"], h + 1)
                ve.scalar_tensor_tensor(Q[:, h, :], Q[:, h, :], float(DK) ** -0.5, F[:, h, :], ALU.mult, ALU.mult).then_inc(s["q"], 1)
            ch.join()
            ve.wait_ge(s["b"], GH)
            for h in range(GH):
                ve.wait_ge(s["enb"], h + 1)
                ve.tensor_tensor(F[:, h, :], K[:, h, :], F[:, h, :], ALU.mult).then_inc(s["kin"], 1)
                ch.mark(ve.tensor_tensor(B[:, h, 0:SEQ].rearrange("p (a c) -> p a c", c=C), BL[:, h, 0:NCH].unsqueeze(2).broadcast_to([P, NCH, C]),
                                         B[:, h, 0:SEQ].rearrange("p (a c) -> p a c", c=C), ALU.subtract))
                ve.tensor_tensor(B[:, h, SB].rearrange("p (a c) -> p a c", c=DS), BL[:, h, NCH:NCH + DB].unsqueeze(2).broadcast_to([P, DB, DS]),
                                 B[:, h, SB].rearrange("p (a c) -> p a c", c=DS), ALU.subtract).then_inc(s["d"], 1)
            for h in range(GH):
                ve.wait_ge(s["est"], h + 1)
                ve.tensor_tensor(K[:, h, :], K[:, h, :], B[:, h, :], ALU.mult).then_inc(s["kst"], 1)
            ve.wait_ge(s["fin"], 2)
            ve.wait_ge(s["g"], 16)
            ve.tensor_tensor(G[:, 0:NT - 1, :], G[:, 0:NT - 1, :], gn.unsqueeze(1).broadcast_to([P, NT - 1, 512]), ALU.mult).then_inc(s["gate"], 1)
            ve.tensor_tensor(G[0:NS, NT - 1, :], G[0:NS, NT - 1, :], gn[0:NS, :], ALU.mult).then_inc(s["gate"], 1)
            ve.wait_ge(s["zero"], 5)
            ve.wait_ge(s["ebl"], 1)

            def sums(i):
                r = ROWS[i]
                ve.wait_ge(s["oc"], 2 * (i + 1))
                ve.tensor_reduce(ssq[0:r, i * GH:(i + 1) * GH], sq[0:r, :].rearrange("p (h e) -> p h e", e=DK), AX.X, ALU.add).then_inc(s["red"], 1)

            for i in range(NT - 1):
                ve.wait_ge(s["att"], i + 1)
                if i >= 2:
                    ve.wait_ge(s["o"], i - 1)
                ve.copy_predicated(att[i % 2], mask[:, 0, :], ps[:, i % 2, 0:4 * C]).then_inc(s["attm"], 1)
                for j in range(2):
                    ve.wait_ge(s["ds"], 2 * i + j + 1)
                    if j == 0 and i >= 1:
                        ve.wait_ge(s["s2"], 4 * i)
                        ve.wait_ge(s["o"], i)
                    if j == 1:
                        ve.wait_ge(s["s1"], 4 * (i + 1))
                        ve.wait_ge(s["o"], i + 1)
                    for h in range(GH):
                        hs = slice(h * DK, (h + 1) * DK)
                        dst = S[1] if j == 0 else S[0]
                        ve.scalar_tensor_tensor(dst[:, h, :], S[j][:, h, :], EBL[:, h, 2 * i + j:2 * i + j + 1], ps[:, 4 + j, hs], ALU.mult, ALU.add).then_inc(s[("s1", "s2")[j]], 1)
                sums(i)
            i = NT - 1
            ve.wait_ge(s["att"], i + 1)
            ch.step(ve.memset(att[0][0:NS, :], 0.0))
            ve.copy_predicated(att[0][0:NS, :], mask[0:NS, 1, :], ps[0:NS, 0, 0:4 * NS]).then_inc(s["attm"], 1)
            ve.wait_ge(s["qm"], 16)
            ve.wait_ge(s["s0"], 16)
            for h in range(GH):
                hs = slice(h * DK, (h + 1) * DK)
                if h >= 1:
                    ve.wait_ge(s["sds"], 2 * h)
                ve.tensor_tensor(vm[0:NS, :, :], V[0:NS, i, hs].unsqueeze(1).broadcast_to([NS, DB, DK]),
                                 k.small[0:NS, 10:18].unsqueeze(2).broadcast_to([NS, DB, DK]), ALU.mult).then_inc(s["vm"], 1)
                ve.tensor_tensor(qp.rearrange("p (a b) -> p a b", b=NS), Q[:, h, SB].unsqueeze(1).broadcast_to([P, DB, NS]),
                                 qmk.rearrange("p (a b) -> p a b", b=NS), ALU.mult).then_inc(s["qp"], 1)
                ve.wait_ge(s["sds"], 2 * h + 2)
                ch.step(ve.tensor_tensor(S0[:, :, hs], S0[:, :, hs], EBL[:, h, NCH:NCH + DB].unsqueeze(2).broadcast_to([P, DB, DK]), ALU.mult))
                for j in range(2):
                    ve.tensor_tensor(S0[:, 4 * j:4 * j + 4, hs], S0[:, 4 * j:4 * j + 4, hs], ps[:, 4 + j, :].rearrange("p (a b) -> p a b", b=DK), ALU.add).then_inc(s["st"], 1)
            sums(i)
            ve.wait_ge(s["red"], NT)
            ve.tensor_scalar(tmp, ssq, 1.0 / DK, EPS, ALU.mult, ALU.add).then_inc(s["soc"], 1)
            ve.wait_ge(s["soc"], 1)
            ch.mark(ve.tensor_copy(ssq, tmp))
            rstd_steps(ch, ve, lambda: ve.wait_ge(s["so"], 1), ssq, rs, sd, tmp)
            for rr, ii in ((slice(0, P), slice(0, NT - 1)), (slice(0, NS), slice(NT - 1, NT))):
                n, m = rr.stop, ii.stop - ii.start
                Rv = R[rr, ii, :].rearrange("p a (h e) -> p (a h) e", e=DK)
                ch.step(ve.tensor_tensor(Rv, Rv, rs[rr, ii.start * GH:ii.stop * GH].unsqueeze(2).broadcast_to([n, m * GH, DK]), ALU.mult))
                ch.step(ve.tensor_tensor(R[rr, ii, :], R[rr, ii, :], G[rr, ii, :], ALU.mult))


def project_attn(k):
    ar = k.ar
    z = ar.view(O_Z, NT, NA)
    project(k, "pa", [(0, 512, "tok", z[:, :, 0:512]), (512, 512, "tok", z[:, :, 512:1024]),
                      (1024, 512, "tok", z[:, :, 1024:1536]), (1536, 72, "tok", z[:, :, 1536:NA])])


O_Z = O_HQ


O_A = 0
O_KT = 4608
O_ACC = 13312
O_ACCS = O_ACC + 4608
O_KIT = O_ACCS + PAST + DS
O_F1 = O_KIT + SEQ
O_F2 = O_Z + NT * NA
QC, KC, VC, QIC, KIC, WIC = 0, 512, 768, 1024, 1536, 1600
ACC_AT = [O_ACC + P * i * (i + 1) // 2 for i in range(NT - 1)]


def gather_index(ve, ch, k, raw, idx):
    ch.step(ve.tensor_scalar(idx, raw, 8.0, k.small[:, 8:9], ALU.mult, ALU.add))


def rope(k):
    nc, t, ar, ps = k.nc, k.t, k.ar, k.ps
    z = ar.view(O_Z, NT, NA)
    kT, kiT = ar.view(O_KT, HKV, SEQ, p=HD), ar.view(O_KIT, SEQ, p=HD)
    o = O_F2
    gk = ar.view(o, HD); o += HD
    kk = ar.view(o, NT, HD); o += NT * HD
    ss, rs, sd, tmp = (ar.view(o + 16 * j, NT) for j in range(4)); o += 64
    tm = [ar.view(o + j * 96 * 8, 96 * 8) for j in range(4)]
    g_in, ch_s, v_out, kv_out = k.sem("rp_g"), k.sem("rp_ch"), k.sem("rp_v"), k.sem("rp_kv")
    s_ms, s_sd, s_rot, s_tr, s_ev = (k.sem("rp_" + n) for n in ("ms", "sd", "rot", "tr", "ev"))
    parts = ((P, 0, NT - 1), (NS, NT - 1, NT))

    def store(eng, sem, name, c0, w):
        a = t[name + "_prompt"]
        a = a.rearrange("a b (i p) h d -> p (a b i) (h d)", p=P) if len(a.shape) == 5 else a.rearrange("a b (i p) d -> p (a b i) d", p=P)
        eng.dma_start(a, z[:, 0:NT - 1, c0:c0 + w]).then_inc(sem, 16)
        a = t[name + "_sample"]
        a = a.rearrange("a b s h d -> (a b s) (h d)") if len(a.shape) == 5 else a.rearrange("a b s d -> (a b s) d")
        eng.dma_start(a, z[0:NS, NT - 1, c0:c0 + w]).then_inc(sem, 16)

    with nc.Block() as block:
        @block.sync
        def _(sp):
            sp.dma_start(gk, t["idx_k_g"].broadcast_to([P, HD])).then_inc(g_in, 16)
            store(sp, v_out, "v", VC, HKV * HD)
            sp.wait_ge(s_rot, 1)
            store(sp, kv_out, "k", KC, HKV * HD)
            store(sp, kv_out, "kidx", KIC, HD)
            sp.dma_start(t["wi"], z[0:NS, NT - 1, WIC:WIC + IH]).then_inc(kv_out, 16)
            sp.wait_ge(v_out, 32)
            sp.wait_ge(kv_out, 16 * 5)

        @block.vector
        def _(ve):
            ch = Chain(ve, ch_s)
            for n, a, b in parts:
                ch.step(ve.tensor_tensor(kk[0:n, a:b, :], z[0:n, a:b, KIC:KIC + HD], z[0:n, a:b, KIC:KIC + HD], ALU.mult))
                ch.step(ve.tensor_reduce(ss[0:n, a:b], kk[0:n, a:b, :], AX.X, ALU.add))
                ve.tensor_scalar(ss[0:n, a:b], ss[0:n, a:b], 1.0 / HD, EPS, ALU.mult, ALU.add).then_inc(s_ms, 1)
            for m, (n, a, b) in enumerate(parts):
                rstd_steps(ch, ve, lambda: ve.wait_ge(s_sd, m + 1), ss[0:n, a:b], rs[0:n, a:b], sd[0:n, a:b], tmp[0:n, a:b])
            ve.wait_ge(g_in, 16)
            for n, a, b in parts:
                zk = z[0:n, a:b, KIC:KIC + HD]
                ch.step(ve.tensor_tensor(zk, zk, rs[0:n, a:b].unsqueeze(2).broadcast_to([n, b - a, HD]), ALU.mult))
                ch.step(ve.tensor_tensor(zk, zk, gk[0:n, :].unsqueeze(1).broadcast_to([n, b - a, HD]), ALU.mult))
                zw = z[0:n, a:b, WIC:WIC + IH]
                ch.step(ve.tensor_scalar(zw, zw, float(IH * HD) ** -0.5, None, ALU.mult))
                for c0, nh in ((QC, H + HKV), (QIC, IH + 1)):
                    for i in range(a, b) if n == P else (a,):
                        zh = z[0:n, i, c0:c0 + nh * HD].rearrange("p (h d) -> p h d", d=HD)
                        x1, x2 = zh[:, :, 0:RH], zh[:, :, RH:ROT]
                        cos = k.rope[0:n, i, 0:1, :].broadcast_to([n, nh, RH])
                        sin = k.rope[0:n, i, 1:2, :].broadcast_to([n, nh, RH])
                        t1, t2, t3, t4 = (x[0:n, 0:nh * RH].rearrange("p (h d) -> p h d", d=RH) for x in tm)
                        ch.mark(ve.tensor_tensor(t1, x1, cos, ALU.mult))
                        ch.mark(ve.tensor_tensor(t2, x2, sin, ALU.mult))
                        ch.mark(ve.tensor_tensor(t3, x2, cos, ALU.mult))
                        ch.step(ve.tensor_tensor(t4, x1, sin, ALU.mult))
                        ch.mark(ve.tensor_tensor(x1, t1, t2, ALU.subtract))
                        ch.step(ve.tensor_tensor(x2, t3, t4, ALU.add))
            ve.sem_inc(s_rot, 1)
            for i in range(NT - 1):
                ve.wait_ge(s_tr, i + 1)
                b = 2 * (i % 2)
                ve.tensor_copy(kT[:, :, i * P:(i + 1) * P], ps[0:HD, b, :].rearrange("p (h n) -> p h n", n=P)).then_inc(s_ev, 1)
                ve.tensor_copy(kiT[:, i * P:(i + 1) * P], ps[0:HD, b + 1, 0:P]).then_inc(s_ev, 1)

        @block.scalar
        def _(act):
            for m, (n, a, b) in enumerate(parts):
                act.wait_ge(s_ms, m + 1)
                act.activation(sd[0:n, a:b], ss[0:n, a:b], ACT.Sqrt).then_inc(s_sd, 1)

        @block.tensor
        def _(pe):
            pe.wait_ge(s_rot, 1)
            for i in range(NT - 1):
                b = 2 * (i % 2)
                if i >= 2:
                    pe.wait_ge(s_ev, 2 * (i - 1))
                for h in range(HKV):
                    pe.transpose(ps[0:HD, b, h * P:(h + 1) * P], z[:, i, KC + h * HD:KC + (h + 1) * HD], k.ident)
                pe.transpose(ps[0:HD, b + 1, 0:P], z[:, i, KIC:KIC + HD], k.ident).then_inc(s_tr, 1)


def scores(k):
    nc, t, ar, ps = k.nc, k.t, k.ar, k.ps
    z = ar.view(O_Z, NT, NA)
    kiT = ar.view(O_KIT, SEQ, p=HD)
    o = O_F1
    rl = [ar.view(o + b * SEQ, SEQ) for b in range(2)]; o += 2 * SEQ
    qiT = ar.view(o, IH, P, p=HD); o += IH * P
    wsel = ar.view(o, DB, NS, p=NS); o += DB * NS
    msel = ar.view(o, DB, NS, p=NS); o += DB * NS
    wiT = ar.view(o, DB, p=NS); o += 8
    raw, idx = ar.view(o, DB, dt=I32), ar.view(k.o_idx, DB, dt=I32); o += 8
    assert o <= O_Z
    o = O_F2
    KI = ar.view(o, DB, 16, HD); o += DB * 16 * HD
    kis = [ar.view(o + b * 512, 512) for b in range(2)]; o += 1024
    rls = [ar.view(o + b * 512, 512, p=NS) for b in range(4)]; o += 2048
    qiS = ar.view(o, DB, IH * DS); o += DB * IH * DS
    kin = ar.view(o, NS, p=HD); o += NS
    assert o <= k.end
    accs = ar.view(O_ACCS, PAST + DS, p=NS)
    names = "tr ev mm rl acc diag pt idx ki wi ms wsel ch qd sq sqc kit kic smm srl fold done new nrl nfold".split()
    s = {n: k.sem("sc_" + n) for n in names}
    nmm = IH * (NT - 1)

    with nc.Block() as block:
        @block.sync
        def _(sp):
            with nc.allow_non_contiguous_dma(reason="a few hundred values"):
                for b in range(DB):
                    sp.dma_start(raw[:, b:b + 1], t["page_table"][b, :].rearrange("(g o) -> g o", o=1).unsqueeze(1).broadcast_to([16, 8, 1])).then_inc(s["pt"], 16)
                    sp.dma_start(wiT[:, b:b + 1], t["wi"][b * DS:(b + 1) * DS, :].rearrange("q (h o) -> h q o", o=1)).then_inc(s["wi"], 16)
            sp.dma_start(msel.rearrange("p a b -> p (a b)"), t["k_msel"]).then_inc(s["ms"], 16)
            sp.wait_ge(s["sqc"], 2)
            sp.dma_start(qiS[HD:P, :, :], qiS[0:HD, :, :]).then_inc(s["qd"], 16)
            sp.wait_ge(s["qd"], 16)

        @block.gpsimd
        def _(po):
            po.wait_ge(s["idx"], 1)
            rows = t["cache_kidx"].rearrange("o n (a b) d -> (o n a) (b d)", b=16)
            for b in range(DB):
                po.indirect_dma_start(KI[:, b, :, :].rearrange("p a d -> p (a d)"), None, rows,
                                      bass.IndirectOffsetOnAxis(ap=idx[:, b:b + 1], axis=0)).then_inc(s["ki"], 16)

        @block.tensor
        def _(pe):
            for g in range(2):
                for h in range(4):
                    hh = 4 * g + h
                    ins = pe.transpose(ps[0:HD, 6, h * NS:(h + 1) * NS] if g == 0 else ps[0:HD, 7, h * NS:(h + 1) * NS],
                                       z[0:NS, NT - 1, QIC + hh * HD:QIC + (hh + 1) * HD], k.ident[0:NS, 0:NS])
                ins.then_inc(s["sq"], 1)
            for i in range(NT - 1):
                for g in range(2):
                    if i >= 1:
                        pe.wait_ge(s["ev"], 2 * (i - 1) + g + 1)
                    for h in range(4):
                        hh = 4 * g + h
                        ins = pe.transpose(ps[0:HD, 4 + g, h * P:(h + 1) * P], z[:, i, QIC + hh * HD:QIC + (hh + 1) * HD], k.ident)
                    ins.then_inc(s["tr"], 1)
                N = P * (i + 1)
                for h in range(IH):
                    n = IH * i + h
                    if h % 4 == 0:
                        pe.wait_ge(s["ev"], 2 * i + h // 4 + 1)
                    if n >= 2:
                        pe.wait_ge(s["rl"], n - 1)
                    b = 2 * (n % 2)
                    for c in range(0, N, 512):
                        w = min(512, N - c)
                        ins = pe.matmul(ps[:, b + c // 512, 0:w], qiT[:, h, :], kiT[:, c:c + w], start=True, stop=True)
                    ins.then_inc(s["mm"], 1)
            pe.wait_ge(s["qd"], 16)
            pe.wait_ge(s["ki"], 16 * DB)
            pe.wait_ge(s["wsel"], 1)
            pe.wait_ge(s["ev"], 2 * (NT - 1))
            pe.wait_ge(s["rl"], nmm)
            n = 0
            for half in range(2):
                def fold(m, par):
                    pe.wait_ge(s["srl"], 2 * m + par + 1)
                    pe.matmul(ps[0:NS, 6 + par, :], wsel[:, m % DB, :], rls[(2 * m + par) % 4], start=(m % DB == 0), stop=(m % DB == DB - 1)).then_inc(s["fold"], 1)

                for b in range(DB):
                    if n >= 2:
                        pe.wait_ge(s["kic"], n - 1)
                    for jj in range(4):
                        ins = pe.transpose(ps[:, n % 2, jj * P:(jj + 1) * P], KI[:, b, 8 * half + 2 * jj:8 * half + 2 * jj + 2, :].rearrange("p a d -> p (a d)"), k.ident)
                    ins.then_inc(s["kit"], 1)
                    pe.wait_ge(s["kic"], n + 1)
                    for par in range(2):
                        if n >= 2:
                            pe.wait_ge(s["srl"], 2 * (n - 2) + par + 1)
                        rs = slice(par * HD, (par + 1) * HD)
                        pe.matmul(ps[0:NS, 2 + 2 * (n % 2) + par, :], qiS[rs, b, :], kis[n % 2][rs, :], start=True, stop=True).then_inc(s["smm"], 1)
                    if half == 1 and b == 1:
                        pe.wait_ge(s["done"], 2)
                    if b >= 1:
                        fold(n - 1, 0)
                        fold(n - 1, 1)
                    n += 1
                fold(n - 1, 0)
                fold(n - 1, 1)
            pe.wait_ge(s["srl"], 4 * DB)
            pe.transpose(ps[0:HD, 0, 0:NS], z[0:NS, NT - 1, KIC:KIC + HD], k.ident[0:NS, 0:NS]).then_inc(s["new"], 1)
            pe.wait_ge(s["nrl"], 1)
            for b in range(DB):
                ins = pe.matmul(ps[0:NS, 2, b * DS:(b + 1) * DS], qiS[0:HD, b, :], kin[:, b * DS:(b + 1) * DS], start=True, stop=True)
            ins.then_inc(s["new"], 1)
            pe.wait_ge(s["nrl"], 2)
            pe.wait_ge(s["done"], 4)
            for b in range(DB):
                ins = pe.matmul(ps[0:NS, 6, 0:DS], wsel[:, b, :], rls[0][:, b * DS:(b + 1) * DS], start=(b == 0), stop=(b == DB - 1))
            ins.then_inc(s["nfold"], 1)

        @block.scalar
        def _(act):
            for g in range(2):
                act.wait_ge(s["sq"], g + 1)
                dst = qiS[0:HD, :, 4 * g * DS:4 * (g + 1) * DS].rearrange("p s (h q) -> p h s q", q=DS)
                for h in range(4):
                    ins = act.activation(dst[:, h, :, :], ps[0:HD, 6 + g, h * NS:(h + 1) * NS].rearrange("p (s q) -> p s q", q=DS), ACT.Copy)
                ins.then_inc(s["sqc"], 1)
            for i in range(NT - 1):
                if i >= 1:
                    act.wait_ge(s["mm"], IH * i)
                for g in range(2):
                    act.wait_ge(s["tr"], 2 * i + g + 1)
                    act.activation(qiT[:, 4 * g:4 * g + 4, :].rearrange("p a b -> p (a b)"), ps[0:HD, 4 + g, :], ACT.Copy).then_inc(s["ev"], 1)
                N = P * (i + 1)
                for h in range(IH):
                    n = IH * i + h
                    act.wait_ge(s["mm"], n + 1)
                    if n >= 2:
                        act.wait_ge(s["acc"], n - 1)
                    b = 2 * (n % 2)
                    act.activation(rl[n % 2][:, 0:N], ps[:, b:b + 2, :].rearrange("p a b -> p (a b)")[:, 0:N], ACT.Relu).then_inc(s["rl"], 1)
            for n in range(2 * DB):
                act.wait_ge(s["kit"], n + 1)
                if n >= 2:
                    act.wait_ge(s["smm"], 2 * (n - 1))
                act.activation(kis[n % 2], ps[:, n % 2, :], ACT.Copy).then_inc(s["kic"], 1)
                for par in range(2):
                    act.wait_ge(s["smm"], 2 * n + par + 1)
                    if n >= 2:
                        act.wait_ge(s["fold"], 2 * (n - 2) + par + 1)
                    act.activation(rls[(2 * n + par) % 4], ps[0:NS, 2 + 2 * (n % 2) + par, :], ACT.Relu).then_inc(s["srl"], 1)
            act.wait_ge(s["new"], 1)
            act.activation(kin, ps[0:HD, 0, 0:NS], ACT.Copy).then_inc(s["nrl"], 1)
            act.wait_ge(s["new"], 2)
            act.wait_ge(s["fold"], 4 * DB)
            act.activation(rls[0][:, 0:NS], ps[0:NS, 2, 0:NS], ACT.Relu).then_inc(s["nrl"], 1)

        @block.vector
        def _(ve):
            ch = Chain(ve, s["ch"])
            ve.wait_ge(s["pt"], 16 * DB)
            gather_index(ve, ch, k, raw, idx)
            ve.sem_inc(s["idx"], 1)
            ve.wait_ge(s["wi"], 16 * DB)
            ve.wait_ge(s["ms"], 16)
            ve.tensor_tensor(wsel, msel, wiT.unsqueeze(2).broadcast_to([NS, DB, NS]), ALU.mult).then_inc(s["wsel"], 1)
            for i in range(NT - 1):
                N = P * (i + 1)
                acc = ar.view(ACC_AT[i], N)
                for h in range(IH):
                    n = IH * i + h
                    w = z[:, i, WIC + h:WIC + h + 1]
                    ve.wait_ge(s["rl"], n + 1)
                    if h == 0:
                        ve.tensor_scalar(acc, rl[n % 2][:, 0:N], w, None, ALU.mult).then_inc(s["acc"], 1)
                    else:
                        ve.wait_ge(s["acc"], n)
                        ve.scalar_tensor_tensor(acc, rl[n % 2][:, 0:N], w, acc, ALU.mult, ALU.add).then_inc(s["acc"], 1)
                ve.wait_ge(s["acc"], IH * (i + 1))
                dg = acc[:, i * P:(i + 1) * P]
                ve.tensor_tensor(dg, dg, k.cb, ALU.add).then_inc(s["diag"], 1)
            grid = accs[:, 0:PAST].rearrange("q (p j) -> q j p", j=16)
            for half in range(2):
                for par in range(2):
                    ve.wait_ge(s["fold"], 2 * DB * (half + 1) - 1 + par)
                    ve.tensor_copy(grid[:, 8 * half + par:8 * half + 8:2, :], ps[0:NS, 6 + par, :].rearrange("q (j p) -> q j p", p=P)).then_inc(s["done"], 1)
            ve.wait_ge(s["nfold"], 1)
            ve.tensor_tensor(accs[:, PAST:PAST + DS], ps[0:NS, 6, 0:DS], k.small[0:NS, 0:DS], ALU.add).then_inc(s["done"], 1)


def select(k):
    nc, ar = k.nc, k.ar
    top, one, spare = ar.view(O_F2, 8), ar.view(O_F2 + 8, 1), ar.view(O_F2 + 16, 1)
    s_ch, s_on = k.sem("se_ch"), k.sem("se_on")
    rows = [(P, ACC_AT[i], P * (i + 1)) for i in range(NT - 1)] + [(NS, O_ACCS, PAST + DS)]

    with nc.Block() as block:
        @block.vector
        def _(ve):
            n = 0
            ve.memset(one, 1.0).then_inc(s_on, 1)
            ve.wait_ge(s_on, 1)
            for i, (r, at, N) in enumerate(rows):
                acc = ar.view(at, N, p=r)
                if P * (i + 1) > TOPK:
                    with ve.Fori(0, TOPK // 8) as j:
                        ve.max(top[0:r, :], acc).then_inc(s_ch, 1)
                        ve.wait_ge(s_ch, n + 2 * j + 1)
                        ve.tensor_copy(spare[0:r, :], one[0:r, :])
                        ve.match_replace(acc, top[0:r, :], acc, TAKEN).then_inc(s_ch, 1)
                        ve.wait_ge(s_ch, n + 2 * j + 2)
                    n += 2 * (TOPK // 8)
                    ve.tensor_scalar(acc, acc, TAKEN, OFF, ALU.not_equal, ALU.mult)
                else:
                    ve.tensor_scalar(acc, acc, 0.5 * NEG, OFF, ALU.is_lt, ALU.mult)


def prompt_attention(k):
    nc, t, ar, ps = k.nc, k.t, k.ar, k.ps
    z = ar.view(O_Z, NT, NA)
    kT, A = ar.view(O_KT, HKV, SEQ, p=HD), ar.view(O_A, NT, 512)
    o = O_F2
    qT = [ar.view(o + b * H * P, H, P, p=HD) for b in range(2)]; o += 2 * H * P
    L = [ar.view(o + b * SEQ, SEQ) for b in range(2)]; o += 2 * SEQ
    E = [ar.view(o + b * SEQ, SEQ) for b in range(2)]; o += 2 * SEQ
    PT = [ar.view(o + b * 512, 4, P) for b in range(4)]; o += 2048
    nmx, den, rden = (ar.view(o + 64 * j, H * (NT - 1)) for j in range(3)); o += 192
    assert o <= k.end
    names = "tr ev mm l mx e pt ptc pv rd o".split()
    s = {n: k.sem("at_" + n) for n in names}
    chunks = [(i, h, c) for i in range(NT - 1) for h in range(H) for c in range(0, i + 1, 4)]
    first = {}
    for m, (i, h, c) in enumerate(chunks):
        first.setdefault((i, h), m)

    with nc.Block() as block:
        @block.tensor
        def _(pe):
            def queries(i):
                if i >= 2:
                    pe.wait_ge(s["o"], i - 1)
                for g in range(2):
                    if g == 1:
                        pe.wait_ge(s["ev"], 2 * i + 1)
                    for h in range(4):
                        hh = 4 * g + h
                        ins = pe.transpose(ps[0:HD, 6 + i % 2, h * P:(h + 1) * P], z[:, i, QC + hh * HD:QC + (hh + 1) * HD], k.ident)
                    ins.then_inc(s["tr"], 1)

            def logits(i, h):
                n = H * i + h
                if h % 4 == 0:
                    pe.wait_ge(s["ev"], 2 * i + h // 4 + 1)
                if n >= 2:
                    pe.wait_ge(s["l"], n - 1)
                b, N = 2 * (n % 2), P * (i + 1)
                for c in range(0, N, 512):
                    w = min(512, N - c)
                    ins = pe.matmul(ps[:, b + c // 512, 0:w], qT[i % 2][:, h, :], kT[:, h // 2, c:c + w], start=True, stop=True)
                ins.then_inc(s["mm"], 1)

            def weigh(i, h):
                n = H * i + h
                m = first[i, h]
                pe.wait_ge(s["e"], n + 1)
                for c in range(0, i + 1, 4):
                    if m >= 2:
                        pe.wait_ge(s["ptc"], m - 1)
                    for u in range(min(4, i + 1 - c)):
                        ins = pe.transpose(ps[:, 4 + m % 2, u * P:(u + 1) * P], E[n % 2][:, (c + u) * P:(c + u + 1) * P], k.ident)
                    ins.then_inc(s["pt"], 1)
                    m += 1
                m = first[i, h]
                if h == 0:
                    pe.wait_ge(s["ev"], 2 * i + 2)
                for c in range(0, i + 1, 4):
                    pe.wait_ge(s["ptc"], m + 1)
                    for u in range(min(4, i + 1 - c)):
                        ins = pe.matmul(ps[:, 6 + i % 2, h * HD:(h + 1) * HD], PT[m % 4][:, u, :], z[:, c + u, VC + (h // 2) * HD:VC + (h // 2 + 1) * HD],
                                        start=(c + u == 0), stop=(c + u == i))
                    m += 1
                ins.then_inc(s["pv"], 1)

            queries(0)
            for n in range(H * (NT - 1) + 1):
                i, h = divmod(n, H)
                if n < H * (NT - 1):
                    logits(i, h)
                    if h == 4 and i + 1 < NT - 1:
                        queries(i + 1)
                if n >= 1:
                    weigh(*divmod(n - 1, H))

        @block.vector
        def _(ve):
            def mask(i, h):
                n, N = H * i + h, P * (i + 1)
                b = 2 * (n % 2)
                ve.wait_ge(s["mm"], n + 1)
                if n >= 2:
                    ve.wait_ge(s["e"], n - 1)
                ve.scalar_tensor_tensor(L[n % 2][:, 0:N], ps[:, b:b + 2, :].rearrange("p a b -> p (a b)")[:, 0:N], float(HD) ** -0.5,
                                        ar.view(ACC_AT[i], N), ALU.mult, ALU.add).then_inc(s["l"], 1)
                ve.wait_ge(s["l"], n + 1)
                ve.tensor_reduce(nmx[:, n:n + 1], L[n % 2][:, 0:N], AX.X, ALU.max, negate=True).then_inc(s["mx"], 1)

            def out(i):
                n = slice(H * i, H * i + H)
                ve.wait_ge(s["e"], n.stop)
                ve.reciprocal(rden[:, n], den[:, n]).then_inc(s["rd"], 1)
                ve.wait_ge(s["rd"], i + 1)
                ve.wait_ge(s["pv"], n.stop)
                ve.tensor_tensor(A[:, i, :].rearrange("p (h d) -> p h d", d=HD), ps[:, 6 + i % 2, :].rearrange("p (h d) -> p h d", d=HD),
                                 rden[:, n].unsqueeze(2).broadcast_to([P, H, HD]), ALU.mult).then_inc(s["o"], 1)

            for n in range(H * (NT - 1) + 2):
                if n < H * (NT - 1):
                    mask(*divmod(n, H))
                if n >= H and n % H == 1:
                    out(n // H - 1)

        @block.scalar
        def _(act):
            def queries(i):
                for g in range(2):
                    if i >= 2 and g == 0:
                        act.wait_ge(s["mm"], H * (i - 1))
                    act.wait_ge(s["tr"], 2 * i + g + 1)
                    act.activation(qT[i % 2][:, 4 * g:4 * g + 4, :].rearrange("p a b -> p (a b)"), ps[0:HD, 6 + i % 2, :], ACT.Copy).then_inc(s["ev"], 1)

            queries(0)
            for n in range(H * (NT - 1) + 1):
                i, h = divmod(n, H)
                if n < H * (NT - 1):
                    N = P * (i + 1)
                    if h == 4 and i + 1 < NT - 1:
                        queries(i + 1)
                    act.wait_ge(s["mx"], n + 1)
                    if n >= 2:
                        act.wait_ge(s["pt"], first.get(divmod(n - 1, H), len(chunks)))
                    act.activation(E[n % 2][:, 0:N], L[n % 2][:, 0:N], ACT.Exp, bias=nmx[:, n:n + 1], accum_out=den[:, n:n + 1]).then_inc(s["e"], 1)
                if n >= 1:
                    i, h = divmod(n - 1, H)
                    m = first[i, h]
                    for c in range(0, i + 1, 4):
                        act.wait_ge(s["pt"], m + 1)
                        if m >= 4:
                            ii, hh, _ = chunks[m - 4]
                            act.wait_ge(s["pv"], H * ii + hh + 1)
                        w = P * min(4, i + 1 - c)
                        act.activation(PT[m % 4].rearrange("p a b -> p (a b)")[:, 0:w], ps[:, 4 + m % 2, 0:w], ACT.Copy).then_inc(s["ptc"], 1)
                        m += 1


def sample_attention(k):
    nc, t, ar, ps = k.nc, k.t, k.ar, k.ps
    z, A = ar.view(O_Z, NT, NA), ar.view(O_A, NT, 512)
    mb = ar.view(O_ACCS, PAST + DS, p=NS)
    NL = PAST + NS
    Kc = [ar.view(a, 16, HKV * HD) for a in (O_KT, O_F2)]
    Vc = [ar.view(a, 16, HKV * HD) for a in (O_ACC, O_F2 + 4096)]
    o = O_KIT
    L = [ar.view(o + b * NL, NL) for b in range(2)]; o += 2 * NL
    QB = ar.view(o, DB, 2, NS); o += 2 * DB * NS
    mbn = ar.view(o, DB, DS, p=NS); o += NS
    kTn = ar.view(o, 2, NS); o += 2 * NS
    idx = ar.view(k.o_idx, DB, dt=I32)
    nmx, den, rden = (ar.view(o + 4 * j, 4) for j in range(3)); o += 12
    assert o <= O_Z, (o, O_Z)
    o = O_F2 + 8192
    kT = [ar.view(o + b * 1024, 2, 512) for b in range(2)]; o += 2048
    PT = [ar.view(o + b * 512, 512) for b in range(2)]; o += 1024
    qr = ar.view(o - 512, 2, 2, P, p=NS)
    rsel = ar.view(o, DB, NS, p=NS); o += DB * NS
    ob = ar.view(o, 256); o += 256
    assert o <= k.end, (o, k.end)
    names = "qr kc0 kc1 vc0 vc1 rs ch qt qc kn knc zero mbn kt ktc mm lc mx e ptt ptc pv rd ob out0 in".split()
    s = {n: k.sem("sa_" + n) for n in names}
    NCK = 5

    with nc.Block() as block:
        @block.sync
        def _(sp):
            sp.dma_start(rsel.rearrange("p a b -> p (a b)"), t["k_rsel"]).then_inc(s["rs"], 16)
            for pr in range(DB // 2):
                sp.wait_ge(s["ob"], pr + 1)
                for j in range(2):
                    for g in range(HKV):
                        dst = t["att"][(2 * pr + j) * DS:(2 * pr + j + 1) * DS, g * 2 * HD:(g + 1) * 2 * HD].rearrange("q (g d) -> g q d", d=HD)
                        sp.dma_start(dst, ob[j * HD + 16 * g:j * HD + 16 * g + 16, g * HD:(g + 1) * HD]).then_inc(s["out0"], 16)
            sp.wait_ge(s["out0"], 16 * DB * HKV)
            sp.dma_start(A[0:NS, NT - 1, :], t["att"]).then_inc(s["in"], 16)
            sp.wait_ge(s["in"], 16)

        @block.gpsimd
        def _(po):
            rk = t["cache_k"].rearrange("o n (a b) h d -> (o n a) (b h d)", b=16)
            rv = t["cache_v"].rearrange("o n (a b) h d -> (o n a) (b h d)", b=16)
            for b in range(DB):
                if b >= 2:
                    po.wait_ge(s["kt"], 4 * (b - 1))
                po.indirect_dma_start(Kc[b % 2].rearrange("p a d -> p (a d)"), None, rk,
                                      bass.IndirectOffsetOnAxis(ap=idx[:, b:b + 1], axis=0)).then_inc(s[f"kc{b % 2}"], 16)
                if b >= 2:
                    po.wait_ge(s["pv"], b - 1)
                po.indirect_dma_start(Vc[b % 2].rearrange("p a d -> p (a d)"), None, rv,
                                      bass.IndirectOffsetOnAxis(ap=idx[:, b:b + 1], axis=0)).then_inc(s[f"vc{b % 2}"], 16)

        @block.tensor
        def _(pe):
            pe.wait_ge(s["qr"], 2)
            for pp in range(2):
                for g in range(2):
                    ins = pe.transpose(ps[:, 6, (2 * pp + g) * NS:(2 * pp + g + 1) * NS], qr[:, pp, g, :], k.ident[0:NS, 0:NS])
            ins.then_inc(s["qt"], 1)
            for pp in range(2):
                ins = pe.transpose(ps[:, 7, pp * NS:(pp + 1) * NS], z[0:NS, NT - 1, KC + pp * P:KC + (pp + 1) * P], k.ident[0:NS, 0:NS])
            ins.then_inc(s["kn"], 1)
            pe.wait_ge(s["qc"], 8)
            pe.wait_ge(s["knc"], 1)
            pe.wait_ge(s["mbn"], 1)
            pe.wait_ge(s["rs"], 16)
            grid = mb[:, 0:PAST].rearrange("q (p j) -> q j p", j=16)

            def keys(b, c):
                m = 4 * b + c
                if c == 0:
                    pe.wait_ge(s[f"kc{b % 2}"], 16 * (b // 2 + 1))
                if m >= 2:
                    pe.wait_ge(s["ktc"], m - 1)
                for pp in range(2):
                    for u in range(4):
                        ins = pe.transpose(ps[:, 2 * (m % 2) + pp, u * P:(u + 1) * P], Kc[b % 2][:, 4 * c + u, pp * P:(pp + 1) * P], k.ident)
                ins.then_inc(s["kt"], 1)

            def logits(b, c):
                m = NCK * b + c
                if m >= 2:
                    pe.wait_ge(s["lc"], m - 1)
                rs = slice(HD * (b % 2), HD * (b % 2) + HD)
                if c < 4:
                    pe.wait_ge(s["ktc"], 4 * b + c + 1)
                    out = ps[rs, 4 + m % 2, :]
                    for pp in range(2):
                        pe.matmul(out, QB[:, b, pp, :], kT[(4 * b + c) % 2][:, pp, :], start=(pp == 0), stop=False)
                    ins = pe.matmul(out, rsel[:, b, :], grid[:, 4 * c:4 * c + 4, :], start=False, stop=True)
                else:
                    out = ps[rs, 4 + m % 2, 0:NS]
                    for pp in range(2):
                        pe.matmul(out, QB[:, b, pp, :], kTn[:, pp, :], start=(pp == 0), stop=False)
                    ins = pe.matmul(out, rsel[:, b, :], mbn.rearrange("q a b -> q (a b)"), start=False, stop=True)
                ins.then_inc(s["mm"], 1)

            def weigh(pr):
                pe.wait_ge(s["e"], pr + 1)
                if pr >= 1:
                    pe.wait_ge(s["ob"], pr)
                for c in range(NCK + 1):
                    if c < NCK:
                        m = NCK * pr + c
                        if m >= 1:
                            pe.wait_ge(s["ptc"], m)
                        for u in range(4 if c < 4 else 1):
                            w = P if c < 4 else NS
                            at = c * 512 + u * P
                            ins = pe.transpose(ps[0:w, 6, u * P:(u + 1) * P], L[pr % 2][:, at:at + w], k.ident)
                        ins.then_inc(s["ptt"], 1)
                        pe.wait_ge(s["ptc"], m + 1)
                        for j in range(2):
                            b = 2 * pr + j
                            if c == 0:
                                pe.wait_ge(s[f"vc{j}"], 16 * (pr + 1))
                            rs = slice(HD * j, HD * j + HD)
                            for u in range(4 if c < 4 else 1):
                                if c < 4:
                                    ins = pe.matmul(ps[rs, 7, 0:256], PT[m % 2][:, u * P + j * HD:u * P + (j + 1) * HD], Vc[j][:, 4 * c + u, :],
                                                    start=(c == 0 and u == 0), stop=False)
                                else:
                                    ins = pe.matmul(ps[rs, 7, 0:256], PT[m % 2][0:NS, j * HD:(j + 1) * HD], z[0:NS, NT - 1, VC:VC + 256],
                                                    start=False, stop=True)
                                    ins.then_inc(s["pv"], 1)

            for b in range(DB):
                keys(b, 0)
                for c in range(NCK):
                    if c + 1 < 4:
                        keys(b, c + 1)
                    logits(b, c)
                if b % 2 == 1:
                    weigh(b // 2)

        @block.vector
        def _(ve):
            ch = Chain(ve, s["ch"])
            for pp in range(2):
                ve.tensor_copy(qr[:, pp, :, :].rearrange("p g (c d) -> p g c d", d=HD), z[0:NS, NT - 1, QC + 4 * pp * HD:QC + (4 * pp + 4) * HD]
                               .rearrange("p (c g d) -> p g c d", g=2, d=HD)).then_inc(s["qr"], 1)
            ve.memset(QB, 0.0).then_inc(s["zero"], 1)
            ch.step(ve.tensor_scalar(mbn, k.small[0:NS, 10:18].unsqueeze(2).broadcast_to([NS, DB, DS]), -OFF, OFF, ALU.mult, ALU.add))
            ve.tensor_tensor(mbn, mbn, mb[:, PAST:PAST + DS].unsqueeze(1).broadcast_to([NS, DB, DS]), ALU.add).then_inc(s["mbn"], 1)
            ve.wait_ge(s["kn"], 1)
            ve.tensor_copy(kTn.rearrange("p a b -> p (a b)"), ps[:, 7, 0:2 * NS]).then_inc(s["knc"], 1)
            ve.wait_ge(s["zero"], 1)
            ve.wait_ge(s["qt"], 1)
            for pp in range(2):
                for g in range(2):
                    for par in range(2):
                        rs = slice(par * HD, (par + 1) * HD)
                        row = ((2 * pp + par) * 2 + g) * DS
                        ve.tensor_scalar(QB[rs, :, pp, row:row + DS], ps[rs, 6, (2 * pp + g) * NS:(2 * pp + g + 1) * NS].rearrange("p (s q) -> p s q", q=DS),
                                         float(HD) ** -0.5, None, ALU.mult).then_inc(s["qc"], 1)

            def copy_keys(m):
                ve.wait_ge(s["kt"], m + 1)
                if m >= 2:
                    b, c = divmod(m - 2, 4)
                    ve.wait_ge(s["mm"], NCK * b + c + 1)
                ve.tensor_copy(kT[m % 2].rearrange("p a b -> p (a b)"), ps[:, 2 * (m % 2):2 * (m % 2) + 2, :].rearrange("p a b -> p (a b)")).then_inc(s["ktc"], 1)

            for pr in range(DB // 2):
                for m in range(8 * pr, 8 * pr + 8):
                    copy_keys(m)
                ve.wait_ge(s["lc"], 2 * NCK * (pr + 1))
                ve.tensor_reduce(nmx[:, pr:pr + 1], L[pr % 2], AX.X, ALU.max, negate=True).then_inc(s["mx"], 1)
                ve.wait_ge(s["e"], pr + 1)
                ve.reciprocal(rden[:, pr:pr + 1], den[:, pr:pr + 1]).then_inc(s["rd"], 1)
                ve.wait_ge(s["rd"], pr + 1)
                ve.wait_ge(s["pv"], 2 * pr + 2)
                if pr >= 1:
                    ve.wait_ge(s["out0"], 16 * 8 * pr)
                ve.tensor_scalar(ob, ps[:, 7, 0:256], rden[:, pr:pr + 1], None, ALU.mult).then_inc(s["ob"], 1)

        @block.scalar
        def _(act):
            for pr in range(DB // 2):
                for m in range(2 * NCK * pr, 2 * NCK * (pr + 1)):
                    b, c = divmod(m, NCK)
                    rs = slice(HD * (b % 2), HD * (b % 2) + HD)
                    w = 512 if c < 4 else NS
                    act.wait_ge(s["mm"], m + 1)
                    if pr >= 2 and m == 2 * NCK * pr:
                        act.wait_ge(s["ptt"], NCK * (pr - 1))
                    act.activation(L[pr % 2][rs, c * 512:c * 512 + w], ps[rs, 4 + m % 2, 0:w], ACT.Copy).then_inc(s["lc"], 1)
                act.wait_ge(s["mx"], pr + 1)
                act.wait_ge(s["lc"], 2 * NCK * (pr + 1))
                act.activation(L[pr % 2], L[pr % 2], ACT.Exp, bias=nmx[:, pr:pr + 1], accum_out=den[:, pr:pr + 1]).then_inc(s["e"], 1)
                for c in range(NCK):
                    m = NCK * pr + c
                    act.wait_ge(s["ptt"], m + 1)
                    w, n = (P, 512) if c < 4 else (NS, P)
                    act.activation(PT[m % 2][0:w, 0:n], ps[0:w, 6, 0:n], ACT.Copy).then_inc(s["ptc"], 1)


NR = 4 + NE
O_RT = 46000
R_W1, R_W2, R_D1, R_D2, R_BE, R_TOK, R_LG = (O_RT + n for n in (0, 16, 32, 48, 64, 96, 128))


def project_out(k):
    nc, t, ar, ps = k.nc, k.t, k.ar, k.ps
    A, R = ar.view(O_A, NT, 512), ar.view(O_R, NT, 512)
    o = O_R + NT * 512
    wo = ar.view(o, KD, D); o += KD * D
    gt, sc, sh = (ar.view(o + j * 2 * D, 2, D) for j in range(3)); o += 6 * D
    g2 = ar.view(o, D); o += D
    x = [ar.view(o + j * D, D) for j in range(2)]; o += 2 * D
    x1 = [ar.view(o + j * D, D) for j in range(2)]; o += 2 * D
    h2 = [ar.view(o + j * D, D) for j in range(2)]; o += 2 * D
    mT = [ar.view(o + j * D, KD, P) for j in range(2)]; o += 2 * D
    hT = [ar.view(o + j * D, KD, P) for j in range(2)]; o += 2 * D
    sq = ar.view(o, D); o += D
    ga = ar.view(o, 512); o += 512
    wr = ar.view(o, KD, NR); o += KD * NR
    cols = [ar.view(o + 16 * j, NT) for j in range(8)]; o += 128
    ssa, rsa, sda, tma, ss, rs, sd, tm = cols
    assert o <= O_RT, o
    lg = ar.view(R_LG, NT, NR)
    names = "w mod ga sqa msa sda an x0 x1 t1 m1 mm gx xo h t2 h2 rt ch ss ms sd so ho init".split()
    s = {n: k.sem("po_" + n) for n in names}
    s_x1o, s_h2o = [k.sem(f"po_x1o{b}") for b in range(2)], [k.sem(f"po_h2o{b}") for b in range(2)]
    parts = ((P, 0, NT - 1), (NS, NT - 1, NT))

    with nc.Block() as block:
        @block.sync
        def _(sp):
            sp.dma_start(ga, t["attn_out_g"].broadcast_to([P, 512])).then_inc(s["ga"], 16)
            sp.dma_start(wo, t["w_out"].rearrange("o (a p) n -> p (o a) n", p=P)).then_inc(s["w"], 16)
            load_scale_shift(sp, k, s["mod"], sc, sh, (g2, t["norm2_g"]), [(gt, 2), (sc, 4), (sh, 3)])
            sp.dma_start(wr[:, :, 0:4], t["w_group"].rearrange("o (a p) n -> p (o a) n", p=P)).then_inc(s["w"], 16)
            sp.dma_start(wr[:, :, 4:NR], t["w_expert_router"].rearrange("o (a p) n -> p (o a) n", p=P)).then_inc(s["w"], 16)
            for i in range(NT):
                if i >= 2:
                    sp.wait_ge(s["xo"], i - 1)
                sp.dma_start(x[i % 2][0:ROWS[i], :], x_rows(t, i)).then_inc(s[f"x{i % 2}"], 16)
            sp.wait_ge(s["w"], 48)

        @block.gpsimd
        def _(po):
            for i in range(NT):
                po.wait_ge(s["xo"], i + 1)
                po.dma_start(tile_rows(t["x1"], i), x1[i % 2][0:ROWS[i], :]).then_inc(s_x1o[i % 2], 16)
                po.wait_ge(s["h"], i + 1)
                po.dma_start(tile_rows(t["h2"], i), h2[i % 2][0:ROWS[i], :]).then_inc(s_h2o[i % 2], 16)
            for b in range(2):
                po.wait_ge(s_x1o[b], 16 * ((NT + 1 - b) // 2))
                po.wait_ge(s_h2o[b], 16 * ((NT + 1 - b) // 2))

        @block.scalar
        def _(act):
            for m, (n, a, b) in enumerate(parts):
                for i in range(a, b):
                    if i >= 1:
                        act.wait_ge(s["sqa"], i)
                    act.activation(sq[0:n, 0:512], A[0:n, i, :], ACT.Square, accum_out=ssa[0:n, i:i + 1]).then_inc(s["sqa"], 1)
            for m, (n, a, b) in enumerate(parts):
                act.wait_ge(s["msa"], m + 1)
                act.activation(sda[0:n, a:b], ssa[0:n, a:b], ACT.Sqrt).then_inc(s["sda"], 1)
            act.wait_ge(s["sqa"], NT)
            for i in range(NT + 1):
                if i < NT:
                    r = ROWS[i]
                    act.wait_ge(s["t1"], i + 1)
                    if i >= 2:
                        act.wait_ge(s["mm"], i - 1)
                    act.activation(mT[i % 2][:, :, 0:r], ps[:, 0:2, :].rearrange("p b (a n) -> p (b a) n", n=P)[:, :, 0:r], ACT.Copy).then_inc(s["m1"], 1)
                    act.wait_ge(s["xo"], i + 1)
                    if i >= 1:
                        act.wait_ge(s["ss"], i)
                    act.activation(sq[0:r, :], x1[i % 2][0:r, :], ACT.Square, accum_out=ss[0:r, i:i + 1]).then_inc(s["ss"], 1)
                    act.wait_ge(s["ms"], i + 1)
                    act.activation(sd[0:r, i:i + 1], ss[0:r, i:i + 1], ACT.Sqrt).then_inc(s["sd"], 1)
                if i >= 1:
                    j, r = i - 1, ROWS[i - 1]
                    act.wait_ge(s["t2"], j + 1)
                    if j >= 2:
                        act.wait_ge(s["rt"], j - 1)
                    act.activation(hT[j % 2][:, :, 0:r], ps[:, 4:6, :].rearrange("p b (a n) -> p (b a) n", n=P)[:, :, 0:r], ACT.Copy).then_inc(s["h2"], 1)

        @block.tensor
        def _(pe):
            pe.wait_ge(s["w"], 48)
            pe.wait_ge(s["an"], 4)
            for i in range(NT + 1):
                if i < NT:
                    r = ROWS[i]
                    if i >= 1:
                        pe.wait_ge(s["m1"], i)
                    for a in range(KD):
                        src = A if a < 4 else R
                        ins = pe.transpose(ps[:, a // 4, (a % 4) * P:(a % 4) * P + r], src[0:r, i, (a % 4) * P:(a % 4 + 1) * P], k.ident[0:r, 0:r])
                    ins.then_inc(s["t1"], 1)
                    pe.wait_ge(s["m1"], i + 1)
                    if i >= 1:
                        pe.wait_ge(s["gx"], i)
                    for c in range(2):
                        for a in range(KD):
                            ins = pe.matmul(ps[0:r, 2 + c, :], mT[i % 2][:, a, 0:r], wo[:, a, c * 512:(c + 1) * 512], start=(a == 0), stop=(a == KD - 1))
                    ins.then_inc(s["mm"], 1)
                if i >= 1:
                    j, r = i - 1, ROWS[i - 1]
                    pe.wait_ge(s["h"], j + 1)
                    if j >= 1:
                        pe.wait_ge(s["h2"], j)
                    for a in range(KD):
                        ins = pe.transpose(ps[:, 4 + a // 4, (a % 4) * P:(a % 4) * P + r], h2[j % 2][0:r, a * P:(a + 1) * P], k.ident[0:r, 0:r])
                    ins.then_inc(s["t2"], 1)
                    pe.wait_ge(s["h2"], j + 1)
                    for a in range(KD):
                        ins = pe.matmul(ps[0:r, 6, j * NR:(j + 1) * NR], hT[j % 2][:, a, 0:r], wr[:, a, :], start=(a == 0), stop=(a == KD - 1))
                    ins.then_inc(s["rt"], 1)

        @block.vector
        def _(ve):
            ch = Chain(ve, s["ch"])
            for m, (n, a, b) in enumerate(parts):
                ve.wait_ge(s["sqa"], b)
                ve.tensor_scalar(ssa[0:n, a:b], ssa[0:n, a:b], 1.0 / 512, EPS, ALU.mult, ALU.add).then_inc(s["msa"], 1)
                ve.wait_ge(s["msa"], m + 1)
            ve.wait_ge(s["ga"], 16)
            for m, (n, a, b) in enumerate(parts):
                rstd_steps(ch, ve, lambda: ve.wait_ge(s["sda"], m + 1), ssa[0:n, a:b], rsa[0:n, a:b], sda[0:n, a:b], tma[0:n, a:b])
                ve.tensor_tensor(A[0:n, a:b, :], A[0:n, a:b, :], rsa[0:n, a:b].unsqueeze(2).broadcast_to([n, b - a, 512]), ALU.mult).then_inc(s["an"], 1)
                ve.wait_ge(s["an"], 2 * m + 1)
                ve.tensor_tensor(A[0:n, a:b, :], A[0:n, a:b, :], ga[0:n, :].unsqueeze(1).broadcast_to([n, b - a, 512]), ALU.mult).then_inc(s["an"], 1)
            ve.wait_ge(s["mod"], 16 * 7)
            ch.step(ve.scalar_tensor_tensor(sc[:, 0, :], sc[:, 0, :], 1.0, g2, ALU.add, ALU.mult))
            ch.step(ve.scalar_tensor_tensor(sc[0:NS, 1, :], sc[0:NS, 1, :], 1.0, g2[0:NS, :], ALU.add, ALU.mult))
            for i in range(NT):
                r, m = ROWS[i], int(i == NT - 1)
                col = slice(i, i + 1)
                ve.wait_ge(s["mm"], i + 1)
                if i >= 2:
                    ve.wait_ge(s_x1o[i % 2], 16 * (i // 2))
                    ve.wait_ge(s["ss"], i - 1)
                ve.tensor_tensor(x1[i % 2][0:r, :], ps[0:r, 2:4, :].rearrange("p a b -> p (a b)"), gt[0:r, m, :], ALU.mult).then_inc(s["gx"], 1)
                ve.wait_ge(s["gx"], i + 1)
                ve.wait_ge(s[f"x{i % 2}"], 16 * (i // 2 + 1))
                ve.tensor_tensor(x1[i % 2][0:r, :], x1[i % 2][0:r, :], x[i % 2][0:r, :], ALU.add).then_inc(s["xo"], 1)
                ve.wait_ge(s["ss"], i + 1)
                ve.tensor_scalar(ss[0:r, col], ss[0:r, col], 1.0 / D, EPS, ALU.mult, ALU.add).then_inc(s["ms"], 1)
                ve.wait_ge(s["ms"], i + 1)
                rstd_steps(ch, ve, lambda: ve.wait_ge(s["sd"], i + 1), ss[0:r, col], rs[0:r, col], sd[0:r, col], tm[0:r, col])
                if i >= 2:
                    ve.wait_ge(s["t2"], i - 1)
                    ve.wait_ge(s_h2o[i % 2], 16 * (i // 2))
                ch.step(ve.scalar_tensor_tensor(h2[i % 2][0:r, :], x1[i % 2][0:r, :], rs[0:r, col], sc[0:r, m, :], ALU.mult, ALU.mult))
                ve.tensor_tensor(h2[i % 2][0:r, :], h2[i % 2][0:r, :], sh[0:r, m, :], ALU.add).then_inc(s["h"], 1)
            ch.step(ve.memset(lg, 0.0))
            ve.wait_ge(s["rt"], NT)
            ch.mark(ve.tensor_copy(lg[:, 0:NT - 1, :].rearrange("p a b -> p (a b)"), ps[:, 6, 0:(NT - 1) * NR]))
            ch.step(ve.tensor_copy(lg[0:NS, NT - 1, :], ps[0:NS, 6, (NT - 1) * NR:NT * NR]))


def route(k):
    nc, t, ar, ps = k.nc, k.t, k.ar, k.ps
    lg = ar.view(R_LG, NT, NR)
    W = [ar.view(R_W1, NT), ar.view(R_W2, NT)]
    Dst = [ar.view(R_D1, NT, dt=I32), ar.view(R_D2, NT, dt=I32)]
    be, tok = ar.view(R_BE, NB, p=1, dt=I32), ar.view(R_TOK, NB, dt=I32)
    o = 0
    def new(*d, **kw):
        nonlocal o
        v = ar.view(o, *d, **kw)
        o += (int(np.prod(d)) + 15) // 16 * 16
        return v
    bias, cst = new(NR), new(128)
    pref, thr, iota_b = cst[:, 0:4], cst[:, 16:16 + NT], cst[:, 32:32 + NB]
    gm, gs, gw, m1, m2, d21, den = (new(NT) for _ in range(7))
    ge, goh, eg, oh1, oh2, key = (new(NT, 4) for _ in range(6))
    tmp4 = new(NT, 4, 4)
    M1, M2 = new(NT, 4, 4), new(NT, 4, 4)
    M, Cs, rk, pr = new(NT, NE), new(NT + 1, NE), new(NT, NE), new(NT, NE)
    cnt, nb, ends, base, onesr = new(NE), new(NE), new(NE), new(NE), new(NE)
    cmpb, cmpe = new(NE, NT), new(NB, NE, p=1)
    bef = new(NB, p=1)
    df = [new(NT), new(NT)]
    ones = new(P)
    tid, zero = new(NT, dt=I32), new(NB, dt=I32)
    tidf = new(NT)
    names = "c ch a1 a2 m rk z scat tok tid dst".split()
    s = {n: k.sem("ro_" + n) for n in names}
    table = t["tok"].rearrange("(b p) o -> p (b o)", p=P)

    with nc.Block() as block:
        @block.sync
        def _(sp):
            sp.dma_start(cst, t["k_route"].broadcast_to([P, 128])).then_inc(s["c"], 16)
            sp.dma_start(bias[:, 0:4], t["b_group"].broadcast_to([P, 4])).then_inc(s["c"], 16)
            sp.dma_start(bias[:, 4:NR], t["b_expert_router"].broadcast_to([P, NE])).then_inc(s["c"], 16)
            sp.dma_start(tidf, t["k_tid"]).then_inc(s["c"], 16)
            sp.wait_ge(s["z"], 1)
            with nc.allow_non_contiguous_dma(reason="4096 values"):
                sp.dma_start(table, zero).then_inc(s["tok"], 16)
                sp.wait_ge(s["tok"], 16)
                sp.wait_ge(s["scat"], 16 * 2 * NT)
                sp.dma_start(tok, table).then_inc(s["tok"], 16)
            sp.wait_ge(s["tok"], 32)

        @block.gpsimd
        def _(po):
            po.wait_ge(s["dst"], 2)
            po.wait_ge(s["tid"], 1)
            po.wait_ge(s["tok"], 16)
            for i in range(NT):
                for j in range(2):
                    r = ROWS[i]
                    po.indirect_dma_start(t["tok"], bass.IndirectOffsetOnAxis(ap=Dst[j][0:r, i:i + 1], axis=0), tid[0:r, i:i + 1], None).then_inc(s["scat"], 16)
            po.wait_ge(s["scat"], 16 * 2 * NT)

        @block.scalar
        def _(act):
            act.wait_ge(s["a1"], 1)
            act.activation(ge, ge, ACT.Exp).then_inc(s["a2"], 1)
            act.wait_ge(s["a1"], 2)
            act.activation(d21, d21, ACT.Exp).then_inc(s["a2"], 1)

        @block.tensor
        def _(pe):
            pe.wait_ge(s["m"], 1)
            pe.matmul(ps[:, 0, 0:NT * NE], k.tri, M.rearrange("p a b -> p (a b)"), start=True, stop=False)
            pe.matmul(ps[:, 0, 0:NT * NE], ones, Cs[:, 0:NT, :].rearrange("p a b -> p (a b)"), start=False, stop=True)
            pe.matmul(ps[:, 1, 0:NE], ones, Cs[:, NT, :], start=True, stop=True).then_inc(s["rk"], 1)

        @block.vector
        def _(ve):
            ch = Chain(ve, s["ch"])
            tt, ts = ve.tensor_tensor, ve.tensor_scalar
            ve.memset(zero, 0).then_inc(s["z"], 1)
            ch.mark(ve.memset(ones, 1.0))
            ch.mark(ve.memset(onesr, 1.0))
            ch.mark(ve.memset(Cs, 0.0))
            ve.wait_ge(s["c"], 64)
            ve.tensor_copy(tid, tidf).then_inc(s["tid"], 1)
            ch.step(tt(lg, lg, bias.unsqueeze(1).broadcast_to([P, NT, NR]), ALU.add))

            def wide(v):
                return v.unsqueeze(2).broadcast_to([P, NT, 4])

            def first_max(x, mx, oh):
                ch.step(ve.tensor_reduce(mx, x, AX.X, ALU.max))
                ch.step(tt(key, x, wide(mx), ALU.is_equal))
                ch.step(tt(key, key, pref.unsqueeze(1).broadcast_to([P, NT, 4]), ALU.mult))
                ch.step(ve.tensor_reduce(gs, key, AX.X, ALU.max))
                ch.step(tt(oh, key, wide(gs), ALU.is_equal))

            gl = lg[:, :, 0:4]
            el = lg[:, :, 4:NR].rearrange("p a (g e) -> p a g e", e=4)
            first_max(gl, gm, goh)
            tt(ge, gl, wide(gm), ALU.subtract).then_inc(s["a1"], 1)
            ch.step(tt(tmp4, el, goh.unsqueeze(3).broadcast_to([P, NT, 4, 4]), ALU.mult))
            ch.step(ve.tensor_reduce(eg, tmp4.rearrange("p a g e -> p a e g"), AX.X, ALU.add))
            first_max(eg, m1, oh1)
            ch.step(ve.scalar_tensor_tensor(eg, oh1, OFF, eg, ALU.mult, ALU.add))
            first_max(eg, m2, oh2)
            tt(d21, m2, m1, ALU.subtract).then_inc(s["a1"], 1)
            for Mj, oh in ((M1, oh1), (M2, oh2)):
                ch.step(tt(Mj, goh.unsqueeze(3).broadcast_to([P, NT, 4, 4]), oh.unsqueeze(2).broadcast_to([P, NT, 4, 4]), ALU.mult))
                ch.step(ve.memset(Mj[NS:P, NT - 1, :, :], 0.0))
            f1, f2 = (x.rearrange("p a g e -> p a (g e)") for x in (M1, M2))
            ch.step(tt(M, f1, f2, ALU.add))
            for i in range(NT):
                ch.step(tt(Cs[:, i + 1, :], Cs[:, i, :], M[:, i, :], ALU.add))
            ve.sem_inc(s["m"], 1)
            ve.wait_ge(s["a2"], 2)
            ch.step(ve.tensor_reduce(gs, ge, AX.X, ALU.add))
            ch.step(ve.reciprocal(gw, gs))
            ch.step(ts(den, d21, 1.0, None, ALU.add))
            ch.step(ve.reciprocal(gs, den))
            ch.step(tt(W[0], gw, gs, ALU.mult))
            ch.step(tt(W[1], W[0], d21, ALU.mult))
            ve.wait_ge(s["rk"], 1)
            ch.mark(ve.tensor_copy(rk.rearrange("p a b -> p (a b)"), ps[:, 0, 0:NT * NE]))
            ch.step(ve.tensor_copy(cnt, ps[:, 1, 0:NE]))
            ch.step(tt(cmpb, cnt.unsqueeze(2).broadcast_to([P, NE, NT]), thr.unsqueeze(1).broadcast_to([P, NE, NT]), ALU.is_gt))
            ch.step(ve.tensor_reduce(nb, cmpb, AX.X, ALU.add))
            ch.step(ve.tensor_tensor_scan(ends, onesr, nb, 0.0, ALU.mult, ALU.add))
            ch.step(tt(base, ends, nb, ALU.subtract))
            ch.step(ts(base, base, float(P), None, ALU.mult))
            ch.step(tt(rk, rk, base.unsqueeze(1).broadcast_to([P, NT, NE]), ALU.add))
            for j, f in enumerate((f1, f2)):
                ch.step(tt(pr, rk, f, ALU.mult))
                ch.step(ve.tensor_reduce(df[j], pr, AX.X, ALU.add))
                ve.tensor_copy(Dst[j], df[j]).then_inc(s["dst"], 1)
            ch.step(tt(cmpe, iota_b[0:1, :].unsqueeze(2).broadcast_to([1, NB, NE]), ends[0:1, :].unsqueeze(1).broadcast_to([1, NB, NE]), ALU.is_ge))
            ch.step(ve.tensor_reduce(bef, cmpe, AX.X, ALU.add))
            ch.step(ts(bef, bef, float(NE - 1), None, ALU.min))
            ch.step(ve.tensor_copy(be, bef))


def experts(k):
    nc, t, ar, ps = k.nc, k.t, k.ar, k.ps
    be, tok = ar.view(R_BE, NB, p=1, dt=I32), ar.view(R_TOK, NB, dt=I32)
    o = 0
    Wt = []
    for b in range(2):
        Wt.append((ar.view(o, KD, FE), ar.view(o + 4096, KD, FE), ar.view(o + 8192, 4, D)))
        o += 12288
    X = [ar.view(o + b * D, D) for b in range(2)]; o += 2 * D
    XT = [ar.view(o + b * D, KD, P) for b in range(2)]; o += 2 * D
    sg, hh = ar.view(o, FE), ar.view(o + FE, FE); o += 2 * FE
    hT = ar.view(o, 4, P); o += 512
    Y = [ar.view(o + b * D, D) for b in range(2)]; o += 2 * D
    assert o <= O_RT, o
    names = "t xt gu sg h ht htc y yc xe".split()
    s = {n: k.sem("ex_" + n) for n in names}
    s_w, s_x, s_yo = ([k.sem(f"ex_{n}{b}") for b in range(2)] for n in ("w", "x", "yo"))
    w1, w3 = (t[n].rearrange("o e (a p) f -> p (o e) a f", p=P) for n in ("w1", "w3"))
    w2 = t["w2"].rearrange("o e (a p) d -> p (o e) a d", p=P)

    def loops(eng, body):
        for b in range(2):
            body(b, b, True)
        with eng.Fori(1, NB // 2) as i:
            for b in range(2):
                body(2 * i + b, b, False)

    with nc.Block() as block:
        @block.sync
        def _(sp):
            def body(n, b, first):
                e = sp.value_load(be[0:1, bass.ds(n, 1)], min_val=0, max_val=NE - 1)
                if not first:
                    sp.wait_ge(s["y"], n - 1)
                for dst, src in zip(Wt[b], (w1, w3, w2)):
                    sp.dma_start(dst, src[:, bass.ds(e, 1), :, :].rearrange("p o a f -> p (o a) f")).then_inc(s_w[b], 16)
            loops(sp, body)

        @block.gpsimd
        def _(po):
            def body(n, b, first):
                if not first:
                    po.wait_ge(s["t"], n - 1)
                po.indirect_dma_start(X[b], None, t["h2"], bass.IndirectOffsetOnAxis(ap=tok[:, n:n + 1], axis=0)).then_inc(s_x[b], 16)
            for n in range(NB):
                body(n, n % 2, n < 2)

        @block.tensor
        def _(pe):
            def turn(n, b, first):
                pe.wait_ge(s_x[b], (n // 2 + 1) * 16)
                if not (isinstance(n, int) and n == 0):
                    pe.wait_ge(s["xt"], n)
                for a in range(KD):
                    ins = pe.transpose(ps[:, a // 4, (a % 4) * P:(a % 4 + 1) * P], X[b][:, a * P:(a + 1) * P], k.ident)
                ins.then_inc(s["t"], 1)

            def body(n, i, b, last):
                pe.wait_ge(s_w[b], (i + 1) * 48)
                pe.wait_ge(s["xt"], n + 1)
                if not (isinstance(n, int) and n == 0):
                    pe.wait_ge(s["h"], n)
                for m in range(2):
                    for a in range(KD):
                        ins = pe.matmul(ps[:, 2 + m, :], XT[b][:, a, :], Wt[b][m][:, a, :], start=(a == 0), stop=(a == KD - 1))
                ins.then_inc(s["gu"], 1)
                if not last:
                    pe.wait_ge(s_x[1 - b], (i + 1 + b) * 16)
                    for a in range(KD):
                        ins = pe.transpose(ps[:, a // 4, (a % 4) * P:(a % 4 + 1) * P], X[1 - b][:, a * P:(a + 1) * P], k.ident)
                    ins.then_inc(s["t"], 1)
                pe.wait_ge(s["h"], n + 1)
                for a in range(4):
                    ins = pe.transpose(ps[:, 4, a * P:(a + 1) * P], hh[:, a * P:(a + 1) * P], k.ident)
                ins.then_inc(s["ht"], 1)
                pe.wait_ge(s["htc"], n + 1)
                if not (isinstance(n, int) and n == 0):
                    pe.wait_ge(s["yc"], n)
                for c in range(2):
                    for a in range(4):
                        ins = pe.matmul(ps[:, 5 + c, :], hT[:, a, :], Wt[b][2][:, a, c * 512:(c + 1) * 512], start=(a == 0), stop=(a == 3))
                ins.then_inc(s["y"], 1)

            turn(0, 0, True)
            body(0, 0, 0, False)
            body(1, 0, 1, False)
            with pe.Fori(1, NB // 2 - 1) as i:
                body(2 * i, i, 0, False)
                body(2 * i + 1, i, 1, False)
            body(NB - 2, NB // 2 - 1, 0, False)
            body(NB - 1, NB // 2 - 1, 1, True)

        @block.scalar
        def _(act):
            def body(n, b, first):
                act.wait_ge(s["t"], n + 1)
                if not first:
                    act.wait_ge(s["gu"], n - 1)
                act.activation(XT[b].rearrange("p a b -> p (a b)"), ps[:, 0:2, :].rearrange("p a b -> p (a b)"), ACT.Copy).then_inc(s["xt"], 1)
                act.wait_ge(s["gu"], n + 1)
                if not (isinstance(n, int) and n == 0):
                    act.wait_ge(s["h"], n)
                act.activation(sg, ps[:, 2, :], ACT.Silu).then_inc(s["sg"], 1)
                act.wait_ge(s["y"], n + 1)
                if not first:
                    act.wait_ge(s_yo[b], (n - b) * 8)
                act.activation(Y[b], ps[:, 5:7, :].rearrange("p a b -> p (a b)"), ACT.Copy).then_inc(s["yc"], 1)
                act.wait_ge(s["yc"], n + 1)
                act.dma_start(t["yslot"][bass.ds(n * P, P), :], Y[b]).then_inc(s_yo[b], 16)
            loops(act, body)
            for b in range(2):
                act.wait_ge(s_yo[b], 16 * NB // 2)

        @block.vector
        def _(ve):
            def body(n, b, first):
                ve.wait_ge(s["sg"], n + 1)
                if not (isinstance(n, int) and n == 0):
                    ve.wait_ge(s["ht"], n)
                ve.tensor_tensor(hh, sg, ps[:, 3, :], ALU.mult).then_inc(s["h"], 1)
                ve.wait_ge(s["ht"], n + 1)
                if not (isinstance(n, int) and n == 0):
                    ve.wait_ge(s["y"], n)
                ve.tensor_copy(hT.rearrange("p a b -> p (a b)"), ps[:, 4, :]).then_inc(s["htc"], 1)
            loops(ve, body)


def combine(k):
    nc, t, ar, ps = k.nc, k.t, k.ar, k.ps
    W = [ar.view(R_W1, NT), ar.view(R_W2, NT)]
    Dst = [ar.view(R_D1, NT, dt=I32), ar.view(R_D2, NT, dt=I32)]
    o = 0
    gt, sc, sh = (ar.view(o + j * 2 * D, 2, D) for j in range(3)); o += 6 * D
    g = ar.view(o, D); o += D
    NBF = 3
    x1 = [ar.view(o + j * D, D) for j in range(NBF)]; o += NBF * D
    ya = [ar.view(o + j * D, D) for j in range(NBF)]; o += NBF * D
    yb = [ar.view(o + j * D, D) for j in range(NBF)]; o += NBF * D
    out = [ar.view(o + j * D, D) for j in range(NBF)]; o += NBF * D
    sq = ar.view(o, D); o += D
    ss, rs, sd, tm = (ar.view(o + 16 * j, NT) for j in range(4)); o += 64
    s = {n: k.sem("co_" + n) for n in "mod ss ms sd ch done res".split()}
    s_x, s_a, s_b, s_o = ([k.sem(f"co_{n}{b}") for b in range(NBF)] for n in ("x", "a", "b", "o"))

    with nc.Block() as block:
        @block.sync
        def _(sp):
            load_scale_shift(sp, k, s["mod"], sc, sh, (g, t["final_g"].rearrange("(o n) -> o n", o=1)), [(gt, 5), (sc, 7), (sh, 6)])
            for i in range(NT + 1):
                if i < NT:
                    if i >= NBF:
                        sp.wait_ge(s["done"], i - NBF + 1)
                    sp.dma_start(x1[i % NBF][0:ROWS[i], :], tile_rows(t["x1"], i)).then_inc(s_x[i % NBF], 16)
                if i >= 1:
                    j = i - 1
                    sp.wait_ge(s["done"], j + 1)
                    dst = t["y_prompt"].rearrange("o s d -> (o s) d")[j * P:(j + 1) * P, :] if j < NT - 1 else t["y_sample"].rearrange("b s d -> (b s) d")
                    sp.dma_start(dst, out[j % NBF][0:ROWS[j], :]).then_inc(s_o[j % NBF], 16)
            for b in range(NBF):
                sp.wait_ge(s_o[b], 16 * ((NT + NBF - 1 - b) // NBF))

        @block.gpsimd
        def _(po):
            for i in range(NT):
                r = ROWS[i]
                if i >= NBF:
                    po.wait_ge(s["done"], i - NBF + 1)
                for y, sm, d in ((ya, s_a, Dst[0]), (yb, s_b, Dst[1])):
                    po.indirect_dma_start(y[i % NBF][0:r, :], None, t["yslot"], bass.IndirectOffsetOnAxis(ap=d[0:r, i:i + 1], axis=0)).then_inc(sm[i % NBF], 16)

        @block.scalar
        def _(act):
            for i in range(NT):
                r = ROWS[i]
                act.wait_ge(s["res"], i + 1)
                if i >= 1:
                    act.wait_ge(s["ss"], i)
                act.activation(sq[0:r, :], x1[i % NBF][0:r, :], ACT.Square, accum_out=ss[0:r, i:i + 1]).then_inc(s["ss"], 1)
                act.wait_ge(s["ms"], i + 1)
                act.activation(sd[0:r, i:i + 1], ss[0:r, i:i + 1], ACT.Sqrt).then_inc(s["sd"], 1)

        @block.vector
        def _(ve):
            ch = Chain(ve, s["ch"])
            ve.wait_ge(s["mod"], 16 * 7)
            ch.step(ve.scalar_tensor_tensor(sc[:, 0, :], sc[:, 0, :], 1.0, g, ALU.add, ALU.mult))
            ch.step(ve.scalar_tensor_tensor(sc[0:NS, 1, :], sc[0:NS, 1, :], 1.0, g[0:NS, :], ALU.add, ALU.mult))
            for i in range(NT):
                r, m, b, col = ROWS[i], int(i == NT - 1), i % NBF, slice(i, i + 1)
                n = 16 * (i // NBF + 1)
                a_, b_, x_ = ya[b][0:r, :], yb[b][0:r, :], x1[b][0:r, :]
                ve.wait_ge(s_a[b], n)
                ch.step(ve.tensor_scalar(a_, a_, W[0][0:r, col], None, ALU.mult))
                ve.wait_ge(s_b[b], n)
                ch.step(ve.scalar_tensor_tensor(a_, b_, W[1][0:r, col], a_, ALU.mult, ALU.add))
                ch.step(ve.tensor_tensor(a_, a_, gt[0:r, m, :], ALU.mult))
                ve.wait_ge(s_x[b], n)
                ve.tensor_tensor(x_, x_, a_, ALU.add).then_inc(s["res"], 1)
                ve.wait_ge(s["ss"], i + 1)
                ve.tensor_scalar(ss[0:r, col], ss[0:r, col], 1.0 / D, EPS, ALU.mult, ALU.add).then_inc(s["ms"], 1)
                ve.wait_ge(s["ms"], i + 1)
                rstd_steps(ch, ve, lambda: ve.wait_ge(s["sd"], i + 1), ss[0:r, col], rs[0:r, col], sd[0:r, col], tm[0:r, col])
                if i >= NBF:
                    ve.wait_ge(s_o[b], 16 * (i // NBF))
                ve.wait_ge(s["res"], i + 1)
                ch.step(ve.scalar_tensor_tensor(out[b][0:r, :], x_, rs[0:r, col], sc[0:r, m, :], ALU.mult, ALU.mult))
                ve.tensor_tensor(out[b][0:r, :], out[b][0:r, :], sh[0:r, m, :], ALU.add).then_inc(s["done"], 1)


_INS = ["x_prompt", "x_sample", "cache_k", "cache_v", "cache_kidx", "state_hgrn", "page_table", "c_prompt",
        "c_sample", "ada_w", "ada_b", "norm1_g", "norm2_g", "w_in", "idx_k_g", "hg_lb_logits", "attn_out_g",
        "hg_out_g", "w_out", "w_group", "b_group", "w_expert_router", "b_expert_router", "w1", "w3", "w2",
        "final_g", "ada_final_w", "ada_final_b"]
_OUTS = [("y_prompt", (1, SEQ, D)), ("y_sample", (DB, DS, D)),
         ("k_prompt", (1, 1, SEQ, HKV, HD)), ("v_prompt", (1, 1, SEQ, HKV, HD)), ("kidx_prompt", (1, 1, SEQ, HD)),
         ("hgrn_prompt", (1, 1, GH, DK, DK)),
         ("k_sample", (1, DB, DS, HKV, HD)), ("v_sample", (1, DB, DS, HKV, HD)), ("kidx_sample", (1, DB, DS, HD)),
         ("hgrn_sample", (1, DB, GH, DK, DK))]
_SCRATCH = [("mod", (1 + DB, 8 * D), F32), ("wi", (NS, IH), F32), ("att", (NS, 512), F32),
            ("x1", (T, D), F32), ("h2", (T, D), F32), ("tok", (NB * P, 1), I32), ("yslot", (NB * P, D), F32)]


def constants():
    p = np.arange(P)
    half = ROT // 2
    inv = (np.float32(THETA) ** (-np.arange(half, dtype=np.float32) * np.float32(2.0 / ROT))).astype(np.float32)
    pos = np.concatenate([np.arange(SEQ), PAST + p % DS]).astype(np.float32).reshape(NT, P)
    ang = (pos[:, :, None] * inv).astype(np.float32)
    rope = np.stack([np.cos(ang), np.sin(ang)], 2).transpose(1, 0, 2, 3)
    tri = (p[:, None] < p[None, :])
    causal = np.where(p[None, :] <= p[:, None], 0.0, NEG)
    small = np.zeros((P, 64))
    for j in range(DS):
        small[:, j] = np.where(j <= p % DS, 0.0, NEG)
    small[:, 8] = p % 8
    small[:, 9] = p
    small[:, 10:18] = (p[:, None] // DS == np.arange(DB)[None, :])
    cols = np.arange(T)
    reset = np.where(cols < SEQ, cols % C != 0, cols % DS != 0)[None, :]
    q = np.arange(C)
    m0 = np.tile(p[:, None] % C <= q[None, :], (1, 4))
    m1 = np.tile((p[:, None] <= q) & (p[:, None] // DS == q // DS), (1, 4))
    qmask = (np.arange(DB)[:, None] == np.arange(NS)[None, :] // DS).reshape(1, -1)
    r = np.arange(NS)
    sq = np.arange(DB)[:, None] * DS
    rsel = r[:, None, None] == (sq + (r % DS)[None, :])[None]
    msel = np.stack([(r[None, :] == (b * DS + r % DS)[:, None]) for b in range(DB)], 1)
    rt = np.zeros((1, 128))
    rt[0, 0:4] = [4, 3, 2, 1]
    rt[0, 16:16 + NT] = np.arange(NT) * P
    rt[0, 32:32 + NB] = np.arange(NB)
    tid = np.arange(NT)[None, :] * P + p[:, None]
    return {"k_route": rt, "k_tid": tid, "k_rsel": rsel.reshape(NS, -1), "k_msel": msel.reshape(NS, -1), "k_reset": reset, "k_masks": np.concatenate([m0, m1], 1), "k_qmask": qmask, "k_ident": np.eye(P), "k_rope": rope.reshape(P, -1), "k_tri": tri, "k_causal": causal, "k_small": small}


def kernel(**inputs):
    import concourse.bacc as _bacc
    from concourse.bass_utils import run_bass_kernel_spmd as _run

    nc = _bacc.Bacc("TRN2", target_bir_lowering=False, num_devices=1)
    arrays, t = {}, {}
    for name in _INS:
        a = np.ascontiguousarray(inputs[name])
        arrays["in_" + name] = a
        t[name] = nc.dram_tensor("in_" + name, a.shape, mybir.dt.from_np(a.dtype), kind="ExternalInput").ap()
    for name, a in constants().items():
        a = np.ascontiguousarray(a, np.float32)
        arrays[name] = a
        t[name] = nc.dram_tensor(name, a.shape, F32, kind="ExternalInput").ap()
    for name, shape in _OUTS:
        t[name] = nc.dram_tensor("out_" + name, shape, F32, kind="ExternalOutput").ap()
    for name, shape, dt in _SCRATCH:
        t[name] = nc.dram_tensor("tmp_" + name, shape, dt, kind="Internal").ap()
    build(nc, t)
    r = _run(nc, [arrays], core_ids=[0])
    return tuple(r.results[0]["out_" + name] for name, _ in _OUTS)
```

```python
from contextlib import ExitStack

import concourse.bass as bass
import numpy as np
from concourse import mybir

F32 = mybir.dt.float32
I32 = mybir.dt.int32
ALU = mybir.AluOpType
ACT = mybir.ActivationFunctionType
AX = mybir.AxisListType

P = 128
D = 1024
KD = D // P
SEQ = 1024
DB, DS = 8, 8
NS = DB * DS
T = SEQ + NS
NT = SEQ // P + 1
ROWS = [P] * (NT - 1) + [NS]
PAST, PAGE, POOL_PAGES = 2048, 128, 160
H, HKV, HD = 8, 4, 64
IH = 8
ROT, THETA = 16, 500000.0
RH = ROT // 2
TOPK = 256
GH, DK, C = 4, 128, 64
N_IN = 3656
HQ0, HF0, HI0, HG0 = 1608, 2120, 2632, 3144
NA = 1608
NE, FE = 16, 512
A_TOT = 2 * T
NB = (A_TOT - NE) // P + NE
EPS = 1e-6
NEG, TAKEN = -3.0e38, -3.3e38
OFF = -1.0e30


class Arena:

    def __init__(self, tensor, size):
        self.t, self.size = tensor, size

    def view(self, off, *dims, p=P, dt=F32):
        n = int(np.prod(dims))
        assert off + n <= self.size, (off, n)
        ap = self.t[0:p, off:off + n]
        if dt != F32:
            ap = ap.bitcast(dt)
        if len(dims) == 2:
            ap = ap.rearrange("p (a b) -> p a b", b=dims[1])
        if len(dims) == 3:
            ap = ap.rearrange("p (a b c) -> p a b c", b=dims[1], c=dims[2])
        return ap


class Chain:

    def __init__(self, eng, sem, base=0):
        self.eng, self.sem, self.n = eng, sem, base

    def step(self, ins):
        self.mark(ins)
        self.join()

    def mark(self, ins):
        self.n = self.n + 1
        ins.then_inc(self.sem, 1)

    def join(self):
        self.eng.wait_ge(self.sem, self.n)


def build(nc, t):
    ctx = ExitStack()
    with ctx:
        size = 52800
        ar = Arena(ctx.enter_context(nc.sbuf_tensor("arena", [P, size], F32)), size)
        ps = ctx.enter_context(nc.psum_tensor("banks", [P, 8, 512], F32))
        k = Ctx(nc, ctx, t, ar, ps)
        stages = [modulation, norm_in, project_attn, rope, index, prompt_attention, sample_attention,
                  hgrn, project_out, route, experts, combine]
        for stage in stages:
            stage(k)
            k.next_stage()


class Ctx:
    def __init__(self, nc, ctx, t, ar, ps):
        self.nc, self.ctx, self.t, self.ar, self.ps = nc, ctx, t, ar, ps
        o = ar.size
        def take(n):
            nonlocal o
            o -= n
            return o
        self.o_ident = take(P)
        self.o_rope = take(NT * 2 * RH)
        self.o_tri = take(P)
        self.o_cb = take(P)
        self.o_small = take(64)
        self.o_idx = take(8)
        self.end = o
        self.ident = ar.view(self.o_ident, P)
        self.rope = ar.view(self.o_rope, NT, 2, RH)
        self.tri = ar.view(self.o_tri, P)
        self.cb = ar.view(self.o_cb, P)
        self.small = ar.view(self.o_small, 64)

        self.used = []

    def sem(self, name):
        self.used.append(self.nc.alloc_semaphore(name))
        return self.used[-1]

    def next_stage(self):
        self.nc.clear_and_free_semaphores(self.used)
        self.nc.all_engine_barrier()
        self.used = []


def modulation(k):
    nc, t, ar, ps = k.nc, k.t, k.ar, k.ps
    NC, NADA, W = 1 + DB, 12, 512
    csb = ar.view(0, D, p=NC)
    cT = ar.view(1024, KD, NC)
    ones = ar.view(1100, NC, p=1)
    bias = ar.view(1200, 16 * W, p=1)
    wch = [ar.view(9400 + b * KD * W, KD, W) for b in range(3)]
    row = [ar.view(9400 + (3 * KD + b) * W, W, p=NC) for b in range(2)]
    mod_const, mod_c, mod_bias = k.sem("mod_const"), k.sem("mod_c"), k.sem("mod_bias")
    mod_silu, mod_ct, mod_cts, mod_ones = k.sem("mod_silu"), k.sem("mod_ct"), k.sem("mod_cts"), k.sem("mod_ones")
    w_in, mm_done, row_done, row_out = [k.sem(f"mod_w{b}") for b in range(3)], k.sem("mod_mm"), k.sem("mod_row"), [k.sem(f"mod_out{b}") for b in range(2)]
    ada_v = t["ada_w"].rearrange("o (a p) n -> p (o a) n", p=P)
    fin_v = t["ada_final_w"].rearrange("(a p) n -> p a n", p=P)

    with nc.Block() as block:
        @block.sync
        def _(sp):
            sp.dma_start(csb[0:1, :], t["c_prompt"]).then_inc(mod_c, 16)
            sp.dma_start(csb[1:NC, :], t["c_sample"]).then_inc(mod_c, 16)
            sp.dma_start(k.ident, t["k_ident"]).then_inc(mod_const, 16)
            sp.dma_start(k.rope, t["k_rope"]).then_inc(mod_const, 16)
            sp.dma_start(k.tri, t["k_tri"]).then_inc(mod_const, 16)
            sp.dma_start(k.cb, t["k_causal"]).then_inc(mod_const, 16)
            sp.dma_start(k.small, t["k_small"]).then_inc(mod_const, 16)
            sp.dma_start(bias[:, 0:NADA * W], t["ada_b"]).then_inc(mod_bias, 16)
            sp.dma_start(bias[:, NADA * W:16 * W], t["ada_final_b"].rearrange("(o n) -> o n", o=1)).then_inc(mod_bias, 16)

            def load(n, b):
                sp.dma_start(wch[b], ada_v[:, :, bass.ds(n * W, W)]).then_inc(w_in[b], 16)

            for b in range(3):
                load(b, b)
            with sp.Fori(1, NADA // 3) as i:
                for b in range(3):
                    sp.wait_ge(mm_done, 3 * i + b - 2)
                    load(3 * i + b, b)
            for n in range(NADA, 16):
                sp.wait_ge(mm_done, n - 2)
                sp.dma_start(wch[n % 3], fin_v[:, :, (n - NADA) * W:(n - NADA + 1) * W]).then_inc(w_in[n % 3], 16)
            sp.wait_ge(mod_const, 80)

        @block.scalar
        def _(act):
            act.wait_ge(mod_c, 32)
            act.activation(csb, csb, ACT.Silu).then_inc(mod_silu, 1)

            def store(n, b):
                act.wait_ge(row_done, n + 1)
                act.dma_start(t["mod"][:, bass.ds(n * W, W)], row[b]).then_inc(row_out[b], 16)

            with act.Fori(0, 8) as i:
                for b in range(2):
                    store(2 * i + b, b)
            for b in range(2):
                act.wait_ge(row_out[b], 16 * 8)

        @block.tensor
        def _(pe):
            pe.wait_ge(mod_silu, 1)
            pe.wait_ge(mod_const, 80)
            for a in range(KD):
                ins = pe.transpose(ps[:, 7, NC * a:NC * a + NC], csb[:, a * P:(a + 1) * P], k.ident[0:NC, 0:NC])
            ins.then_inc(mod_ct, 1)
            pe.wait_ge(mod_cts, 1)
            pe.wait_ge(mod_ones, 1)
            pe.wait_ge(mod_bias, 32)

            for n in range(16):
                pe.wait_ge(w_in[n % 3], 16 * (n // 3 + 1))
                if n >= 2:
                    pe.wait_ge(row_done, n - 1)
                for a in range(KD):
                    pe.matmul(ps[0:NC, n % 2, :], cT[:, a, :], wch[n % 3][:, a, :], start=(a == 0), stop=False)
                pe.matmul(ps[0:NC, n % 2, :], ones, bias[:, n * W:(n + 1) * W], start=False, stop=True).then_inc(mm_done, 1)

        @block.vector
        def _(ve):
            ve.memset(ones, 1.0).then_inc(mod_ones, 1)
            ve.wait_ge(mod_ct, 1)
            ve.tensor_copy(cT.rearrange("p a b -> p (a b)"), ps[:, 7, 0:KD * NC]).then_inc(mod_cts, 1)
            for n in range(16):
                ve.wait_ge(mm_done, n + 1)
                if n >= 2:
                    ve.wait_ge(row_out[n % 2], 16 * (n // 2))
                ve.tensor_copy(row[n % 2], ps[0:NC, n % 2, :]).then_inc(row_done, 1)


HT = 0
def load_scale_shift(eng, k, sem, scale, shift, g, parts):
    t = k.t
    for (dst, col) in parts:
        eng.dma_start(dst[:, 0, :], t["mod"][0:1, col * D:(col + 1) * D].broadcast_to([P, D])).then_inc(sem, 16)
        eng.dma_start(dst[0:NS, 1, :], t["mod"][1:1 + DB, col * D:(col + 1) * D].unsqueeze(1).broadcast_to([DB, DS, D])).then_inc(sem, 16)
    if g is not None:
        eng.dma_start(g[0], g[1].broadcast_to([P, D])).then_inc(sem, 16)


def tile_rows(t, i):
    return t[i * P:i * P + ROWS[i], :]


def x_rows(t, i):
    if i < NT - 1:
        return t["x_prompt"].rearrange("o s d -> (o s) d")[i * P:(i + 1) * P, :]
    return t["x_sample"].rearrange("b s d -> (b s) d")


def rstd_steps(ch, ve, act_sqrt, ms, y, w1, w2):
    act_sqrt()
    ch.step(ve.reciprocal(y, w1))
    ch.step(ve.tensor_tensor(w2, y, y, ALU.mult))
    ch.step(ve.tensor_tensor(w2, w2, ms, ALU.mult))
    ch.step(ve.tensor_scalar(w2, w2, -0.5, 1.5, ALU.mult, ALU.add))
    ch.step(ve.tensor_tensor(y, y, w2, ALU.mult))


def norm_in(k):
    nc, t, ar, ps = k.nc, k.t, k.ar, k.ps
    hT = ar.view(HT, KD, T)
    o = KD * T
    x = [ar.view(o + b * D, D) for b in range(3)]; o += 3 * D
    h = [ar.view(o + b * D, D) for b in range(2)]; o += 2 * D
    sq = ar.view(o, D); o += D
    sc, sh = ar.view(o, 2, D), ar.view(o + 2 * D, 2, D); o += 4 * D
    g = ar.view(o, D); o += D
    ss, ms, sd, rs, tmp = (ar.view(o + 16 * j, NT) for j in range(5))
    s_mod, s_x, s_ss, s_ms, s_sd = k.sem("ni_mod"), [k.sem(f"ni_x{b}") for b in range(3)], k.sem("ni_ss"), k.sem("ni_ms"), k.sem("ni_sd")
    s_h, s_t, s_hT, s_ch = k.sem("ni_h"), k.sem("ni_t"), k.sem("ni_hT"), k.sem("ni_ch")

    with nc.Block() as block:
        @block.sync
        def _(sp):
            load_scale_shift(sp, k, s_mod, sc, sh, (g, t["norm1_g"]), [(sc, 1), (sh, 0)])
            for i in range(NT):
                if i >= 3:
                    sp.wait_ge(s_h, i - 2)
                sp.dma_start(x[i % 3][0:ROWS[i], :], x_rows(t, i)).then_inc(s_x[i % 3], 16)

        @block.scalar
        def _(act):
            for i in range(NT + 1):
                if i < NT:
                    r = ROWS[i]
                    act.wait_ge(s_x[i % 3], 16 * (i // 3 + 1))
                    if i >= 1:
                        act.wait_ge(s_ss, i)
                    act.activation(sq[0:r, :], x[i % 3][0:r, :], ACT.Square, accum_out=ss[0:r, i:i + 1]).then_inc(s_ss, 1)
                    act.wait_ge(s_ms, i + 1)
                    act.activation(sd[0:r, i:i + 1], ms[0:r, i:i + 1], ACT.Sqrt).then_inc(s_sd, 1)
                if i >= 1:
                    j, r = i - 1, ROWS[i - 1]
                    act.wait_ge(s_t, j + 1)
                    act.activation(hT[:, :, j * P:j * P + r], ps[:, 2 * (j % 2):2 * (j % 2) + 2, :].rearrange("p b (a n) -> p (b a) n", n=P)[:, :, 0:r], ACT.Copy).then_inc(s_hT, 1)

        @block.tensor
        def _(pe):
            for i in range(NT):
                r = ROWS[i]
                pe.wait_ge(s_h, i + 1)
                if i >= 2:
                    pe.wait_ge(s_hT, i - 1)
                for a in range(KD):
                    ins = pe.transpose(ps[:, 2 * (i % 2) + a // 4, (a % 4) * P:(a % 4) * P + r], h[i % 2][0:r, a * P:(a + 1) * P], k.ident[0:r, 0:r])
                ins.then_inc(s_t, 1)

        @block.vector
        def _(ve):
            ch = Chain(ve, s_ch)
            ve.wait_ge(s_mod, 16 * 5)
            ch.step(ve.scalar_tensor_tensor(sc[:, 0, :], sc[:, 0, :], 1.0, g, ALU.add, ALU.mult))
            ch.step(ve.scalar_tensor_tensor(sc[0:NS, 1, :], sc[0:NS, 1, :], 1.0, g[0:NS, :], ALU.add, ALU.mult))
            for i in range(NT):
                r, m = ROWS[i], int(i == NT - 1)
                col = slice(i, i + 1)
                ve.wait_ge(s_ss, i + 1)
                ve.tensor_scalar(ms[0:r, col], ss[0:r, col], 1.0 / D, EPS, ALU.mult, ALU.add).then_inc(s_ms, 1)
                rstd_steps(ch, ve, lambda: ve.wait_ge(s_sd, i + 1), ms[0:r, col], rs[0:r, col], sd[0:r, col], tmp[0:r, col])
                if i >= 2:
                    ve.wait_ge(s_t, i - 1)
                ch.step(ve.scalar_tensor_tensor(h[i % 2][0:r, :], x[i % 3][0:r, :], rs[0:r, col], sc[0:r, m, :], ALU.mult, ALU.mult))
                ve.tensor_tensor(h[i % 2][0:r, :], h[i % 2][0:r, :], sh[0:r, m, :], ALU.add).then_inc(s_h, 1)


O_A = 0
O_R = NT * 512
O_Z = KD * T
O_ACC = O_Z + NT * NA
O_ACCS = O_ACC + P * (NT - 1) * NT // 2
O_KIT = O_ACCS + PAST + DS
O_F = O_KIT + SEQ
O_KT = NT * 512
QC, KC, VC, QIC, KIC, WIC = 0, 512, 768, 1024, 1536, 1600
ACC_AT = [O_ACC + P * i * (i + 1) // 2 for i in range(NT - 1)]
O_K = O_R + NT * 512
O_HQ = O_K + 12288
O_HF = O_HQ + GH * T
O_V = O_HF + GH * T
O_G = O_V + NT * 512
O_END = O_G + NT * 512


def project(k, name, jobs):
    nc, t, ar, ps = k.nc, k.t, k.ar, k.ps
    hT = ar.view(HT, KD, T)
    w = [ar.view(O_F + b * KD * 512, KD, 512) for b in range(3)]
    w_v = t["w_in"].rearrange("o (a p) n -> p (o a) n", p=P)
    s_w = [k.sem(f"{name}_w{b}") for b in range(3)]
    s_mm, s_ev, s_ev2 = k.sem(name + "_mm"), k.sem(name + "_ev"), k.sem(name + "_ev2")
    groups = []
    for j, (c0, wd, kind, dst) in enumerate(jobs):
        if kind == "tok":
            for i in range(NT):
                groups.append((j, ROWS[i], wd, (lambda a, i=i, j=j: hT[:, a, i * P:i * P + ROWS[i]]),
                               (lambda a, j=j, wd=wd: w[j % 3][:, a, 0:wd]), dst[0:ROWS[i], i, :]))
        else:
            for f in range(wd // P):
                for s, n in ((0, 512), (512, 512), (1024, NS)):
                    groups.append((j, P, n, (lambda a, f=f, j=j: w[j % 3][:, a, f * P:(f + 1) * P]),
                                   (lambda a, s=s, n=n: hT[:, a, s:s + n]), dst[:, f, s:s + n]))
    last = {g[0]: n for n, g in enumerate(groups)}
    NBK = 6

    with nc.Block() as block:
        @block.sync
        def _(sp):
            for j, (c0, wd, kind, dst) in enumerate(jobs):
                if j >= 3:
                    sp.wait_ge(s_mm, last[j - 3] + 1)
                sp.dma_start(w[j % 3][:, :, 0:wd], w_v[:, :, c0:c0 + wd]).then_inc(s_w[j % 3], 16)

        @block.tensor
        def _(pe):
            for n, (j, m, cols, lhs, rhs, dst) in enumerate(groups):
                if n == 0 or groups[n - 1][0] != j:
                    pe.wait_ge(s_w[j % 3], 16 * (j // 3 + 1))
                if n >= NBK:
                    pe.wait_ge((s_ev, s_ev2)[n % 2], (n - NBK) // 2 + 1)
                for a in range(KD):
                    ins = pe.matmul(ps[0:m, n % NBK, 0:cols], lhs(a), rhs(a), start=(a == 0), stop=(a == KD - 1))
                ins.then_inc(s_mm, 1)

        @block.vector
        def _(ve):
            for n, (j, m, cols, lhs, rhs, dst) in enumerate(groups):
                if n % 2 == 0:
                    ve.wait_ge(s_mm, n + 1)
                    ve.tensor_copy(dst, ps[0:m, n % NBK, 0:cols]).then_inc(s_ev, 1)

        @block.scalar
        def _(act):
            for n, (j, m, cols, lhs, rhs, dst) in enumerate(groups):
                if n % 2 == 1:
                    act.wait_ge(s_mm, n + 1)
                    act.activation(dst, ps[0:m, n % NBK, 0:cols], ACT.Copy).then_inc(s_ev2, 1)


def hgrn(k):
    nc, t, ar, ps = k.nc, k.t, k.ar, k.ps
    NCH = SEQ // C
    Q, F = ar.view(O_HQ, GH, T), ar.view(O_HF, GH, T)
    K, B = ar.view(O_K, GH, T), ar.view(O_K + GH * T, GH, T)
    o = O_K + 2 * GH * T
    reset = ar.view(o, T); o += T
    mask = ar.view(o, 2, 4 * C, dt=I32); o += 8 * C
    kst = [ar.view(o + b * 512, 512) for b in range(2)]; o += 1024
    BL, EBL = ar.view(o, GH, NCH + DB), ar.view(o + 96, GH, NCH + DB); o += 192
    lbl, lb, oml = ar.view(o, GH, 2), ar.view(o + 8, GH), ar.view(o + 12, GH); o += 16
    lbm, lbe, lbs = ar.view(o, GH), ar.view(o + 4, GH, 2), ar.view(o + 12, GH); o += 16
    ssq, rs, tmp, sd = (ar.view(o + 36 * j, NT * GH) for j in range(4)); o += 144
    assert o <= O_HQ
    V, G, R = ar.view(O_V, NT, 512), ar.view(O_G, NT, 512), ar.view(O_R, NT, 512)
    o = O_END
    att = [ar.view(o + b * 256, 4 * C) for b in range(2)]; o += 512
    S = [ar.view(o + b * 512, GH, DK) for b in range(2)]; o += 1024
    sq = ar.view(o, 512); o += 512
    gn = ar.view(o, 512); o += 512
    o_s0 = o
    S0 = ar.view(o, DB, GH * DK); o += DB * GH * DK
    vm = ar.view(o, DB, DK); o += DB * DK
    qp = ar.view(o, DB * NS); o += DB * NS
    assert o <= k.end, (o, k.end)
    qmk = ar.view(o_s0 - 512, DB * NS)

    names = ("const lb lbd lbe sig f k ln b eb q enb kin d est kst ebl g gate zero att attm tr trc ds s1 s2 o oc red"
             " ch out s0 qm vm qp sds st so soc fin zf zq zv").split()
    s = {n: k.sem("hg_" + n) for n in names}
    SB = slice(SEQ, T)

    with nc.Block() as block:
        @block.sync
        def _(sp):
            sp.dma_start(F, t["hf"]).then_inc(s["zf"], 16)
            sp.dma_start(Q, t["hq"]).then_inc(s["zq"], 16)
            for dst, src in ((V, t["hv"]), (G, t["hg"])):
                sp.dma_start(dst[:, 0:NT - 1, :], src[:, 0:NT - 1, :]).then_inc(s["zv"], 16)
                sp.dma_start(dst[0:NS, NT - 1, :], src[0:NS, NT - 1, :]).then_inc(s["zv"], 16)
            sp.dma_start(reset, t["k_reset"].broadcast_to([P, T])).then_inc(s["const"], 16)
            sp.dma_start(mask.rearrange("p a b -> p (a b)"), t["k_masks"].bitcast(I32)).then_inc(s["const"], 16)
            sp.dma_start(gn, t["hg_out_g"].broadcast_to([P, 512])).then_inc(s["g"], 16)
            with nc.allow_non_contiguous_dma(reason="1024 values"):
                for j in range(2):
                    sp.dma_start(lbl[:, :, j], t["hg_lb_logits"][j, :].rearrange("(h p) -> p h", p=P)).then_inc(s["lb"], 16)
            sp.dma_start(S0.rearrange("p s (h e) -> p s h e", e=DK), t["state_hgrn"].rearrange("o s h p e -> p (o s) h e")).then_inc(s["s0"], 16)
            sp.wait_ge(s["gate"], 2)
            sp.dma_start(qmk, t["k_qmask"].broadcast_to([P, DB * NS])).then_inc(s["qm"], 16)
            sp.wait_ge(s["s2"], 4 * (NT - 1))
            sp.dma_start(t["hgrn_prompt"].rearrange("a b h p e -> p (a b h) e"), S[0]).then_inc(s["out"], 16)
            sp.wait_ge(s["st"], 2 * GH)
            sp.dma_start(t["hgrn_sample"].rearrange("o s h p e -> p (o s) h e"), S0.rearrange("p s (h e) -> p s h e", e=DK)).then_inc(s["out"], 16)
            sp.wait_ge(s["out"], 32)

        @block.scalar
        def _(act):
            act.wait_ge(s["zf"], 16)
            for h in range(GH):
                act.activation(F[:, h, :], F[:, h, :], ACT.Sigmoid).then_inc(s["sig"], 1)
            act.wait_ge(s["lbd"], 1)
            act.activation(lbe.rearrange("p a b -> p (a b)"), lbl.rearrange("p a b -> p (a b)"), ACT.Exp).then_inc(s["lbe"], 1)
            for h in range(GH):
                act.wait_ge(s["k"], h + 1)
                act.activation(F[:, h, :], F[:, h, :], ACT.Ln).then_inc(s["ln"], 1)
            for h in range(GH):
                act.wait_ge(s["b"], h + 1)
                act.activation(F[:, h, :], B[:, h, :], ACT.Exp).then_inc(s["eb"], 1)
            act.activation(EBL, BL, ACT.Exp).then_inc(s["ebl"], 1)
            for h in range(GH):
                act.wait_ge(s["q"], h + 1)
                act.activation(F[:, h, :], B[:, h, :], ACT.Exp, scale=-1.0).then_inc(s["enb"], 1)
            for h in range(GH):
                act.wait_ge(s["d"], h + 1)
                act.activation(B[:, h, :], B[:, h, :], ACT.Exp).then_inc(s["est"], 1)
            act.wait_ge(s["zv"], 64)
            act.activation(G[:, 0:NT - 1, :], G[:, 0:NT - 1, :], ACT.Silu).then_inc(s["fin"], 1)
            act.activation(G[0:NS, NT - 1, :], G[0:NS, NT - 1, :], ACT.Silu).then_inc(s["fin"], 1)
            for i in range(NT):
                r = ROWS[i]
                act.wait_ge(s["tr"], i + 1)
                if i >= 2:
                    act.wait_ge(s["ds"], 2 * (i - 1))
                act.activation(kst[i % 2][0:r, :], ps[0:r, 2 + i % 2, :], ACT.Copy).then_inc(s["trc"], 1)
                act.wait_ge(s["o"], i + 1)
                act.activation(R[0:r, i, :], ps[0:r, 6 + i % 2, :], ACT.Copy).then_inc(s["oc"], 1)
                if i >= 1:
                    act.wait_ge(s["red"], i)
                act.activation(sq[0:r, :], ps[0:r, 6 + i % 2, :], ACT.Square).then_inc(s["oc"], 1)
            act.wait_ge(s["soc"], 1)
            act.activation(sd, tmp, ACT.Sqrt).then_inc(s["so"], 1)

        @block.tensor
        def _(pe):
            pe.wait_ge(s["zv"], 64)
            pe.wait_ge(s["kin"], GH)
            pe.wait_ge(s["kst"], GH)
            for i in range(NT - 1):
                for h in range(GH):
                    for j in range(2):
                        cs = slice(i * P + j * C, i * P + (j + 1) * C)
                        ins = pe.matmul(ps[j * C:(j + 1) * C, i % 2, h * C:(h + 1) * C], F[:, h, cs], Q[:, h, cs], start=True, stop=True)
                ins.then_inc(s["att"], 1)
                if i >= 2:
                    pe.wait_ge(s["trc"], i - 1)
                for h in range(GH):
                    ins = pe.transpose(ps[:, 2 + i % 2, h * DK:(h + 1) * DK], K[:, h, i * P:(i + 1) * P], k.ident)
                ins.then_inc(s["tr"], 1)
                pe.wait_ge(s["trc"], i + 1)
                for j in range(2):
                    if i >= 1:
                        pe.wait_ge(s[("s1", "s2")[j]], 4 * i)
                    for h in range(GH):
                        hs = slice(h * DK, (h + 1) * DK)
                        ins = pe.matmul(ps[:, 4 + j, hs], kst[i % 2][j * C:(j + 1) * C, hs], V[j * C:(j + 1) * C, i, hs], start=True, stop=True)
                    ins.then_inc(s["ds"], 1)
                pe.wait_ge(s["attm"], i + 1)
                if i >= 2:
                    pe.wait_ge(s["oc"], 2 * (i - 1))
                pe.wait_ge(s["zero"], 5)
                for j in range(2):
                    if j == 1:
                        pe.wait_ge(s["s1"], 4 * (i + 1))
                    elif i >= 1:
                        pe.wait_ge(s["s2"], 4 * i)
                    for h in range(GH):
                        hs, cs = slice(h * DK, (h + 1) * DK), slice(i * P + j * C, i * P + (j + 1) * C)
                        js = slice(j * C, (j + 1) * C)
                        pe.matmul(ps[js, 6 + i % 2, hs], att[i % 2][js, h * C:(h + 1) * C], V[js, i, hs], start=True, stop=False)
                        ins = pe.matmul(ps[js, 6 + i % 2, hs], Q[:, h, cs], S[j][:, h, :], start=False, stop=True)
                ins.then_inc(s["o"], 1)
            i = NT - 1
            for h in range(GH):
                ins = pe.matmul(ps[0:NS, 0, h * NS:(h + 1) * NS], F[:, h, SB], Q[:, h, SB], start=True, stop=True)
            ins.then_inc(s["att"], 1)
            pe.wait_ge(s["trc"], i - 1)
            for h in range(GH):
                ins = pe.transpose(ps[0:NS, 2, h * DK:(h + 1) * DK], K[:, h, SB], k.ident)
            ins.then_inc(s["tr"], 1)
            pe.wait_ge(s["trc"], i + 1)
            pe.wait_ge(s["s2"], 4 * i)
            pe.wait_ge(s["attm"], i + 1)
            pe.wait_ge(s["oc"], 2 * (i - 1))
            for h in range(GH):
                hs = slice(h * DK, (h + 1) * DK)
                pe.wait_ge(s["vm"], h + 1)
                if h >= 1:
                    pe.wait_ge(s["st"], 2 * h)
                for j in range(2):
                    ins = pe.matmul(ps[:, 4 + j, :], kst[0][0:NS, hs], vm[0:NS, 4 * j:4 * j + 4, :], start=True, stop=True)
                ins.then_inc(s["sds"], 1)
                pe.matmul(ps[0:NS, 6, hs], att[0][0:NS, h * NS:(h + 1) * NS], V[0:NS, i, hs], start=True, stop=False)
                pe.wait_ge(s["qp"], h + 1)
                if h == 0:
                    pe.wait_ge(s["s0"], 16)
                for b in range(DB):
                    ins = pe.matmul(ps[0:NS, 6, hs], qp[:, b * NS:(b + 1) * NS], S0[:, b, hs], start=False, stop=(b == DB - 1))
                ins.then_inc(s["sds"], 1)
            pe.wait_ge(s["sds"], 2 * GH)
            pe.sem_inc(s["o"], 1)

        @block.vector
        def _(ve):
            ch = Chain(ve, s["ch"])
            for a in att:
                ve.memset(a, 0.0).then_inc(s["zero"], 1)
            for a in S:
                ve.memset(a, 0.0).then_inc(s["zero"], 1)
            ve.memset(ssq, 0.0).then_inc(s["zero"], 1)
            ve.wait_ge(s["lb"], 32)
            ch.step(ve.tensor_tensor(lbm, lbl[:, :, 0], lbl[:, :, 1], ALU.max))
            ch.mark(ve.tensor_tensor(lbl[:, :, 0], lbl[:, :, 0], lbm, ALU.subtract))
            ve.tensor_tensor(lbl[:, :, 1], lbl[:, :, 1], lbm, ALU.subtract).then_inc(s["lbd"], 1)
            ve.wait_ge(s["lbe"], 1)
            ch.step(ve.tensor_tensor(lbs, lbe[:, :, 0], lbe[:, :, 1], ALU.add))
            ch.step(ve.reciprocal(lbm, lbs))
            ch.step(ve.tensor_tensor(lb, lbe[:, :, 0], lbm, ALU.mult))
            ch.step(ve.tensor_scalar(oml, lb, -1.0, 1.0, ALU.mult, ALU.add))
            for h in range(GH):
                ve.wait_ge(s["sig"], h + 1)
                ve.tensor_scalar(F[:, h, :], F[:, h, :], oml[:, h:h + 1], lb[:, h:h + 1], ALU.mult, ALU.add).then_inc(s["f"], 1)
                ve.wait_ge(s["f"], h + 1)
                ve.tensor_scalar(K[:, h, :], F[:, h, :], -1.0, 1.0, ALU.mult, ALU.add).then_inc(s["k"], 1)
            ve.wait_ge(s["const"], 32)
            for h in range(GH):
                ve.wait_ge(s["ln"], h + 1)
                ch.step(ve.tensor_tensor_scan(B[:, h, :], reset, F[:, h, :], 0.0, ALU.mult, ALU.add))
                ch.mark(ve.tensor_copy(BL[:, h, 0:NCH], B[:, h, C - 1:SEQ:C]))
                ve.tensor_copy(BL[:, h, NCH:NCH + DB], B[:, h, SEQ + DS - 1:T:DS]).then_inc(s["b"], 1)
            ve.wait_ge(s["zq"], 16)
            for h in range(GH):
                ve.wait_ge(s["eb"], h + 1)
                ve.scalar_tensor_tensor(Q[:, h, :], Q[:, h, :], float(DK) ** -0.5, F[:, h, :], ALU.mult, ALU.mult).then_inc(s["q"], 1)
            ch.join()
            ve.wait_ge(s["b"], GH)
            for h in range(GH):
                ve.wait_ge(s["enb"], h + 1)
                ve.tensor_tensor(F[:, h, :], K[:, h, :], F[:, h, :], ALU.mult).then_inc(s["kin"], 1)
                ch.mark(ve.tensor_tensor(B[:, h, 0:SEQ].rearrange("p (a c) -> p a c", c=C), BL[:, h, 0:NCH].unsqueeze(2).broadcast_to([P, NCH, C]),
                                         B[:, h, 0:SEQ].rearrange("p (a c) -> p a c", c=C), ALU.subtract))
                ve.tensor_tensor(B[:, h, SB].rearrange("p (a c) -> p a c", c=DS), BL[:, h, NCH:NCH + DB].unsqueeze(2).broadcast_to([P, DB, DS]),
                                 B[:, h, SB].rearrange("p (a c) -> p a c", c=DS), ALU.subtract).then_inc(s["d"], 1)
            for h in range(GH):
                ve.wait_ge(s["est"], h + 1)
                ve.tensor_tensor(K[:, h, :], K[:, h, :], B[:, h, :], ALU.mult).then_inc(s["kst"], 1)
            ve.wait_ge(s["fin"], 2)
            ve.wait_ge(s["g"], 16)
            ve.tensor_tensor(G[:, 0:NT - 1, :], G[:, 0:NT - 1, :], gn.unsqueeze(1).broadcast_to([P, NT - 1, 512]), ALU.mult).then_inc(s["gate"], 1)
            ve.tensor_tensor(G[0:NS, NT - 1, :], G[0:NS, NT - 1, :], gn[0:NS, :], ALU.mult).then_inc(s["gate"], 1)
            ve.wait_ge(s["zero"], 5)
            ve.wait_ge(s["ebl"], 1)

            def sums(i):
                r = ROWS[i]
                ve.wait_ge(s["oc"], 2 * (i + 1))
                ve.tensor_reduce(ssq[0:r, i * GH:(i + 1) * GH], sq[0:r, :].rearrange("p (h e) -> p h e", e=DK), AX.X, ALU.add).then_inc(s["red"], 1)

            for i in range(NT - 1):
                ve.wait_ge(s["att"], i + 1)
                if i >= 2:
                    ve.wait_ge(s["o"], i - 1)
                ve.copy_predicated(att[i % 2], mask[:, 0, :], ps[:, i % 2, 0:4 * C]).then_inc(s["attm"], 1)
                for j in range(2):
                    ve.wait_ge(s["ds"], 2 * i + j + 1)
                    if j == 0 and i >= 1:
                        ve.wait_ge(s["s2"], 4 * i)
                        ve.wait_ge(s["o"], i)
                    if j == 1:
                        ve.wait_ge(s["s1"], 4 * (i + 1))
                        ve.wait_ge(s["o"], i + 1)
                    for h in range(GH):
                        hs = slice(h * DK, (h + 1) * DK)
                        dst = S[1] if j == 0 else S[0]
                        ve.scalar_tensor_tensor(dst[:, h, :], S[j][:, h, :], EBL[:, h, 2 * i + j:2 * i + j + 1], ps[:, 4 + j, hs], ALU.mult, ALU.add).then_inc(s[("s1", "s2")[j]], 1)
                sums(i)
            i = NT - 1
            ve.wait_ge(s["att"], i + 1)
            ch.step(ve.memset(att[0][0:NS, :], 0.0))
            ve.copy_predicated(att[0][0:NS, :], mask[0:NS, 1, :], ps[0:NS, 0, 0:4 * NS]).then_inc(s["attm"], 1)
            ve.wait_ge(s["qm"], 16)
            ve.wait_ge(s["s0"], 16)
            ve.wait_ge(s["zv"], 64)
            for h in range(GH):
                hs = slice(h * DK, (h + 1) * DK)
                if h >= 1:
                    ve.wait_ge(s["sds"], 2 * h)
                ve.tensor_tensor(vm[0:NS, :, :], V[0:NS, i, hs].unsqueeze(1).broadcast_to([NS, DB, DK]),
                                 k.small[0:NS, 10:18].unsqueeze(2).broadcast_to([NS, DB, DK]), ALU.mult).then_inc(s["vm"], 1)
                ve.tensor_tensor(qp.rearrange("p (a b) -> p a b", b=NS), Q[:, h, SB].unsqueeze(1).broadcast_to([P, DB, NS]),
                                 qmk.rearrange("p (a b) -> p a b", b=NS), ALU.mult).then_inc(s["qp"], 1)
                ve.wait_ge(s["sds"], 2 * h + 2)
                ch.step(ve.tensor_tensor(S0[:, :, hs], S0[:, :, hs], EBL[:, h, NCH:NCH + DB].unsqueeze(2).broadcast_to([P, DB, DK]), ALU.mult))
                for j in range(2):
                    ve.tensor_tensor(S0[:, 4 * j:4 * j + 4, hs], S0[:, 4 * j:4 * j + 4, hs], ps[:, 4 + j, :].rearrange("p (a b) -> p a b", b=DK), ALU.add).then_inc(s["st"], 1)
            sums(i)
            ve.wait_ge(s["red"], NT)
            ve.tensor_scalar(tmp, ssq, 1.0 / DK, EPS, ALU.mult, ALU.add).then_inc(s["soc"], 1)
            ve.wait_ge(s["soc"], 1)
            ch.mark(ve.tensor_copy(ssq, tmp))
            rstd_steps(ch, ve, lambda: ve.wait_ge(s["so"], 1), ssq, rs, sd, tmp)
            for rr, ii in ((slice(0, P), slice(0, NT - 1)), (slice(0, NS), slice(NT - 1, NT))):
                n, m = rr.stop, ii.stop - ii.start
                Rv = R[rr, ii, :].rearrange("p a (h e) -> p (a h) e", e=DK)
                ch.step(ve.tensor_tensor(Rv, Rv, rs[rr, ii.start * GH:ii.stop * GH].unsqueeze(2).broadcast_to([n, m * GH, DK]), ALU.mult))
                ch.step(ve.tensor_tensor(R[rr, ii, :], R[rr, ii, :], G[rr, ii, :], ALU.mult))


def project_attn(k):
    ar = k.ar
    z = ar.view(O_Z, NT, NA)
    project(k, "pa", [(0, 512, "tok", z[:, :, 0:512]), (512, 512, "tok", z[:, :, 512:1024]),
                      (1024, 512, "tok", z[:, :, 1024:1536]), (1536, 72, "tok", z[:, :, 1536:NA])])


def gather_index(ve, ch, k, raw, idx):
    ch.step(ve.tensor_scalar(idx, raw, 8.0, k.small[:, 8:9], ALU.mult, ALU.add))


def rope(k):
    nc, t, ar, ps = k.nc, k.t, k.ar, k.ps
    z = ar.view(O_Z, NT, NA)
    kiT = ar.view(O_KIT, SEQ, p=HD)
    o = O_F
    gk = ar.view(o, HD); o += HD
    kk = ar.view(o, NT, HD); o += NT * HD
    ss, rs, sd, tmp = (ar.view(o + 16 * j, NT) for j in range(4)); o += 64
    tm = [ar.view(o + j * 96 * 8, 96 * 8) for j in range(4)]
    g_in, ch_s, v_out, kv_out = k.sem("rp_g"), k.sem("rp_ch"), k.sem("rp_v"), k.sem("rp_kv")
    s_ms, s_sd, s_rot, s_tr, s_ev = (k.sem("rp_" + n) for n in ("ms", "sd", "rot", "tr", "ev"))
    parts = ((P, 0, NT - 1), (NS, NT - 1, NT))

    def store(eng, sem, name, c0, w):
        a = t[name + "_prompt"]
        a = a.rearrange("a b (i p) h d -> p (a b i) (h d)", p=P) if len(a.shape) == 5 else a.rearrange("a b (i p) d -> p (a b i) d", p=P)
        eng.dma_start(a, z[:, 0:NT - 1, c0:c0 + w]).then_inc(sem, 16)
        a = t[name + "_sample"]
        a = a.rearrange("a b s h d -> (a b s) (h d)") if len(a.shape) == 5 else a.rearrange("a b s d -> (a b s) d")
        eng.dma_start(a, z[0:NS, NT - 1, c0:c0 + w]).then_inc(sem, 16)

    with nc.Block() as block:
        @block.sync
        def _(sp):
            sp.dma_start(gk, t["idx_k_g"].broadcast_to([P, HD])).then_inc(g_in, 16)
            store(sp, v_out, "v", VC, HKV * HD)
            sp.wait_ge(s_rot, 1)
            store(sp, kv_out, "k", KC, HKV * HD)
            store(sp, kv_out, "kidx", KIC, HD)
            sp.dma_start(t["wi"], z[0:NS, NT - 1, WIC:WIC + IH]).then_inc(kv_out, 16)
            sp.wait_ge(v_out, 32)
            sp.wait_ge(kv_out, 16 * 5)

        @block.vector
        def _(ve):
            ch = Chain(ve, ch_s)
            for n, a, b in parts:
                ch.step(ve.tensor_tensor(kk[0:n, a:b, :], z[0:n, a:b, KIC:KIC + HD], z[0:n, a:b, KIC:KIC + HD], ALU.mult))
                ch.step(ve.tensor_reduce(ss[0:n, a:b], kk[0:n, a:b, :], AX.X, ALU.add))
                ve.tensor_scalar(ss[0:n, a:b], ss[0:n, a:b], 1.0 / HD, EPS, ALU.mult, ALU.add).then_inc(s_ms, 1)
            for m, (n, a, b) in enumerate(parts):
                rstd_steps(ch, ve, lambda: ve.wait_ge(s_sd, m + 1), ss[0:n, a:b], rs[0:n, a:b], sd[0:n, a:b], tmp[0:n, a:b])
            ve.wait_ge(g_in, 16)
            for n, a, b in parts:
                zk = z[0:n, a:b, KIC:KIC + HD]
                ch.step(ve.tensor_tensor(zk, zk, rs[0:n, a:b].unsqueeze(2).broadcast_to([n, b - a, HD]), ALU.mult))
                ch.step(ve.tensor_tensor(zk, zk, gk[0:n, :].unsqueeze(1).broadcast_to([n, b - a, HD]), ALU.mult))
                zw = z[0:n, a:b, WIC:WIC + IH]
                ch.step(ve.tensor_scalar(zw, zw, float(IH * HD) ** -0.5, None, ALU.mult))
                for c0, nh in ((QC, H + HKV), (QIC, IH + 1)):
                    for i in range(a, b) if n == P else (a,):
                        zh = z[0:n, i, c0:c0 + nh * HD].rearrange("p (h d) -> p h d", d=HD)
                        x1, x2 = zh[:, :, 0:RH], zh[:, :, RH:ROT]
                        cos = k.rope[0:n, i, 0:1, :].broadcast_to([n, nh, RH])
                        sin = k.rope[0:n, i, 1:2, :].broadcast_to([n, nh, RH])
                        t1, t2, t3, t4 = (x[0:n, 0:nh * RH].rearrange("p (h d) -> p h d", d=RH) for x in tm)
                        ch.mark(ve.tensor_tensor(t1, x1, cos, ALU.mult))
                        ch.mark(ve.tensor_tensor(t2, x2, sin, ALU.mult))
                        ch.mark(ve.tensor_tensor(t3, x2, cos, ALU.mult))
                        ch.step(ve.tensor_tensor(t4, x1, sin, ALU.mult))
                        ch.mark(ve.tensor_tensor(x1, t1, t2, ALU.subtract))
                        ch.step(ve.tensor_tensor(x2, t3, t4, ALU.add))
            ve.sem_inc(s_rot, 1)
            for i in range(NT - 1):
                ve.wait_ge(s_tr, i + 1)
                b = 2 * (i % 2)
                ve.tensor_copy(kiT[:, i * P:(i + 1) * P], ps[0:HD, b, 0:P]).then_inc(s_ev, 1)

        @block.scalar
        def _(act):
            for m, (n, a, b) in enumerate(parts):
                act.wait_ge(s_ms, m + 1)
                act.activation(sd[0:n, a:b], ss[0:n, a:b], ACT.Sqrt).then_inc(s_sd, 1)

        @block.tensor
        def _(pe):
            pe.wait_ge(s_rot, 1)
            for i in range(NT - 1):
                b = 2 * (i % 2)
                if i >= 2:
                    pe.wait_ge(s_ev, i - 1)
                pe.transpose(ps[0:HD, b, 0:P], z[:, i, KIC:KIC + HD], k.ident).then_inc(s_tr, 1)


def index(k):
    nc, t, ar, ps = k.nc, k.t, k.ar, k.ps
    z, hT = ar.view(O_Z, NT, NA), ar.view(HT, KD, T)
    kiT = ar.view(O_KIT, SEQ, p=HD)
    o = O_F
    wp = [ar.view(o + b * KD * 512, KD, 512) for b in range(2)]; o += 2 * KD * 512
    stage = [ar.view(o + b * 512, 512) for b in range(4)]; o += 2048
    rl = [ar.view(o + b * SEQ, SEQ) for b in range(2)]; o += 2 * SEQ
    qiT = ar.view(o, IH, P, p=HD); o += IH * P
    wsel = ar.view(o, DB, NS, p=NS); o += DB * NS
    msel = ar.view(o, DB, NS, p=NS); o += DB * NS
    wiT = ar.view(o, DB, p=NS); o += 8
    raw, idx, idh = ar.view(o, DB, dt=I32), ar.view(k.o_idx, DB, dt=I32), ar.view(o + 8, 2, DB, dt=I32); o += 24
    NKI = 4
    KI = [ar.view(o + b * 512, 8, HD) for b in range(NKI)]; o += NKI * 512
    kis = [ar.view(o + b * 512, 512) for b in range(2)]; o += 1024
    rls = [ar.view(o + b * 512, 512, p=NS) for b in range(4)]; o += 2048
    qiS = ar.view(o, DB, IH * DS); o += DB * IH * DS
    kin = ar.view(o, NS, p=HD); o += NS
    top = [ar.view(o + 8 * j, 8) for j in range(2)]; o += 16
    one, spare = ar.view(o, 1), [ar.view(o + 4 + 4 * j, 1) for j in range(2)]; o += 16
    assert o <= k.end, (o, k.end)
    accs = ar.view(O_ACCS, PAST + DS, p=NS)
    names = "tr ev mm rl acc diag pt idx wi ms wsel ch qd sq sqc kit kic smm srl fold done new nrl nfold top on pmm pev".split()
    s = {n: k.sem("ix_" + n) for n in names}
    s_ki, s_pw, s_st = [k.sem(f"ix_ki{b}") for b in range(NKI)], [k.sem(f"ix_pw{b}") for b in range(2)], [k.sem(f"ix_st{b}") for b in range(4)]
    nmm = IH * (NT - 1)
    FIRST, SECOND = 4, 6
    LATE, PB = 4, (6, 7, 0, 1)

    w_v = t["w_in"].rearrange("o (a p) n -> p (o a) n", p=P)
    chunks = ((HF0, "feat", t["hf"]), (HQ0, "feat", t["hq"]), (HI0, "tok", t["hv"]), (HG0, "tok", t["hg"]))
    groups = []
    for j, (c0, kind, dst) in enumerate(chunks):
        if kind == "tok":
            for i in range(NT):
                groups.append((j, ROWS[i], 512, (lambda a, i=i: hT[:, a, i * P:i * P + ROWS[i]]),
                               (lambda a, j=j: wp[j % 2][:, a, :]), dst[0:ROWS[i], i, :]))
        else:
            for f in range(GH):
                for c, n in ((0, 512), (512, 512), (1024, NS)):
                    groups.append((j, P, n, (lambda a, f=f, j=j: wp[j % 2][:, a, f * P:(f + 1) * P]),
                                   (lambda a, c=c, n=n: hT[:, a, c:c + n]), dst[:, f, c:c + n]))
    last = {g[0]: n for n, g in enumerate(groups)}

    with nc.Block() as block:
        @block.sync
        def _(sp):
            with nc.allow_non_contiguous_dma(reason="a few hundred values"):
                for b in range(DB):
                    sp.dma_start(raw[:, b:b + 1], t["page_table"][b, :].rearrange("(g o) -> g o", o=1).unsqueeze(1).broadcast_to([16, 8, 1])).then_inc(s["pt"], 16)
                    sp.dma_start(wiT[:, b:b + 1], t["wi"][b * DS:(b + 1) * DS, :].rearrange("q (h o) -> h q o", o=1)).then_inc(s["wi"], 16)
            sp.dma_start(msel.rearrange("p a b -> p (a b)"), t["k_msel"]).then_inc(s["ms"], 16)
            sp.wait_ge(s["sqc"], 2)
            sp.dma_start(qiS[HD:P, :, :], qiS[0:HD, :, :]).then_inc(s["qd"], 16)

            def load(j):
                sp.dma_start(wp[j % 2], w_v[:, :, chunks[j][0]:chunks[j][0] + 512]).then_inc(s_pw[j % 2], 16)

            load(0)
            load(1)
            sp.wait_ge(s["qd"], 16)
            for n, g in enumerate(groups):
                if n - 1 == last.get(g[0] - 1) and g[0] + 1 < len(chunks):
                    sp.wait_ge(s["pmm"], n)
                    load(g[0] + 1)
                sp.wait_ge(s["pev"], n + 1)
                sp.dma_start(g[5], stage[n % 4][0:g[1], 0:g[2]]).then_inc(s_st[n % 4], 16)
            for b in range(4):
                sp.wait_ge(s_st[b], 16 * ((len(groups) + 3 - b) // 4))

        @block.gpsimd
        def _(po):
            po.wait_ge(s["idx"], 1)
            rows = t["cache_kidx"].rearrange("o n (a b) d -> (o n a) (b d)", b=8)
            for m in range(2 * DB):
                half, b = divmod(m, DB)
                if m >= NKI:
                    po.wait_ge(s["kit"], m - NKI + 1)
                po.indirect_dma_start(KI[m % NKI].rearrange("p a d -> p (a d)"), None, rows,
                                      bass.IndirectOffsetOnAxis(ap=idh[:, half, b:b + 1], axis=0)).then_inc(s_ki[m % NKI], 16)

        @block.tensor
        def _(pe):
            def prompt(i):
                for g in range(2):
                    if i >= 1:
                        pe.wait_ge(s["ev"], 2 * (i - 1) + g + 1)
                    for h in range(4):
                        hh = 4 * g + h
                        ins = pe.transpose(ps[0:HD, 4 + g, h * P:(h + 1) * P], z[:, i, QIC + hh * HD:QIC + (hh + 1) * HD], k.ident)
                    ins.then_inc(s["tr"], 1)
                N = P * (i + 1)
                for h in range(IH):
                    n = IH * i + h
                    if h % 4 == 0:
                        pe.wait_ge(s["ev"], 2 * i + h // 4 + 1)
                    if n >= 2:
                        pe.wait_ge(s["rl"], n - 1)
                    b = 2 * (n % 2)
                    for c in range(0, N, 512):
                        w = min(512, N - c)
                        ins = pe.matmul(ps[:, b + c // 512, 0:w], qiT[:, h, :], kiT[:, c:c + w], start=True, stop=True)
                    ins.then_inc(s["mm"], 1)

            def fold(m, par):
                pe.wait_ge(s["srl"], 2 * m + par + 1)
                pe.matmul(ps[0:NS, 6 + par, :], wsel[:, m % DB, :], rls[(2 * m + par) % 4], start=(m % DB == 0), stop=(m % DB == DB - 1)).then_inc(s["fold"], 1)

            def sample(half):
                tiles = (FIRST, SECOND)[half]
                pe.wait_ge(s["ev"], 2 * tiles)
                pe.wait_ge(s["rl"], IH * tiles)
                for n in range(DB * half, DB * half + DB):
                    b = n % DB
                    pe.wait_ge(s_ki[n % NKI], 16 * (n // NKI + 1))
                    if n >= 2:
                        pe.wait_ge(s["kic"], n - 1)
                    for jj in range(4):
                        ins = pe.transpose(ps[:, n % 2, jj * P:(jj + 1) * P], KI[n % NKI][:, 2 * jj:2 * jj + 2, :].rearrange("p a d -> p (a d)"), k.ident)
                    ins.then_inc(s["kit"], 1)
                    pe.wait_ge(s["kic"], n + 1)
                    for par in range(2):
                        if n >= 2:
                            pe.wait_ge(s["srl"], 2 * (n - 2) + par + 1)
                        rs = slice(par * HD, (par + 1) * HD)
                        pe.matmul(ps[0:NS, 2 + 2 * (n % 2) + par, :], qiS[rs, b, :], kis[n % 2][rs, :], start=True, stop=True).then_inc(s["smm"], 1)
                    if half == 1 and b == 1:
                        pe.wait_ge(s["done"], 2)
                    if b >= 1:
                        fold(n - 1, 0)
                        fold(n - 1, 1)
                fold(DB * half + DB - 1, 0)
                fold(DB * half + DB - 1, 1)
                pe.wait_ge(s["srl"], 2 * DB * (half + 1))

            for g in range(2):
                for h in range(4):
                    hh = 4 * g + h
                    ins = pe.transpose(ps[0:HD, 6 + g, h * NS:(h + 1) * NS],
                                       z[0:NS, NT - 1, QIC + hh * HD:QIC + (hh + 1) * HD], k.ident[0:NS, 0:NS])
                ins.then_inc(s["sq"], 1)
            for i in range(FIRST):
                prompt(i)
            pe.wait_ge(s["qd"], 16)
            pe.wait_ge(s["wsel"], 1)
            sample(0)
            for i in range(FIRST, SECOND):
                prompt(i)
            sample(1)
            pe.transpose(ps[0:HD, 0, 0:NS], z[0:NS, NT - 1, KIC:KIC + HD], k.ident[0:NS, 0:NS]).then_inc(s["new"], 1)
            pe.wait_ge(s["nrl"], 1)
            for b in range(DB):
                ins = pe.matmul(ps[0:NS, 2, b * DS:(b + 1) * DS], qiS[0:HD, b, :], kin[:, b * DS:(b + 1) * DS], start=True, stop=True)
            ins.then_inc(s["new"], 1)
            pe.wait_ge(s["nrl"], 2)
            for b in range(DB):
                ins = pe.matmul(ps[0:NS, 4, 0:DS], wsel[:, b, :], rls[0][:, b * DS:(b + 1) * DS], start=(b == 0), stop=(b == DB - 1))
            ins.then_inc(s["nfold"], 1)
            for n, (j, m, cols, lhs, rhs, dst) in enumerate(groups):
                if n == LATE:
                    pe.wait_ge(s["done"], 5)
                    pe.wait_ge(s["pev"], n)
                    for i in range(SECOND, NT - 1):
                        prompt(i)
                    pe.wait_ge(s["rl"], nmm)
                if n == 0:
                    pe.wait_ge(s["done"], 4)
                if n == 0 or groups[n - 1][0] != j:
                    pe.wait_ge(s_pw[j % 2], 16 * (j // 2 + 1))
                if n >= 4:
                    pe.wait_ge(s["pev"], n - 3)
                for a in range(KD):
                    ins = pe.matmul(ps[0:m, PB[n % 4], 0:cols], lhs(a), rhs(a), start=(a == 0), stop=(a == KD - 1))
                ins.then_inc(s["pmm"], 1)

        @block.scalar
        def _(act):
            def prompt(i):
                if i >= 1:
                    act.wait_ge(s["mm"], IH * i)
                for g in range(2):
                    act.wait_ge(s["tr"], 2 * i + g + 1)
                    act.activation(qiT[:, 4 * g:4 * g + 4, :].rearrange("p a b -> p (a b)"), ps[0:HD, 4 + g, :], ACT.Copy).then_inc(s["ev"], 1)
                N = P * (i + 1)
                for h in range(IH):
                    n = IH * i + h
                    act.wait_ge(s["mm"], n + 1)
                    if n >= 2:
                        act.wait_ge(s["acc"], n - 1)
                    b = 2 * (n % 2)
                    act.activation(rl[n % 2][:, 0:N], ps[:, b:b + 2, :].rearrange("p a b -> p (a b)")[:, 0:N], ACT.Relu).then_inc(s["rl"], 1)

            def sample(half):
                for n in range(DB * half, DB * half + DB):
                    act.wait_ge(s["kit"], n + 1)
                    if n >= 2:
                        act.wait_ge(s["smm"], 2 * (n - 1))
                    act.activation(kis[n % 2], ps[:, n % 2, :], ACT.Copy).then_inc(s["kic"], 1)
                    for par in range(2):
                        act.wait_ge(s["smm"], 2 * n + par + 1)
                        if n >= 2:
                            act.wait_ge(s["fold"], 2 * (n - 2) + par + 1)
                        act.activation(rls[(2 * n + par) % 4], ps[0:NS, 2 + 2 * (n % 2) + par, :], ACT.Relu).then_inc(s["srl"], 1)

            for g in range(2):
                act.wait_ge(s["sq"], g + 1)
                dst = qiS[0:HD, :, 4 * g * DS:4 * (g + 1) * DS].rearrange("p s (h q) -> p h s q", q=DS)
                for h in range(4):
                    ins = act.activation(dst[:, h, :, :], ps[0:HD, 6 + g, h * NS:(h + 1) * NS].rearrange("p (s q) -> p s q", q=DS), ACT.Copy)
                ins.then_inc(s["sqc"], 1)
            for i in range(FIRST):
                prompt(i)
            sample(0)
            for i in range(FIRST, SECOND):
                prompt(i)
            sample(1)
            act.wait_ge(s["new"], 1)
            act.activation(kin, ps[0:HD, 0, 0:NS], ACT.Copy).then_inc(s["nrl"], 1)
            act.wait_ge(s["new"], 2)
            act.wait_ge(s["fold"], 4 * DB)
            act.activation(rls[0][:, 0:NS], ps[0:NS, 2, 0:NS], ACT.Relu).then_inc(s["nrl"], 1)
            for n, (j, m, cols, lhs, rhs, dst) in enumerate(groups):
                if n == LATE:
                    for i in range(SECOND, NT - 1):
                        prompt(i)
                act.wait_ge(s["pmm"], n + 1)
                if n >= 4:
                    act.wait_ge(s_st[n % 4], 16 * (n // 4))
                act.activation(stage[n % 4][0:m, 0:cols], ps[0:m, PB[n % 4], 0:cols], ACT.Copy).then_inc(s["pev"], 1)

        @block.vector
        def _(ve):
            ch = Chain(ve, s["ch"])
            ve.memset(one, 1.0).then_inc(s["on"], 1)
            ve.wait_ge(s["pt"], 16 * DB)
            gather_index(ve, ch, k, raw, idx)
            for half in range(2):
                ch.step(ve.tensor_scalar(idh[:, half, :], idx, 2.0, float(half), ALU.mult, ALU.add))
            ve.sem_inc(s["idx"], 1)
            ve.wait_ge(s["wi"], 16 * DB)
            ve.wait_ge(s["ms"], 16)
            ve.tensor_tensor(wsel, msel, wiT.unsqueeze(2).broadcast_to([NS, DB, NS]), ALU.mult).then_inc(s["wsel"], 1)
            ve.wait_ge(s["on"], 1)

            def weigh(i):
                N = P * (i + 1)
                acc = ar.view(ACC_AT[i], N)
                for h in range(IH):
                    n = IH * i + h
                    w = z[:, i, WIC + h:WIC + h + 1]
                    ve.wait_ge(s["rl"], n + 1)
                    if h == 0:
                        ve.tensor_scalar(acc, rl[n % 2][:, 0:N], w, None, ALU.mult).then_inc(s["acc"], 1)
                    else:
                        ve.wait_ge(s["acc"], n)
                        ve.scalar_tensor_tensor(acc, rl[n % 2][:, 0:N], w, acc, ALU.mult, ALU.add).then_inc(s["acc"], 1)
                ve.wait_ge(s["acc"], IH * (i + 1))
                dg = acc[:, i * P:(i + 1) * P]
                ve.tensor_tensor(dg, dg, k.cb, ALU.add).then_inc(s["diag"], 1)
                ve.wait_ge(s["diag"], i + 1)
                if N <= TOPK:
                    ve.tensor_scalar(acc, acc, 0.5 * NEG, OFF, ALU.is_lt, ALU.mult)

            grid = accs[:, 0:PAST].rearrange("q (p j) -> q j p", j=16)

            def past(half):
                for par in range(2):
                    ve.wait_ge(s["fold"], 2 * DB * (half + 1) - 1 + par)
                    ve.tensor_copy(grid[:, 8 * half + par:8 * half + 8:2, :], ps[0:NS, 6 + par, :].rearrange("q (j p) -> q j p", p=P)).then_inc(s["done"], 1)

            taken = 0

            def select(*accs_):
                nonlocal taken
                m = len(accs_)
                with ve.Fori(0, TOPK // 8) as j:
                    base = taken + 2 * m * j
                    for u, acc in enumerate(accs_):
                        ve.max(top[u][0:acc.shape[0], :], acc).then_inc(s["top"], 1)
                    for u, acc in enumerate(accs_):
                        ve.wait_ge(s["top"], base + u + 1)
                        ve.tensor_copy(spare[u], one)
                        ve.match_replace(acc, top[u][0:acc.shape[0], :], acc, TAKEN).then_inc(s["top"], 1)
                    ve.wait_ge(s["top"], base + 2 * m)
                taken += 2 * m * (TOPK // 8)
                for acc in accs_:
                    ve.tensor_scalar(acc, acc, TAKEN, OFF, ALU.not_equal, ALU.mult)

            def tile(i):
                return ar.view(ACC_AT[i], P * (i + 1))

            for i in range(FIRST):
                weigh(i)
            select(tile(2), tile(3))
            past(0)
            for i in range(FIRST, SECOND):
                weigh(i)
            select(tile(4), tile(5))
            past(1)
            ve.wait_ge(s["nfold"], 1)
            ve.tensor_tensor(accs[:, PAST:PAST + DS], ps[0:NS, 4, 0:DS], k.small[0:NS, 0:DS], ALU.add).then_inc(s["done"], 1)
            for i in range(SECOND, NT - 1):
                weigh(i)
            ve.wait_ge(s["done"], 5)
            select(tile(6), tile(7))
            select(accs)


def prompt_attention(k):
    nc, t, ar, ps = k.nc, k.t, k.ar, k.ps
    z = ar.view(O_Z, NT, NA)
    kT, A = ar.view(O_KT, HKV, SEQ, p=HD), ar.view(O_A, NT, 512)
    o = O_F
    qT = [ar.view(o + b * H * P, H, P, p=HD) for b in range(2)]; o += 2 * H * P
    L = [ar.view(o + b * SEQ, SEQ) for b in range(2)]; o += 2 * SEQ
    E = [ar.view(o + b * SEQ, SEQ) for b in range(2)]; o += 2 * SEQ
    PT = [ar.view(o + b * 512, 4, P) for b in range(4)]; o += 2048
    nmx, den, rden = (ar.view(o + 64 * j, H * (NT - 1)) for j in range(3)); o += 192
    assert o <= k.end
    names = "ks kc tr ev mm l mx e pt ptc pv rd o".split()
    s = {n: k.sem("at_" + n) for n in names}
    chunks = [(i, h, c) for i in range(NT - 1) for h in range(H) for c in range(0, i + 1, 4)]
    first = {}
    for m, (i, h, c) in enumerate(chunks):
        first.setdefault((i, h), m)

    with nc.Block() as block:
        @block.tensor
        def _(pe):
            def queries(i):
                if i >= 2:
                    pe.wait_ge(s["o"], i - 1)
                for g in range(2):
                    if g == 1:
                        pe.wait_ge(s["ev"], 2 * i + 1)
                    for h in range(4):
                        hh = 4 * g + h
                        ins = pe.transpose(ps[0:HD, 6 + i % 2, h * P:(h + 1) * P], z[:, i, QC + hh * HD:QC + (hh + 1) * HD], k.ident)
                    ins.then_inc(s["tr"], 1)

            def logits(i, h):
                n = H * i + h
                if h % 4 == 0:
                    pe.wait_ge(s["ev"], 2 * i + h // 4 + 1)
                if n >= 2:
                    pe.wait_ge(s["l"], n - 1)
                b, N = 2 * (n % 2), P * (i + 1)
                for c in range(0, N, 512):
                    w = min(512, N - c)
                    ins = pe.matmul(ps[:, b + c // 512, 0:w], qT[i % 2][:, h, :], kT[:, h // 2, c:c + w], start=True, stop=True)
                ins.then_inc(s["mm"], 1)

            def weigh(i, h):
                n = H * i + h
                m = first[i, h]
                pe.wait_ge(s["e"], n + 1)
                for c in range(0, i + 1, 4):
                    if m >= 2:
                        pe.wait_ge(s["ptc"], m - 1)
                    for u in range(min(4, i + 1 - c)):
                        ins = pe.transpose(ps[:, 4 + m % 2, u * P:(u + 1) * P], E[n % 2][:, (c + u) * P:(c + u + 1) * P], k.ident)
                    ins.then_inc(s["pt"], 1)
                    m += 1
                m = first[i, h]
                if h == 0:
                    pe.wait_ge(s["ev"], 2 * i + 2)
                for c in range(0, i + 1, 4):
                    pe.wait_ge(s["ptc"], m + 1)
                    for u in range(min(4, i + 1 - c)):
                        ins = pe.matmul(ps[:, 6 + i % 2, h * HD:(h + 1) * HD], PT[m % 4][:, u, :], z[:, c + u, VC + (h // 2) * HD:VC + (h // 2 + 1) * HD],
                                        start=(c + u == 0), stop=(c + u == i))
                    m += 1
                ins.then_inc(s["pv"], 1)

            for i in range(NT - 1):
                if i >= 4:
                    pe.wait_ge(s["kc"], i - 3)
                for h in range(HKV):
                    ins = pe.transpose(ps[0:HD, i % 4, h * P:(h + 1) * P], z[:, i, KC + h * HD:KC + (h + 1) * HD], k.ident)
                ins.then_inc(s["ks"], 1)
            queries(0)
            pe.wait_ge(s["kc"], NT - 1)
            for n in range(H * (NT - 1) + 1):
                i, h = divmod(n, H)
                if n < H * (NT - 1):
                    logits(i, h)
                    if h == 4 and i + 1 < NT - 1:
                        queries(i + 1)
                if n >= 1:
                    weigh(*divmod(n - 1, H))

        @block.vector
        def _(ve):
            def mask(i, h):
                n, N = H * i + h, P * (i + 1)
                b = 2 * (n % 2)
                ve.wait_ge(s["mm"], n + 1)
                if n >= 2:
                    ve.wait_ge(s["e"], n - 1)
                ve.scalar_tensor_tensor(L[n % 2][:, 0:N], ps[:, b:b + 2, :].rearrange("p a b -> p (a b)")[:, 0:N], float(HD) ** -0.5,
                                        ar.view(ACC_AT[i], N), ALU.mult, ALU.add).then_inc(s["l"], 1)
                ve.wait_ge(s["l"], n + 1)
                ve.tensor_reduce(nmx[:, n:n + 1], L[n % 2][:, 0:N], AX.X, ALU.max, negate=True).then_inc(s["mx"], 1)

            def out(i):
                n = slice(H * i, H * i + H)
                ve.wait_ge(s["e"], n.stop)
                ve.reciprocal(rden[:, n], den[:, n]).then_inc(s["rd"], 1)
                ve.wait_ge(s["rd"], i + 1)
                ve.wait_ge(s["pv"], n.stop)
                ve.tensor_tensor(A[:, i, :].rearrange("p (h d) -> p h d", d=HD), ps[:, 6 + i % 2, :].rearrange("p (h d) -> p h d", d=HD),
                                 rden[:, n].unsqueeze(2).broadcast_to([P, H, HD]), ALU.mult).then_inc(s["o"], 1)

            for i in range(NT - 1):
                ve.wait_ge(s["ks"], i + 1)
                ve.tensor_copy(kT[:, :, i * P:(i + 1) * P], ps[0:HD, i % 4, :].rearrange("p (h n) -> p h n", n=P)).then_inc(s["kc"], 1)
            for n in range(H * (NT - 1) + 2):
                if n < H * (NT - 1):
                    mask(*divmod(n, H))
                if n >= H and n % H == 1:
                    out(n // H - 1)

        @block.scalar
        def _(act):
            def queries(i):
                for g in range(2):
                    if i >= 2 and g == 0:
                        act.wait_ge(s["mm"], H * (i - 1))
                    act.wait_ge(s["tr"], 2 * i + g + 1)
                    act.activation(qT[i % 2][:, 4 * g:4 * g + 4, :].rearrange("p a b -> p (a b)"), ps[0:HD, 6 + i % 2, :], ACT.Copy).then_inc(s["ev"], 1)

            queries(0)
            for n in range(H * (NT - 1) + 1):
                i, h = divmod(n, H)
                if n < H * (NT - 1):
                    N = P * (i + 1)
                    if h == 4 and i + 1 < NT - 1:
                        queries(i + 1)
                    act.wait_ge(s["mx"], n + 1)
                    if n >= 2:
                        act.wait_ge(s["pt"], first.get(divmod(n - 1, H), len(chunks)))
                    act.activation(E[n % 2][:, 0:N], L[n % 2][:, 0:N], ACT.Exp, bias=nmx[:, n:n + 1], accum_out=den[:, n:n + 1]).then_inc(s["e"], 1)
                if n >= 1:
                    i, h = divmod(n - 1, H)
                    m = first[i, h]
                    for c in range(0, i + 1, 4):
                        act.wait_ge(s["pt"], m + 1)
                        if m >= 4:
                            ii, hh, _ = chunks[m - 4]
                            act.wait_ge(s["pv"], H * ii + hh + 1)
                        w = P * min(4, i + 1 - c)
                        act.activation(PT[m % 4].rearrange("p a b -> p (a b)")[:, 0:w], ps[:, 4 + m % 2, 0:w], ACT.Copy).then_inc(s["ptc"], 1)
                        m += 1


def sample_attention(k):
    nc, t, ar, ps = k.nc, k.t, k.ar, k.ps
    z, A = ar.view(O_Z, NT, NA), ar.view(O_A, NT, 512)
    mb = ar.view(O_ACCS, PAST + DS, p=NS)
    NL = PAST + NS
    Kc = [ar.view(a, 16, HKV * HD) for a in (O_KT, O_F)]
    Vc = [ar.view(a, 16, HKV * HD) for a in (O_ACC, O_F + 4096)]
    o = O_F + 8192
    L = [ar.view(o + b * NL, NL) for b in range(2)]; o += 2 * NL
    QB = ar.view(o, DB, 2, NS); o += 2 * DB * NS
    mbn = ar.view(o, DB, DS, p=NS); o += NS
    kTn = ar.view(o, 2, NS); o += 2 * NS
    idx = ar.view(k.o_idx, DB, dt=I32)
    nmx, den, rden = (ar.view(o + 4 * j, 4) for j in range(3)); o += 12
    kT = [ar.view(o + b * 1024, 2, 512) for b in range(2)]; o += 2048
    PT = [ar.view(o + b * 512, 512) for b in range(2)]; o += 1024
    qr = ar.view(o - 512, 2, 2, P, p=NS)
    rsel = ar.view(o, DB, NS, p=NS); o += DB * NS
    ob = ar.view(o, 256); o += 256
    assert o <= k.end, (o, k.end)
    names = "qr kc0 kc1 vc0 vc1 rs ch qt qc kn knc zero mbn kt ktc mm lc mx e ptt ptc pv rd ob out0 in".split()
    s = {n: k.sem("sa_" + n) for n in names}
    NCK = 5

    with nc.Block() as block:
        @block.sync
        def _(sp):
            sp.dma_start(rsel.rearrange("p a b -> p (a b)"), t["k_rsel"]).then_inc(s["rs"], 16)
            for pr in range(DB // 2):
                sp.wait_ge(s["ob"], pr + 1)
                for j in range(2):
                    for g in range(HKV):
                        dst = t["att"][(2 * pr + j) * DS:(2 * pr + j + 1) * DS, g * 2 * HD:(g + 1) * 2 * HD].rearrange("q (g d) -> g q d", d=HD)
                        sp.dma_start(dst, ob[j * HD + 16 * g:j * HD + 16 * g + 16, g * HD:(g + 1) * HD]).then_inc(s["out0"], 16)
            sp.wait_ge(s["out0"], 16 * DB * HKV)
            sp.dma_start(A[0:NS, NT - 1, :], t["att"]).then_inc(s["in"], 16)
            sp.wait_ge(s["in"], 16)

        @block.gpsimd
        def _(po):
            rk = t["cache_k"].rearrange("o n (a b) h d -> (o n a) (b h d)", b=16)
            rv = t["cache_v"].rearrange("o n (a b) h d -> (o n a) (b h d)", b=16)
            for b in range(DB):
                if b >= 2:
                    po.wait_ge(s["kt"], 4 * (b - 1))
                po.indirect_dma_start(Kc[b % 2].rearrange("p a d -> p (a d)"), None, rk,
                                      bass.IndirectOffsetOnAxis(ap=idx[:, b:b + 1], axis=0)).then_inc(s[f"kc{b % 2}"], 16)
                if b >= 2:
                    po.wait_ge(s["pv"], b - 1)
                po.indirect_dma_start(Vc[b % 2].rearrange("p a d -> p (a d)"), None, rv,
                                      bass.IndirectOffsetOnAxis(ap=idx[:, b:b + 1], axis=0)).then_inc(s[f"vc{b % 2}"], 16)

        @block.tensor
        def _(pe):
            pe.wait_ge(s["qr"], 2)
            for pp in range(2):
                for g in range(2):
                    ins = pe.transpose(ps[:, 6, (2 * pp + g) * NS:(2 * pp + g + 1) * NS], qr[:, pp, g, :], k.ident[0:NS, 0:NS])
            ins.then_inc(s["qt"], 1)
            for pp in range(2):
                ins = pe.transpose(ps[:, 7, pp * NS:(pp + 1) * NS], z[0:NS, NT - 1, KC + pp * P:KC + (pp + 1) * P], k.ident[0:NS, 0:NS])
            ins.then_inc(s["kn"], 1)
            pe.wait_ge(s["qc"], 8)
            pe.wait_ge(s["knc"], 1)
            pe.wait_ge(s["mbn"], 1)
            pe.wait_ge(s["rs"], 16)
            grid = mb[:, 0:PAST].rearrange("q (p j) -> q j p", j=16)

            def keys(b, c):
                m = 4 * b + c
                if c == 0:
                    pe.wait_ge(s[f"kc{b % 2}"], 16 * (b // 2 + 1))
                if m >= 2:
                    pe.wait_ge(s["ktc"], m - 1)
                for pp in range(2):
                    for u in range(4):
                        ins = pe.transpose(ps[:, 2 * (m % 2) + pp, u * P:(u + 1) * P], Kc[b % 2][:, 4 * c + u, pp * P:(pp + 1) * P], k.ident)
                ins.then_inc(s["kt"], 1)

            def logits(b, c):
                m = NCK * b + c
                if m >= 2:
                    pe.wait_ge(s["lc"], m - 1)
                rs = slice(HD * (b % 2), HD * (b % 2) + HD)
                if c < 4:
                    pe.wait_ge(s["ktc"], 4 * b + c + 1)
                    out = ps[rs, 4 + m % 2, :]
                    for pp in range(2):
                        pe.matmul(out, QB[:, b, pp, :], kT[(4 * b + c) % 2][:, pp, :], start=(pp == 0), stop=False)
                    ins = pe.matmul(out, rsel[:, b, :], grid[:, 4 * c:4 * c + 4, :], start=False, stop=True)
                else:
                    out = ps[rs, 4 + m % 2, 0:NS]
                    for pp in range(2):
                        pe.matmul(out, QB[:, b, pp, :], kTn[:, pp, :], start=(pp == 0), stop=False)
                    ins = pe.matmul(out, rsel[:, b, :], mbn.rearrange("q a b -> q (a b)"), start=False, stop=True)
                ins.then_inc(s["mm"], 1)

            def weigh(pr):
                pe.wait_ge(s["e"], pr + 1)
                if pr >= 1:
                    pe.wait_ge(s["ob"], pr)
                for c in range(NCK + 1):
                    if c < NCK:
                        m = NCK * pr + c
                        if m >= 1:
                            pe.wait_ge(s["ptc"], m)
                        for u in range(4 if c < 4 else 1):
                            w = P if c < 4 else NS
                            at = c * 512 + u * P
                            ins = pe.transpose(ps[0:w, 6, u * P:(u + 1) * P], L[pr % 2][:, at:at + w], k.ident)
                        ins.then_inc(s["ptt"], 1)
                        pe.wait_ge(s["ptc"], m + 1)
                        for j in range(2):
                            b = 2 * pr + j
                            if c == 0:
                                pe.wait_ge(s[f"vc{j}"], 16 * (pr + 1))
                            rs = slice(HD * j, HD * j + HD)
                            for u in range(4 if c < 4 else 1):
                                if c < 4:
                                    ins = pe.matmul(ps[rs, 7, 0:256], PT[m % 2][:, u * P + j * HD:u * P + (j + 1) * HD], Vc[j][:, 4 * c + u, :],
                                                    start=(c == 0 and u == 0), stop=False)
                                else:
                                    ins = pe.matmul(ps[rs, 7, 0:256], PT[m % 2][0:NS, j * HD:(j + 1) * HD], z[0:NS, NT - 1, VC:VC + 256],
                                                    start=False, stop=True)
                                    ins.then_inc(s["pv"], 1)

            for b in range(DB):
                keys(b, 0)
                for c in range(NCK):
                    if c + 1 < 4:
                        keys(b, c + 1)
                    logits(b, c)
                if b % 2 == 1:
                    weigh(b // 2)

        @block.vector
        def _(ve):
            ch = Chain(ve, s["ch"])
            for pp in range(2):
                ve.tensor_copy(qr[:, pp, :, :].rearrange("p g (c d) -> p g c d", d=HD), z[0:NS, NT - 1, QC + 4 * pp * HD:QC + (4 * pp + 4) * HD]
                               .rearrange("p (c g d) -> p g c d", g=2, d=HD)).then_inc(s["qr"], 1)
            ve.memset(QB, 0.0).then_inc(s["zero"], 1)
            ch.step(ve.tensor_scalar(mbn, k.small[0:NS, 10:18].unsqueeze(2).broadcast_to([NS, DB, DS]), -OFF, OFF, ALU.mult, ALU.add))
            ve.tensor_tensor(mbn, mbn, mb[:, PAST:PAST + DS].unsqueeze(1).broadcast_to([NS, DB, DS]), ALU.add).then_inc(s["mbn"], 1)
            ve.wait_ge(s["kn"], 1)
            ve.tensor_copy(kTn.rearrange("p a b -> p (a b)"), ps[:, 7, 0:2 * NS]).then_inc(s["knc"], 1)
            ve.wait_ge(s["zero"], 1)
            ve.wait_ge(s["qt"], 1)
            for pp in range(2):
                for g in range(2):
                    for par in range(2):
                        rs = slice(par * HD, (par + 1) * HD)
                        row = ((2 * pp + par) * 2 + g) * DS
                        ve.tensor_scalar(QB[rs, :, pp, row:row + DS], ps[rs, 6, (2 * pp + g) * NS:(2 * pp + g + 1) * NS].rearrange("p (s q) -> p s q", q=DS),
                                         float(HD) ** -0.5, None, ALU.mult).then_inc(s["qc"], 1)

            def copy_keys(m):
                ve.wait_ge(s["kt"], m + 1)
                if m >= 2:
                    b, c = divmod(m - 2, 4)
                    ve.wait_ge(s["mm"], NCK * b + c + 1)
                ve.tensor_copy(kT[m % 2].rearrange("p a b -> p (a b)"), ps[:, 2 * (m % 2):2 * (m % 2) + 2, :].rearrange("p a b -> p (a b)")).then_inc(s["ktc"], 1)

            for pr in range(DB // 2):
                for m in range(8 * pr, 8 * pr + 8):
                    copy_keys(m)
                ve.wait_ge(s["lc"], 2 * NCK * (pr + 1))
                ve.tensor_reduce(nmx[:, pr:pr + 1], L[pr % 2], AX.X, ALU.max, negate=True).then_inc(s["mx"], 1)
                ve.wait_ge(s["e"], pr + 1)
                ve.reciprocal(rden[:, pr:pr + 1], den[:, pr:pr + 1]).then_inc(s["rd"], 1)
                ve.wait_ge(s["rd"], pr + 1)
                ve.wait_ge(s["pv"], 2 * pr + 2)
                if pr >= 1:
                    ve.wait_ge(s["out0"], 16 * 8 * pr)
                ve.tensor_scalar(ob, ps[:, 7, 0:256], rden[:, pr:pr + 1], None, ALU.mult).then_inc(s["ob"], 1)

        @block.scalar
        def _(act):
            for pr in range(DB // 2):
                for m in range(2 * NCK * pr, 2 * NCK * (pr + 1)):
                    b, c = divmod(m, NCK)
                    rs = slice(HD * (b % 2), HD * (b % 2) + HD)
                    w = 512 if c < 4 else NS
                    act.wait_ge(s["mm"], m + 1)
                    if pr >= 2 and m == 2 * NCK * pr:
                        act.wait_ge(s["ptt"], NCK * (pr - 1))
                    act.activation(L[pr % 2][rs, c * 512:c * 512 + w], ps[rs, 4 + m % 2, 0:w], ACT.Copy).then_inc(s["lc"], 1)
                act.wait_ge(s["mx"], pr + 1)
                act.wait_ge(s["lc"], 2 * NCK * (pr + 1))
                act.activation(L[pr % 2], L[pr % 2], ACT.Exp, bias=nmx[:, pr:pr + 1], accum_out=den[:, pr:pr + 1]).then_inc(s["e"], 1)
                for c in range(NCK):
                    m = NCK * pr + c
                    act.wait_ge(s["ptt"], m + 1)
                    w, n = (P, 512) if c < 4 else (NS, P)
                    act.activation(PT[m % 2][0:w, 0:n], ps[0:w, 6, 0:n], ACT.Copy).then_inc(s["ptc"], 1)


NR = 4 + NE
O_RT = 46000
R_W1, R_W2, R_D1, R_D2, R_BE, R_TOK, R_CH, R_BUF, R_NU, R_LG = (O_RT + n for n in (0, 16, 32, 48, 64, 96, 128, 160, 192, 208))


def project_out(k):
    nc, t, ar, ps = k.nc, k.t, k.ar, k.ps
    A, R = ar.view(O_A, NT, 512), ar.view(O_R, NT, 512)
    o = O_R + NT * 512
    wo = ar.view(o, KD, D); o += KD * D
    gt, sc, sh = (ar.view(o + j * 2 * D, 2, D) for j in range(3)); o += 6 * D
    g2 = ar.view(o, D); o += D
    x = [ar.view(o + j * D, D) for j in range(2)]; o += 2 * D
    x1 = [ar.view(o + j * D, D) for j in range(2)]; o += 2 * D
    h2 = [ar.view(o + j * D, D) for j in range(2)]; o += 2 * D
    mT = [ar.view(o + j * D, KD, P) for j in range(2)]; o += 2 * D
    hT = [ar.view(o + j * D, KD, P) for j in range(2)]; o += 2 * D
    sq = ar.view(o, D); o += D
    ga = ar.view(o, 512); o += 512
    wr = ar.view(o, KD, NR); o += KD * NR
    cols = [ar.view(o + 16 * j, NT) for j in range(8)]; o += 128
    ssa, rsa, sda, tma, ss, rs, sd, tm = cols
    assert o <= O_RT, o
    lg = ar.view(R_LG, NT, NR)
    names = "w mod ga sqa msa sda an x0 x1 t1 m1 mm gx xo h t2 h2 rt ch ss ms sd so ho init".split()
    s = {n: k.sem("po_" + n) for n in names}
    s_x1o, s_h2o = [k.sem(f"po_x1o{b}") for b in range(2)], [k.sem(f"po_h2o{b}") for b in range(2)]
    parts = ((P, 0, NT - 1), (NS, NT - 1, NT))

    with nc.Block() as block:
        @block.sync
        def _(sp):
            sp.dma_start(ga, t["attn_out_g"].broadcast_to([P, 512])).then_inc(s["ga"], 16)
            sp.dma_start(wo, t["w_out"].rearrange("o (a p) n -> p (o a) n", p=P)).then_inc(s["w"], 16)
            load_scale_shift(sp, k, s["mod"], sc, sh, (g2, t["norm2_g"]), [(gt, 2), (sc, 4), (sh, 3)])
            sp.dma_start(wr[:, :, 0:4], t["w_group"].rearrange("o (a p) n -> p (o a) n", p=P)).then_inc(s["w"], 16)
            sp.dma_start(wr[:, :, 4:NR], t["w_expert_router"].rearrange("o (a p) n -> p (o a) n", p=P)).then_inc(s["w"], 16)
            for i in range(NT):
                if i >= 2:
                    sp.wait_ge(s["xo"], i - 1)
                sp.dma_start(x[i % 2][0:ROWS[i], :], x_rows(t, i)).then_inc(s[f"x{i % 2}"], 16)
            sp.wait_ge(s["w"], 48)

        @block.gpsimd
        def _(po):
            for i in range(NT):
                po.wait_ge(s["xo"], i + 1)
                po.dma_start(tile_rows(t["x1"], i), x1[i % 2][0:ROWS[i], :]).then_inc(s_x1o[i % 2], 16)
                po.wait_ge(s["h"], i + 1)
                po.dma_start(tile_rows(t["h2"], i), h2[i % 2][0:ROWS[i], :]).then_inc(s_h2o[i % 2], 16)
            for b in range(2):
                po.wait_ge(s_x1o[b], 16 * ((NT + 1 - b) // 2))
                po.wait_ge(s_h2o[b], 16 * ((NT + 1 - b) // 2))

        @block.scalar
        def _(act):
            for m, (n, a, b) in enumerate(parts):
                for i in range(a, b):
                    if i >= 1:
                        act.wait_ge(s["sqa"], i)
                    act.activation(sq[0:n, 0:512], A[0:n, i, :], ACT.Square, accum_out=ssa[0:n, i:i + 1]).then_inc(s["sqa"], 1)
            for m, (n, a, b) in enumerate(parts):
                act.wait_ge(s["msa"], m + 1)
                act.activation(sda[0:n, a:b], ssa[0:n, a:b], ACT.Sqrt).then_inc(s["sda"], 1)
            act.wait_ge(s["sqa"], NT)
            for i in range(NT + 1):
                if i < NT:
                    r = ROWS[i]
                    act.wait_ge(s["t1"], i + 1)
                    if i >= 2:
                        act.wait_ge(s["mm"], i - 1)
                    act.activation(mT[i % 2][:, :, 0:r], ps[:, 0:2, :].rearrange("p b (a n) -> p (b a) n", n=P)[:, :, 0:r], ACT.Copy).then_inc(s["m1"], 1)
                    act.wait_ge(s["xo"], i + 1)
                    if i >= 1:
                        act.wait_ge(s["ss"], i)
                    act.activation(sq[0:r, :], x1[i % 2][0:r, :], ACT.Square, accum_out=ss[0:r, i:i + 1]).then_inc(s["ss"], 1)
                    act.wait_ge(s["ms"], i + 1)
                    act.activation(sd[0:r, i:i + 1], ss[0:r, i:i + 1], ACT.Sqrt).then_inc(s["sd"], 1)
                if i >= 1:
                    j, r = i - 1, ROWS[i - 1]
                    act.wait_ge(s["t2"], j + 1)
                    if j >= 2:
                        act.wait_ge(s["rt"], j - 1)
                    act.activation(hT[j % 2][:, :, 0:r], ps[:, 4:6, :].rearrange("p b (a n) -> p (b a) n", n=P)[:, :, 0:r], ACT.Copy).then_inc(s["h2"], 1)

        @block.tensor
        def _(pe):
            pe.wait_ge(s["w"], 48)
            pe.wait_ge(s["an"], 4)
            for i in range(NT + 1):
                if i < NT:
                    r = ROWS[i]
                    if i >= 1:
                        pe.wait_ge(s["m1"], i)
                    for a in range(KD):
                        src = A if a < 4 else R
                        ins = pe.transpose(ps[:, a // 4, (a % 4) * P:(a % 4) * P + r], src[0:r, i, (a % 4) * P:(a % 4 + 1) * P], k.ident[0:r, 0:r])
                    ins.then_inc(s["t1"], 1)
                    pe.wait_ge(s["m1"], i + 1)
                    if i >= 1:
                        pe.wait_ge(s["gx"], i)
                    for c in range(2):
                        for a in range(KD):
                            ins = pe.matmul(ps[0:r, 2 + c, :], mT[i % 2][:, a, 0:r], wo[:, a, c * 512:(c + 1) * 512], start=(a == 0), stop=(a == KD - 1))
                    ins.then_inc(s["mm"], 1)
                if i >= 1:
                    j, r = i - 1, ROWS[i - 1]
                    pe.wait_ge(s["h"], j + 1)
                    if j >= 1:
                        pe.wait_ge(s["h2"], j)
                    for a in range(KD):
                        ins = pe.transpose(ps[:, 4 + a // 4, (a % 4) * P:(a % 4) * P + r], h2[j % 2][0:r, a * P:(a + 1) * P], k.ident[0:r, 0:r])
                    ins.then_inc(s["t2"], 1)
                    pe.wait_ge(s["h2"], j + 1)
                    for a in range(KD):
                        ins = pe.matmul(ps[0:r, 6, j * NR:(j + 1) * NR], hT[j % 2][:, a, 0:r], wr[:, a, :], start=(a == 0), stop=(a == KD - 1))
                    ins.then_inc(s["rt"], 1)

        @block.vector
        def _(ve):
            ch = Chain(ve, s["ch"])
            for m, (n, a, b) in enumerate(parts):
                ve.wait_ge(s["sqa"], b)
                ve.tensor_scalar(ssa[0:n, a:b], ssa[0:n, a:b], 1.0 / 512, EPS, ALU.mult, ALU.add).then_inc(s["msa"], 1)
                ve.wait_ge(s["msa"], m + 1)
            ve.wait_ge(s["ga"], 16)
            for m, (n, a, b) in enumerate(parts):
                rstd_steps(ch, ve, lambda: ve.wait_ge(s["sda"], m + 1), ssa[0:n, a:b], rsa[0:n, a:b], sda[0:n, a:b], tma[0:n, a:b])
                ve.tensor_tensor(A[0:n, a:b, :], A[0:n, a:b, :], rsa[0:n, a:b].unsqueeze(2).broadcast_to([n, b - a, 512]), ALU.mult).then_inc(s["an"], 1)
                ve.wait_ge(s["an"], 2 * m + 1)
                ve.tensor_tensor(A[0:n, a:b, :], A[0:n, a:b, :], ga[0:n, :].unsqueeze(1).broadcast_to([n, b - a, 512]), ALU.mult).then_inc(s["an"], 1)
            ve.wait_ge(s["mod"], 16 * 7)
            ch.step(ve.scalar_tensor_tensor(sc[:, 0, :], sc[:, 0, :], 1.0, g2, ALU.add, ALU.mult))
            ch.step(ve.scalar_tensor_tensor(sc[0:NS, 1, :], sc[0:NS, 1, :], 1.0, g2[0:NS, :], ALU.add, ALU.mult))
            for i in range(NT):
                r, m = ROWS[i], int(i == NT - 1)
                col = slice(i, i + 1)
                ve.wait_ge(s["mm"], i + 1)
                if i >= 2:
                    ve.wait_ge(s_x1o[i % 2], 16 * (i // 2))
                    ve.wait_ge(s["ss"], i - 1)
                ve.tensor_tensor(x1[i % 2][0:r, :], ps[0:r, 2:4, :].rearrange("p a b -> p (a b)"), gt[0:r, m, :], ALU.mult).then_inc(s["gx"], 1)
                ve.wait_ge(s["gx"], i + 1)
                ve.wait_ge(s[f"x{i % 2}"], 16 * (i // 2 + 1))
                ve.tensor_tensor(x1[i % 2][0:r, :], x1[i % 2][0:r, :], x[i % 2][0:r, :], ALU.add).then_inc(s["xo"], 1)
                ve.wait_ge(s["ss"], i + 1)
                ve.tensor_scalar(ss[0:r, col], ss[0:r, col], 1.0 / D, EPS, ALU.mult, ALU.add).then_inc(s["ms"], 1)
                ve.wait_ge(s["ms"], i + 1)
                rstd_steps(ch, ve, lambda: ve.wait_ge(s["sd"], i + 1), ss[0:r, col], rs[0:r, col], sd[0:r, col], tm[0:r, col])
                if i >= 2:
                    ve.wait_ge(s["t2"], i - 1)
                    ve.wait_ge(s_h2o[i % 2], 16 * (i // 2))
                ch.step(ve.scalar_tensor_tensor(h2[i % 2][0:r, :], x1[i % 2][0:r, :], rs[0:r, col], sc[0:r, m, :], ALU.mult, ALU.mult))
                ve.tensor_tensor(h2[i % 2][0:r, :], h2[i % 2][0:r, :], sh[0:r, m, :], ALU.add).then_inc(s["h"], 1)
            ch.step(ve.memset(lg, 0.0))
            ve.wait_ge(s["rt"], NT)
            ch.mark(ve.tensor_copy(lg[:, 0:NT - 1, :].rearrange("p a b -> p (a b)"), ps[:, 6, 0:(NT - 1) * NR]))
            ch.step(ve.tensor_copy(lg[0:NS, NT - 1, :], ps[0:NS, 6, (NT - 1) * NR:NT * NR]))


def route(k):
    nc, t, ar, ps = k.nc, k.t, k.ar, k.ps
    lg = ar.view(R_LG, NT, NR)
    W = [ar.view(R_W1, NT), ar.view(R_W2, NT)]
    Dst = [ar.view(R_D1, NT, dt=I32), ar.view(R_D2, NT, dt=I32)]
    be, tok = ar.view(R_BE, NB, p=1, dt=I32), ar.view(R_TOK, NB, dt=I32)
    o = 0
    def new(*d, **kw):
        nonlocal o
        v = ar.view(o, *d, **kw)
        o += (int(np.prod(d)) + 15) // 16 * 16
        return v
    bias, cst = new(NR), new(128)
    pref, thr, iota_b = cst[:, 0:4], cst[:, 16:16 + NT], cst[:, 32:32 + NB]
    gm, gs, gw, m1, m2, d21, den = (new(NT) for _ in range(7))
    ge, goh, eg, oh1, oh2, key = (new(NT, 4) for _ in range(6))
    tmp4 = new(NT, 4, 4)
    M1, M2 = new(NT, 4, 4), new(NT, 4, 4)
    M, Cs, rk, pr = new(NT, NE), new(NT + 1, NE), new(NT, NE), new(NT, NE)
    cnt, nb, ends, base, onesr = new(NE), new(NE), new(NE), new(NE), new(NE)
    cmpb, cmpe = new(NE, NT), new(NB, NE, p=1)
    bef, chf, flip, buff = (new(NB, p=1) for _ in range(4))
    chg, buf, used = ar.view(R_CH, NB, p=1, dt=I32), ar.view(R_BUF, NB, p=1, dt=I32), ar.view(R_NU, 1, p=1, dt=I32)
    df = [new(NT), new(NT)]
    ones = new(P)
    tid, zero = new(NT, dt=I32), new(NB, dt=I32)
    tidf = new(NT)
    names = "c ch a1 a2 m rk z scat tok tid dst".split()
    s = {n: k.sem("ro_" + n) for n in names}
    table = t["tok"].rearrange("(b p) o -> p (b o)", p=P)

    with nc.Block() as block:
        @block.sync
        def _(sp):
            sp.dma_start(cst, t["k_route"].broadcast_to([P, 128])).then_inc(s["c"], 16)
            sp.dma_start(bias[:, 0:4], t["b_group"].broadcast_to([P, 4])).then_inc(s["c"], 16)
            sp.dma_start(bias[:, 4:NR], t["b_expert_router"].broadcast_to([P, NE])).then_inc(s["c"], 16)
            sp.dma_start(tidf, t["k_tid"]).then_inc(s["c"], 16)
            sp.wait_ge(s["z"], 1)
            with nc.allow_non_contiguous_dma(reason="4096 values"):
                sp.dma_start(table, zero).then_inc(s["tok"], 16)
                sp.wait_ge(s["tok"], 16)
                sp.wait_ge(s["scat"], 16 * 2 * NT)
                sp.dma_start(tok, table).then_inc(s["tok"], 16)
            sp.wait_ge(s["tok"], 32)

        @block.gpsimd
        def _(po):
            po.wait_ge(s["dst"], 2)
            po.wait_ge(s["tid"], 1)
            po.wait_ge(s["tok"], 16)
            for i in range(NT):
                for j in range(2):
                    r = ROWS[i]
                    po.indirect_dma_start(t["tok"], bass.IndirectOffsetOnAxis(ap=Dst[j][0:r, i:i + 1], axis=0), tid[0:r, i:i + 1], None).then_inc(s["scat"], 16)
            po.wait_ge(s["scat"], 16 * 2 * NT)

        @block.scalar
        def _(act):
            act.wait_ge(s["a1"], 1)
            act.activation(ge, ge, ACT.Exp).then_inc(s["a2"], 1)
            act.wait_ge(s["a1"], 2)
            act.activation(d21, d21, ACT.Exp).then_inc(s["a2"], 1)

        @block.tensor
        def _(pe):
            pe.wait_ge(s["m"], 1)
            pe.matmul(ps[:, 0, 0:NT * NE], k.tri, M.rearrange("p a b -> p (a b)"), start=True, stop=False)
            pe.matmul(ps[:, 0, 0:NT * NE], ones, Cs[:, 0:NT, :].rearrange("p a b -> p (a b)"), start=False, stop=True)
            pe.matmul(ps[:, 1, 0:NE], ones, Cs[:, NT, :], start=True, stop=True).then_inc(s["rk"], 1)

        @block.vector
        def _(ve):
            ch = Chain(ve, s["ch"])
            tt, ts = ve.tensor_tensor, ve.tensor_scalar
            ve.memset(zero, 0).then_inc(s["z"], 1)
            ch.mark(ve.memset(ones, 1.0))
            ch.mark(ve.memset(onesr, 1.0))
            ch.mark(ve.memset(Cs, 0.0))
            ch.mark(ve.memset(chf, 1.0))
            ve.wait_ge(s["c"], 64)
            ve.tensor_copy(tid, tidf).then_inc(s["tid"], 1)
            ch.step(tt(lg, lg, bias.unsqueeze(1).broadcast_to([P, NT, NR]), ALU.add))

            def wide(v):
                return v.unsqueeze(2).broadcast_to([P, NT, 4])

            def first_max(x, mx, oh):
                ch.step(ve.tensor_reduce(mx, x, AX.X, ALU.max))
                ch.step(tt(key, x, wide(mx), ALU.is_equal))
                ch.step(tt(key, key, pref.unsqueeze(1).broadcast_to([P, NT, 4]), ALU.mult))
                ch.step(ve.tensor_reduce(gs, key, AX.X, ALU.max))
                ch.step(tt(oh, key, wide(gs), ALU.is_equal))

            gl = lg[:, :, 0:4]
            el = lg[:, :, 4:NR].rearrange("p a (g e) -> p a g e", e=4)
            first_max(gl, gm, goh)
            tt(ge, gl, wide(gm), ALU.subtract).then_inc(s["a1"], 1)
            ch.step(tt(tmp4, el, goh.unsqueeze(3).broadcast_to([P, NT, 4, 4]), ALU.mult))
            ch.step(ve.tensor_reduce(eg, tmp4.rearrange("p a g e -> p a e g"), AX.X, ALU.add))
            first_max(eg, m1, oh1)
            ch.step(ve.scalar_tensor_tensor(eg, oh1, OFF, eg, ALU.mult, ALU.add))
            first_max(eg, m2, oh2)
            tt(d21, m2, m1, ALU.subtract).then_inc(s["a1"], 1)
            for Mj, oh in ((M1, oh1), (M2, oh2)):
                ch.step(tt(Mj, goh.unsqueeze(3).broadcast_to([P, NT, 4, 4]), oh.unsqueeze(2).broadcast_to([P, NT, 4, 4]), ALU.mult))
                ch.step(ve.memset(Mj[NS:P, NT - 1, :, :], 0.0))
            f1, f2 = (x.rearrange("p a g e -> p a (g e)") for x in (M1, M2))
            ch.step(tt(M, f1, f2, ALU.add))
            for i in range(NT):
                ch.step(tt(Cs[:, i + 1, :], Cs[:, i, :], M[:, i, :], ALU.add))
            ve.sem_inc(s["m"], 1)
            ve.wait_ge(s["a2"], 2)
            ch.step(ve.tensor_reduce(gs, ge, AX.X, ALU.add))
            ch.step(ve.reciprocal(gw, gs))
            ch.step(ts(den, d21, 1.0, None, ALU.add))
            ch.step(ve.reciprocal(gs, den))
            ch.step(tt(W[0], gw, gs, ALU.mult))
            ch.step(tt(W[1], W[0], d21, ALU.mult))
            ve.wait_ge(s["rk"], 1)
            ch.mark(ve.tensor_copy(rk.rearrange("p a b -> p (a b)"), ps[:, 0, 0:NT * NE]))
            ch.step(ve.tensor_copy(cnt, ps[:, 1, 0:NE]))
            ch.step(tt(cmpb, cnt.unsqueeze(2).broadcast_to([P, NE, NT]), thr.unsqueeze(1).broadcast_to([P, NE, NT]), ALU.is_gt))
            ch.step(ve.tensor_reduce(nb, cmpb, AX.X, ALU.add))
            ch.step(ve.tensor_tensor_scan(ends, onesr, nb, 0.0, ALU.mult, ALU.add))
            ch.step(tt(base, ends, nb, ALU.subtract))
            ch.step(ts(base, base, float(P), None, ALU.mult))
            ch.step(tt(rk, rk, base.unsqueeze(1).broadcast_to([P, NT, NE]), ALU.add))
            for j, f in enumerate((f1, f2)):
                ch.step(tt(pr, rk, f, ALU.mult))
                ch.step(ve.tensor_reduce(df[j], pr, AX.X, ALU.add))
                ve.tensor_copy(Dst[j], df[j]).then_inc(s["dst"], 1)
            ch.step(tt(cmpe, iota_b[0:1, :].unsqueeze(2).broadcast_to([1, NB, NE]), ends[0:1, :].unsqueeze(1).broadcast_to([1, NB, NE]), ALU.is_ge))
            ch.step(ve.tensor_reduce(bef, cmpe, AX.X, ALU.add))
            ch.step(ts(bef, bef, float(NE - 1), None, ALU.min))
            ch.step(ve.tensor_copy(be, bef))
            ch.step(tt(chf[:, 1:NB], bef[:, 1:NB], bef[:, 0:NB - 1], ALU.not_equal))
            ch.step(ts(flip, chf, -2.0, 1.0, ALU.mult, ALU.add))
            ch.step(ve.tensor_tensor_scan(buff, flip, chf, 1.0, ALU.mult, ALU.add))
            ch.mark(ve.tensor_copy(chg, chf))
            ch.mark(ve.tensor_copy(buf, buff))
            ch.step(ve.tensor_copy(used, ends[0:1, NE - 1:NE]))


def experts(k):
    nc, t, ar, ps = k.nc, k.t, k.ar, k.ps
    be, tok = ar.view(R_BE, NB, p=1, dt=I32), ar.view(R_TOK, NB, dt=I32)
    chg, buf, used = ar.view(R_CH, NB, p=1, dt=I32), ar.view(R_BUF, NB, p=1, dt=I32), ar.view(R_NU, 1, p=1, dt=I32)
    SURE = A_TOT // P // 2 * 2
    WSZ = 12288
    Wt = ar.view(0, 2, WSZ)
    o = 2 * WSZ
    X = [ar.view(o + b * D, D) for b in range(2)]; o += 2 * D
    XT = [ar.view(o + b * D, KD, P) for b in range(2)]; o += 2 * D
    sg, hh = ar.view(o, FE), ar.view(o + FE, FE); o += 2 * FE
    hT = ar.view(o, 4, P); o += 512
    Y = [ar.view(o + b * D, D) for b in range(2)]; o += 2 * D
    assert o <= O_RT, o
    names = "t xt g u sg h ht htc y yc".split()
    s = {n: k.sem("ex_" + n) for n in names}
    s_w, s_x, s_yo = ([k.sem(f"ex_{n}{b}") for b in range(2)] for n in ("w", "x", "yo"))
    w1, w3 = (t[n].rearrange("o e (a p) f -> p (o e) a f", p=P) for n in ("w1", "w3"))
    w2 = t["w2"].rearrange("o e (a p) d -> p (o e) a d", p=P)

    def loops(eng, body, otherwise=None):
        count = eng.value_load(used, min_val=0, max_val=NB)
        for b in range(2):
            body(b, b, True)
        with eng.Fori(1, SURE // 2) as i:
            for b in range(2):
                body(2 * i + b, b, False)
        with eng.Fori(SURE // 2, NB // 2) as i:
            for b in range(2):
                with eng.If(count > 2 * i + b):
                    body(2 * i + b, b, False)
                if otherwise:
                    with eng.Else():
                        otherwise(2 * i + b, b)

    with nc.Block() as block:
        @block.sync
        def _(sp):
            def body(n, b, first):
                e = sp.value_load(be[0:1, bass.ds(n, 1)], min_val=0, max_val=NE - 1)
                at = sp.value_load(buf[0:1, bass.ds(n, 1)], min_val=0, max_val=1)
                new = sp.value_load(chg[0:1, bass.ds(n, 1)], min_val=0, max_val=1)
                if not first:
                    sp.wait_ge(s["y"], n - 1)
                for j, (src, wd) in enumerate(((w1, FE), (w3, FE), (w2, D))):
                    dst = Wt[:, bass.ds(at, 1), j * 4096:(j + 1) * 4096].rearrange("p o (a f) -> p (o a) f", f=wd)
                    sp.dma_start(dst, src[:, bass.ds(e, 1), :, :].rearrange("p o a f -> p (o a) f"), cond=new).then_inc(s_w[b], 16)
            loops(sp, body)

        @block.gpsimd
        def _(po):
            count = po.value_load(used, min_val=0, max_val=NB)

            def body(n, b, first):
                if not first:
                    po.wait_ge(s["t"], n - 1)
                po.indirect_dma_start(X[b], None, t["h2"], bass.IndirectOffsetOnAxis(ap=tok[:, n % NB:n % NB + 1], axis=0)).then_inc(s_x[b], 16)
            for n in range(NB + 1):
                if n <= SURE:
                    body(n, n % 2, n < 2)
                else:
                    with po.If(count + 1 > n):
                        body(n, n % 2, False)

        @block.tensor
        def _(pe):
            def turn(b, half):
                for a in range(4 * half, 4 * half + 4):
                    ins = pe.transpose(ps[:, half, (a % 4) * P:(a % 4 + 1) * P], X[b][:, a * P:(a + 1) * P], k.ident)
                if half:
                    ins.then_inc(s["t"], 1)

            def body(n, i, b):
                at = pe.value_load(buf[0:1, bass.ds(n, 1)], min_val=0, max_val=1)

                def w(off, width):
                    return Wt[:, bass.ds(at, 1), off:off + width].rearrange("p o a -> p (o a)")

                pe.wait_ge(s_w[b], (i + 1) * 48)
                pe.wait_ge(s["xt"], n + 1)
                if not (isinstance(n, int) and n == 0):
                    pe.wait_ge(s["h"], n)
                for m in range(2):
                    for a in range(KD):
                        ins = pe.matmul(ps[:, 2 + m, :], XT[b][:, a, :], w(m * 4096 + a * FE, FE), start=(a == 0), stop=(a == KD - 1))
                    ins.then_inc(s["gu"[m]], 1)
                pe.wait_ge(s_x[1 - b], (i + 1 + b) * 16)
                turn(1 - b, 0)
                pe.wait_ge(s["h"], n + 1)
                for a in range(4):
                    ins = pe.transpose(ps[:, 4, a * P:(a + 1) * P], hh[:, a * P:(a + 1) * P], k.ident)
                ins.then_inc(s["ht"], 1)
                turn(1 - b, 1)
                pe.wait_ge(s["htc"], n + 1)
                if not (isinstance(n, int) and n == 0):
                    pe.wait_ge(s["yc"], n)
                for c in range(2):
                    for a in range(4):
                        ins = pe.matmul(ps[:, 5 + c, :], hT[:, a, :], w(8192 + a * D + c * 512, 512), start=(a == 0), stop=(a == 3))
                ins.then_inc(s["y"], 1)

            count = pe.value_load(used, min_val=0, max_val=NB)
            pe.wait_ge(s_x[0], 16)
            turn(0, 0)
            turn(0, 1)
            body(0, 0, 0)
            body(1, 0, 1)
            with pe.Fori(1, SURE // 2) as i:
                body(2 * i, i, 0)
                body(2 * i + 1, i, 1)
            with pe.Fori(SURE // 2, NB // 2) as i:
                for b in range(2):
                    with pe.If(count > 2 * i + b):
                        body(2 * i + b, i, b)

        @block.scalar
        def _(act):
            def body(n, b, first):
                act.wait_ge(s["g"], n + 1)
                if not (isinstance(n, int) and n == 0):
                    act.wait_ge(s["h"], n)
                act.activation(sg, ps[:, 2, :], ACT.Silu).then_inc(s["sg"], 1)
                act.wait_ge(s["y"], n + 1)
                if not first:
                    act.wait_ge(s_yo[b], (n - b) * 8)
                act.activation(Y[b], ps[:, 5:7, :].rearrange("p a b -> p (a b)"), ACT.Copy).then_inc(s["yc"], 1)
                act.wait_ge(s["yc"], n + 1)
                act.dma_start(t["yslot"][bass.ds(n * P, P), :], Y[b]).then_inc(s_yo[b], 16)
            def unused(n, b):
                act.dma_start(t["yslot"][bass.ds(n * P, P), :], Y[b]).then_inc(s_yo[b], 16)

            loops(act, body, unused)
            for b in range(2):
                act.wait_ge(s_yo[b], 16 * NB // 2)

        @block.vector
        def _(ve):
            def columns(n, b):
                ve.wait_ge(s["t"], n + 1)
                ve.tensor_copy(XT[b].rearrange("p a b -> p (a b)"), ps[:, 0:2, :].rearrange("p a b -> p (a b)")).then_inc(s["xt"], 1)

            def body(n, b, first):
                ve.wait_ge(s["sg"], n + 1)
                ve.wait_ge(s["u"], n + 1)
                if not (isinstance(n, int) and n == 0):
                    ve.wait_ge(s["ht"], n)
                ve.tensor_tensor(hh, sg, ps[:, 3, :], ALU.mult).then_inc(s["h"], 1)
                ve.wait_ge(s["ht"], n + 1)
                if not (isinstance(n, int) and n == 0):
                    ve.wait_ge(s["y"], n)
                ve.tensor_copy(hT.rearrange("p a b -> p (a b)"), ps[:, 4, :]).then_inc(s["htc"], 1)
                columns(n + 1, 1 - b)

            columns(0, 0)
            loops(ve, body)


def combine(k):
    nc, t, ar, ps = k.nc, k.t, k.ar, k.ps
    W = [ar.view(R_W1, NT), ar.view(R_W2, NT)]
    Dst = [ar.view(R_D1, NT, dt=I32), ar.view(R_D2, NT, dt=I32)]
    o = 0
    gt, sc, sh = (ar.view(o + j * 2 * D, 2, D) for j in range(3)); o += 6 * D
    g = ar.view(o, D); o += D
    NBF = 3
    x1 = [ar.view(o + j * D, D) for j in range(NBF)]; o += NBF * D
    ya = [ar.view(o + j * D, D) for j in range(NBF)]; o += NBF * D
    yb = [ar.view(o + j * D, D) for j in range(NBF)]; o += NBF * D
    out = [ar.view(o + j * D, D) for j in range(NBF)]; o += NBF * D
    sq = ar.view(o, D); o += D
    ss, rs, sd, tm = (ar.view(o + 16 * j, NT) for j in range(4)); o += 64
    s = {n: k.sem("co_" + n) for n in "mod ss ms sd ch done res".split()}
    s_x, s_a, s_b, s_o = ([k.sem(f"co_{n}{b}") for b in range(NBF)] for n in ("x", "a", "b", "o"))

    with nc.Block() as block:
        @block.sync
        def _(sp):
            load_scale_shift(sp, k, s["mod"], sc, sh, (g, t["final_g"].rearrange("(o n) -> o n", o=1)), [(gt, 5), (sc, 7), (sh, 6)])
            for i in range(NT + 1):
                if i < NT:
                    if i >= NBF:
                        sp.wait_ge(s["done"], i - NBF + 1)
                    sp.dma_start(x1[i % NBF][0:ROWS[i], :], tile_rows(t["x1"], i)).then_inc(s_x[i % NBF], 16)
                if i >= 1:
                    j = i - 1
                    sp.wait_ge(s["done"], j + 1)
                    dst = t["y_prompt"].rearrange("o s d -> (o s) d")[j * P:(j + 1) * P, :] if j < NT - 1 else t["y_sample"].rearrange("b s d -> (b s) d")
                    sp.dma_start(dst, out[j % NBF][0:ROWS[j], :]).then_inc(s_o[j % NBF], 16)
            for b in range(NBF):
                sp.wait_ge(s_o[b], 16 * ((NT + NBF - 1 - b) // NBF))

        @block.gpsimd
        def _(po):
            for i in range(NT):
                r = ROWS[i]
                if i >= NBF:
                    po.wait_ge(s["done"], i - NBF + 1)
                for y, sm, d in ((ya, s_a, Dst[0]), (yb, s_b, Dst[1])):
                    po.indirect_dma_start(y[i % NBF][0:r, :], None, t["yslot"], bass.IndirectOffsetOnAxis(ap=d[0:r, i:i + 1], axis=0)).then_inc(sm[i % NBF], 16)

        @block.scalar
        def _(act):
            for i in range(NT):
                r = ROWS[i]
                act.wait_ge(s["res"], i + 1)
                if i >= 1:
                    act.wait_ge(s["ss"], i)
                act.activation(sq[0:r, :], x1[i % NBF][0:r, :], ACT.Square, accum_out=ss[0:r, i:i + 1]).then_inc(s["ss"], 1)
                act.wait_ge(s["ms"], i + 1)
                act.activation(sd[0:r, i:i + 1], ss[0:r, i:i + 1], ACT.Sqrt).then_inc(s["sd"], 1)

        @block.vector
        def _(ve):
            ch = Chain(ve, s["ch"])
            ve.wait_ge(s["mod"], 16 * 7)
            ch.step(ve.scalar_tensor_tensor(sc[:, 0, :], sc[:, 0, :], 1.0, g, ALU.add, ALU.mult))
            ch.step(ve.scalar_tensor_tensor(sc[0:NS, 1, :], sc[0:NS, 1, :], 1.0, g[0:NS, :], ALU.add, ALU.mult))
            for i in range(NT):
                r, m, b, col = ROWS[i], int(i == NT - 1), i % NBF, slice(i, i + 1)
                n = 16 * (i // NBF + 1)
                a_, b_, x_ = ya[b][0:r, :], yb[b][0:r, :], x1[b][0:r, :]
                ve.wait_ge(s_a[b], n)
                ch.step(ve.tensor_scalar(a_, a_, W[0][0:r, col], None, ALU.mult))
                ve.wait_ge(s_b[b], n)
                ch.step(ve.scalar_tensor_tensor(a_, b_, W[1][0:r, col], a_, ALU.mult, ALU.add))
                ch.step(ve.tensor_tensor(a_, a_, gt[0:r, m, :], ALU.mult))
                ve.wait_ge(s_x[b], n)
                ve.tensor_tensor(x_, x_, a_, ALU.add).then_inc(s["res"], 1)
                ve.wait_ge(s["ss"], i + 1)
                ve.tensor_scalar(ss[0:r, col], ss[0:r, col], 1.0 / D, EPS, ALU.mult, ALU.add).then_inc(s["ms"], 1)
                ve.wait_ge(s["ms"], i + 1)
                rstd_steps(ch, ve, lambda: ve.wait_ge(s["sd"], i + 1), ss[0:r, col], rs[0:r, col], sd[0:r, col], tm[0:r, col])
                if i >= NBF:
                    ve.wait_ge(s_o[b], 16 * (i // NBF))
                ve.wait_ge(s["res"], i + 1)
                ch.step(ve.scalar_tensor_tensor(out[b][0:r, :], x_, rs[0:r, col], sc[0:r, m, :], ALU.mult, ALU.mult))
                ve.tensor_tensor(out[b][0:r, :], out[b][0:r, :], sh[0:r, m, :], ALU.add).then_inc(s["done"], 1)


_INS = ["x_prompt", "x_sample", "cache_k", "cache_v", "cache_kidx", "state_hgrn", "page_table", "c_prompt",
        "c_sample", "ada_w", "ada_b", "norm1_g", "norm2_g", "w_in", "idx_k_g", "hg_lb_logits", "attn_out_g",
        "hg_out_g", "w_out", "w_group", "b_group", "w_expert_router", "b_expert_router", "w1", "w3", "w2",
        "final_g", "ada_final_w", "ada_final_b"]
_OUTS = [("y_prompt", (1, SEQ, D)), ("y_sample", (DB, DS, D)),
         ("k_prompt", (1, 1, SEQ, HKV, HD)), ("v_prompt", (1, 1, SEQ, HKV, HD)), ("kidx_prompt", (1, 1, SEQ, HD)),
         ("hgrn_prompt", (1, 1, GH, DK, DK)),
         ("k_sample", (1, DB, DS, HKV, HD)), ("v_sample", (1, DB, DS, HKV, HD)), ("kidx_sample", (1, DB, DS, HD)),
         ("hgrn_sample", (1, DB, GH, DK, DK))]
_SCRATCH = [("mod", (1 + DB, 8 * D), F32), ("wi", (NS, IH), F32), ("att", (NS, 512), F32),
            ("x1", (T, D), F32), ("h2", (T, D), F32), ("hq", (P, GH, T), F32), ("hf", (P, GH, T), F32), ("hv", (P, NT, 512), F32), ("hg", (P, NT, 512), F32),
            ("tok", (NB * P, 1), I32), ("yslot", (NB * P, D), F32)]


def constants():
    p = np.arange(P)
    half = ROT // 2
    inv = (np.float32(THETA) ** (-np.arange(half, dtype=np.float32) * np.float32(2.0 / ROT))).astype(np.float32)
    pos = np.concatenate([np.arange(SEQ), PAST + p % DS]).astype(np.float32).reshape(NT, P)
    ang = (pos[:, :, None] * inv).astype(np.float32)
    rope = np.stack([np.cos(ang), np.sin(ang)], 2).transpose(1, 0, 2, 3)
    tri = (p[:, None] < p[None, :])
    causal = np.where(p[None, :] <= p[:, None], 0.0, NEG)
    small = np.zeros((P, 64))
    for j in range(DS):
        small[:, j] = np.where(j <= p % DS, 0.0, NEG)
    small[:, 8] = p % 8
    small[:, 9] = p
    small[:, 10:18] = (p[:, None] // DS == np.arange(DB)[None, :])
    cols = np.arange(T)
    reset = np.where(cols < SEQ, cols % C != 0, cols % DS != 0)[None, :]
    q = np.arange(C)
    m0 = np.tile(p[:, None] % C <= q[None, :], (1, 4))
    m1 = np.tile((p[:, None] <= q) & (p[:, None] // DS == q // DS), (1, 4))
    qmask = (np.arange(DB)[:, None] == np.arange(NS)[None, :] // DS).reshape(1, -1)
    r = np.arange(NS)
    sq = np.arange(DB)[:, None] * DS
    rsel = r[:, None, None] == (sq + (r % DS)[None, :])[None]
    msel = np.stack([(r[None, :] == (b * DS + r % DS)[:, None]) for b in range(DB)], 1)
    rt = np.zeros((1, 128))
    rt[0, 0:4] = [4, 3, 2, 1]
    rt[0, 16:16 + NT] = np.arange(NT) * P
    rt[0, 32:32 + NB] = np.arange(NB)
    tid = np.arange(NT)[None, :] * P + p[:, None]
    return {"k_route": rt, "k_tid": tid, "k_rsel": rsel.reshape(NS, -1), "k_msel": msel.reshape(NS, -1), "k_reset": reset, "k_masks": np.concatenate([m0, m1], 1), "k_qmask": qmask, "k_ident": np.eye(P), "k_rope": rope.reshape(P, -1), "k_tri": tri, "k_causal": causal, "k_small": small}


def kernel(**inputs):
    import concourse.bacc as _bacc
    from concourse.bass_utils import run_bass_kernel_spmd as _run

    nc = _bacc.Bacc("TRN2", target_bir_lowering=False, num_devices=1)
    arrays, t = {}, {}
    for name in _INS:
        a = np.ascontiguousarray(inputs[name])
        arrays["in_" + name] = a
        t[name] = nc.dram_tensor("in_" + name, a.shape, mybir.dt.from_np(a.dtype), kind="ExternalInput").ap()
    for name, a in constants().items():
        a = np.ascontiguousarray(a, np.float32)
        arrays[name] = a
        t[name] = nc.dram_tensor(name, a.shape, F32, kind="ExternalInput").ap()
    for name, shape in _OUTS:
        t[name] = nc.dram_tensor("out_" + name, shape, F32, kind="ExternalOutput").ap()
    for name, shape, dt in _SCRATCH:
        t[name] = nc.dram_tensor("tmp_" + name, shape, dt, kind="Internal").ap()
    build(nc, t)
    r = _run(nc, [arrays], core_ids=[0])
    return tuple(r.results[0]["out_" + name] for name, _ in _OUTS)
```

```python
from contextlib import ExitStack

import concourse.bass as bass
import numpy as np
from concourse import mybir

F32 = mybir.dt.float32
I32 = mybir.dt.int32
ALU = mybir.AluOpType
ACT = mybir.ActivationFunctionType
AX = mybir.AxisListType

P = 128
D = 1024
KD = D // P
SEQ = 1024
DB, DS = 8, 8
NS = DB * DS
T = SEQ + NS
NT = SEQ // P + 1
ROWS = [P] * (NT - 1) + [NS]
PAST, PAGE, POOL_PAGES = 2048, 128, 160
H, HKV, HD = 8, 4, 64
IH = 8
ROT, THETA = 16, 500000.0
RH = ROT // 2
TOPK = 256
GH, DK, C = 4, 128, 64
N_IN = 3656
HQ0, HF0, HI0, HG0 = 1608, 2120, 2632, 3144
NA = 1608
NE, FE = 16, 512
A_TOT = 2 * T
NC = 1 + DB
ADA1 = 4
ADA2, ADA3 = 9, 12
NB = (A_TOT - NE) // P + NE
EPS = 1e-6
NEG, TAKEN = -3.0e38, -3.3e38
OFF = -1.0e30


class Arena:

    def __init__(self, tensor, size):
        self.t, self.size = tensor, size

    def view(self, off, *dims, p=P, dt=F32):
        n = int(np.prod(dims))
        assert off + n <= self.size, (off, n)
        ap = self.t[0:p, off:off + n]
        if dt != F32:
            ap = ap.bitcast(dt)
        if len(dims) == 2:
            ap = ap.rearrange("p (a b) -> p a b", b=dims[1])
        if len(dims) == 3:
            ap = ap.rearrange("p (a b c) -> p a b c", b=dims[1], c=dims[2])
        return ap


class Chain:

    def __init__(self, eng, sem, base=0):
        self.eng, self.sem, self.n = eng, sem, base

    def step(self, ins):
        self.mark(ins)
        self.join()

    def mark(self, ins):
        self.n = self.n + 1
        ins.then_inc(self.sem, 1)

    def join(self):
        self.eng.wait_ge(self.sem, self.n)


def build(nc, t):
    ctx = ExitStack()
    with ctx:
        size = 52800
        ar = Arena(ctx.enter_context(nc.sbuf_tensor("arena", [P, size], F32)), size)
        ps = ctx.enter_context(nc.psum_tensor("banks", [P, 8, 512], F32))
        k = Ctx(nc, ctx, t, ar, ps)
        stages = [modulation, norm_project, rope, index, prompt_attention, sample_attention, hgrn,
                  project_out, route, experts, combine]
        for stage in stages:
            stage(k)
            k.next_stage()


class Ctx:
    def __init__(self, nc, ctx, t, ar, ps):
        self.nc, self.ctx, self.t, self.ar, self.ps = nc, ctx, t, ar, ps
        o = ar.size
        def take(n):
            nonlocal o
            o -= n
            return o
        self.o_ident = take(P)
        self.o_rope = take(NT * 2 * RH)
        self.o_tri = take(P)
        self.o_cb = take(P)
        self.o_small = take(64)
        self.o_idx = take(8)
        self.o_c = take(KD * NC)
        self.o_ones = take(NC)
        self.end = o
        self.ident = ar.view(self.o_ident, P)
        self.rope = ar.view(self.o_rope, NT, 2, RH)
        self.tri = ar.view(self.o_tri, P)
        self.cb = ar.view(self.o_cb, P)
        self.small = ar.view(self.o_small, 64)

        self.cT = ar.view(self.o_c, KD, NC)
        self.ones = ar.view(self.o_ones, NC, p=1)

        self.used = []

    def sem(self, name):
        self.used.append(self.nc.alloc_semaphore(name))
        return self.used[-1]

    def next_stage(self):
        self.nc.clear_and_free_semaphores(self.used)
        self.nc.all_engine_barrier()
        self.used = []


HT = 0
O_A = 0
O_R = NT * 512
O_Z = KD * T
O_ACC = O_Z + NT * NA
O_ACCS = O_ACC + P * (NT - 1) * NT // 2
O_KIT = O_ACCS + PAST + DS
O_F = O_KIT + SEQ
O_KT = NT * 512
QC, KC, VC, QIC, KIC, WIC = 0, 512, 768, 1024, 1536, 1600
ACC_AT = [O_ACC + P * i * (i + 1) // 2 for i in range(NT - 1)]
O_K = O_R + NT * 512
O_HQ = O_K + 12288
O_HF = O_HQ + GH * T
O_V = O_HF + GH * T
O_G = O_V + NT * 512
O_END = O_G + NT * 512
O_X = O_ACC
O_RS = 51900


def modulation(k):
    nc, t, ar, ps = k.nc, k.t, k.ar, k.ps
    W = 512
    csb, cT, ones = ar.view(0, D, p=NC), k.cT, k.ones
    bias = ar.view(1200, ADA1 * W, p=1)
    row = [ar.view(3300 + b * W, W, p=NC) for b in range(ADA1)]
    sq = [ar.view(6000 + b * D, D) for b in range(2)]
    x, rs = ar.view(O_X, NT, D), ar.view(O_RS, NT)
    ss, sd, tmp = (ar.view(O_RS + 16 * j, NT) for j in range(1, 4))
    wch = [ar.view(O_X + NT * D + b * KD * W, KD, W) for b in range(ADA1)]
    names = "const c bias silu ct cts ones mm row out x zero sq ms sd ch".split()
    s = {n: k.sem("mod_" + n) for n in names}
    s_w = [k.sem(f"mod_w{b}") for b in range(ADA1)]
    ada_v = t["ada_w"].rearrange("o (a p) n -> p (o a) n", p=P)

    with nc.Block() as block:
        @block.sync
        def _(sp):
            sp.dma_start(csb[0:1, :], t["c_prompt"]).then_inc(s["c"], 16)
            sp.dma_start(csb[1:NC, :], t["c_sample"]).then_inc(s["c"], 16)
            sp.dma_start(k.ident, t["k_ident"]).then_inc(s["const"], 16)
            sp.dma_start(bias, t["ada_b"][:, 0:ADA1 * W]).then_inc(s["bias"], 16)
            for dst, src in ((k.rope, "k_rope"), (k.tri, "k_tri"), (k.cb, "k_causal"), (k.small, "k_small")):
                sp.dma_start(dst, t[src]).then_inc(s["const"], 16)
            for n in range(ADA1):
                sp.dma_start(wch[n], ada_v[:, :, n * W:(n + 1) * W]).then_inc(s_w[n], 16)
            sp.dma_start(x[:, 0:NT - 1, :], t["x_prompt"].rearrange("o (i p) d -> p (o i) d", p=P)).then_inc(s["x"], 16)
            sp.dma_start(x[0:NS, NT - 1, :], x_rows(t, NT - 1)).then_inc(s["x"], 16)
            sp.wait_ge(s["const"], 80)

        @block.scalar
        def _(act):
            act.wait_ge(s["c"], 32)
            act.activation(csb, csb, ACT.Silu).then_inc(s["silu"], 1)
            act.wait_ge(s["x"], 32)
            act.wait_ge(s["zero"], 1)
            for i in range(NT):
                r = ROWS[i]
                if i >= 2:
                    act.wait_ge(s["sq"], i - 1)
                act.activation(sq[i % 2][0:r, :], x[0:r, i, :], ACT.Square, accum_out=ss[0:r, i:i + 1]).then_inc(s["sq"], 1)
            act.wait_ge(s["ms"], 1)
            act.activation(sd, ss, ACT.Sqrt).then_inc(s["sd"], 1)
            for n in range(ADA1):
                act.wait_ge(s["row"], n + 1)
                act.dma_start(t["mod"][:, n * W:(n + 1) * W], row[n]).then_inc(s["out"], 16)
            act.wait_ge(s["out"], 16 * ADA1)

        @block.tensor
        def _(pe):
            pe.wait_ge(s["silu"], 1)
            pe.wait_ge(s["const"], 80)
            for a in range(KD):
                ins = pe.transpose(ps[:, 7, NC * a:NC * a + NC], csb[:, a * P:(a + 1) * P], k.ident[0:NC, 0:NC])
            ins.then_inc(s["ct"], 1)
            pe.wait_ge(s["cts"], 1)
            pe.wait_ge(s["ones"], 1)
            pe.wait_ge(s["bias"], 16)
            for n in range(ADA1):
                pe.wait_ge(s_w[n], 16)
                for a in range(KD):
                    pe.matmul(ps[0:NC, n, :], cT[:, a, :], wch[n][:, a, :], start=(a == 0), stop=False)
                pe.matmul(ps[0:NC, n, :], ones, bias[:, n * W:(n + 1) * W], start=False, stop=True).then_inc(s["mm"], 1)

        @block.vector
        def _(ve):
            ch = Chain(ve, s["ch"])
            ve.memset(ones, 1.0).then_inc(s["ones"], 1)
            ve.memset(ss, 0.0).then_inc(s["zero"], 1)
            ve.wait_ge(s["ct"], 1)
            ve.tensor_copy(cT.rearrange("p a b -> p (a b)"), ps[:, 7, 0:KD * NC]).then_inc(s["cts"], 1)
            for n in range(ADA1):
                ve.wait_ge(s["mm"], n + 1)
                ve.tensor_copy(row[n], ps[0:NC, n, :]).then_inc(s["row"], 1)
            ve.wait_ge(s["sq"], NT)
            ve.tensor_scalar(ss, ss, 1.0 / D, EPS, ALU.mult, ALU.add).then_inc(s["ms"], 1)
            ve.wait_ge(s["ms"], 1)
            rstd_steps(ch, ve, lambda: ve.wait_ge(s["sd"], 1), ss, rs, sd, tmp)


def modulation_chunks(t):
    ada = t["ada_w"].rearrange("o (a p) n -> p (o a) n", p=P)
    fin = t["ada_final_w"].rearrange("(a p) n -> p a n", p=P)
    return ([(ada, t["ada_b"], n) for n in range(12)]
            + [(fin, t["ada_final_b"].rearrange("(o n) -> o n", o=1), n) for n in range(4)])


def scale_shift_parts(k, g, parts):
    mod, moves = k.t["mod"], []
    for dst, col in parts:
        cs = slice(col * D, (col + 1) * D)
        moves.append((dst[:, 0, :], mod[0:1, cs].broadcast_to([P, D])))
        moves.append((dst[0:NS, 1, :], mod[1:1 + DB, cs].unsqueeze(1).broadcast_to([DB, DS, D])))
    return moves + [(g[0], g[1].broadcast_to([P, D]))]


def load_scale_shift(eng, k, sem, g, parts):
    for dst, src in scale_shift_parts(k, g, parts):
        eng.dma_start(dst, src).then_inc(sem, 16)


def tile_rows(t, i):
    return t[i * P:i * P + ROWS[i], :]


def x_rows(t, i):
    if i < NT - 1:
        return t["x_prompt"].rearrange("o s d -> (o s) d")[i * P:(i + 1) * P, :]
    return t["x_sample"].rearrange("b s d -> (b s) d")


def rstd_steps(ch, ve, act_sqrt, ms, y, w1, w2):
    act_sqrt()
    ch.step(ve.reciprocal(y, w1))
    ch.step(ve.tensor_tensor(w2, y, y, ALU.mult))
    ch.step(ve.tensor_tensor(w2, w2, ms, ALU.mult))
    ch.step(ve.tensor_scalar(w2, w2, -0.5, 1.5, ALU.mult, ALU.add))
    ch.step(ve.tensor_tensor(y, y, w2, ALU.mult))


def norm_project(k):
    nc, t, ar, ps = k.nc, k.t, k.ar, k.ps
    hT, z = ar.view(HT, KD, T), ar.view(O_Z, NT, NA)
    x, rs = ar.view(O_X, NT, D), ar.view(O_RS, NT)
    o = O_X + NT * D
    w = [ar.view(o + b * KD * 512, KD, 512) for b in range(3)]; o += 3 * KD * 512
    h = [ar.view(o + b * D, D) for b in range(2)]; o += 2 * D
    sc, sh = ar.view(o, 2, D), ar.view(o + 2 * D, 2, D); o += 4 * D
    g = ar.view(o, D); o += D
    assert o <= O_RS
    w_v = t["w_in"].rearrange("o (a p) n -> p (o a) n", p=P)
    jobs = [(c, min(512, NA - c)) for c in range(0, NA, 512)]
    groups = [(j, i) for j in range(len(jobs)) for i in range(NT)]
    NBK = 6
    names = "mod ch h t hT mm ev".split()
    s = {n: k.sem("np_" + n) for n in names}
    s_w = [k.sem(f"np_w{b}") for b in range(3)]

    with nc.Block() as block:
        @block.sync
        def _(sp):
            def load(j):
                c, wd = jobs[j]
                sp.dma_start(w[j % 3][:, :, 0:wd], w_v[:, :, c:c + wd]).then_inc(s_w[j % 3], 16)

            load_scale_shift(sp, k, s["mod"], (g, t["norm1_g"]), [(sc, 1), (sh, 0)])
            for j in range(len(jobs)):
                if j >= 3:
                    sp.wait_ge(s["mm"], NT * (j - 2))
                load(j)

        @block.vector
        def _(ve):
            ch = Chain(ve, s["ch"])
            ve.wait_ge(s["mod"], 16 * 5)
            ch.step(ve.scalar_tensor_tensor(sc[:, 0, :], sc[:, 0, :], 1.0, g, ALU.add, ALU.mult))
            ch.step(ve.scalar_tensor_tensor(sc[0:NS, 1, :], sc[0:NS, 1, :], 1.0, g[0:NS, :], ALU.add, ALU.mult))
            for i in range(NT):
                r, m = ROWS[i], int(i == NT - 1)
                if i >= 2:
                    ve.wait_ge(s["t"], i - 1)
                ch.step(ve.scalar_tensor_tensor(h[i % 2][0:r, :], x[0:r, i, :], rs[0:r, i:i + 1], sc[0:r, m, :], ALU.mult, ALU.mult))
                ve.tensor_tensor(h[i % 2][0:r, :], h[i % 2][0:r, :], sh[0:r, m, :], ALU.add).then_inc(s["h"], 1)

        @block.tensor
        def _(pe):
            def turn(i):
                r = ROWS[i]
                pe.wait_ge(s["h"], i + 1)
                if i >= 1:
                    pe.wait_ge(s["hT"], i)
                for a in range(KD):
                    ins = pe.transpose(ps[:, 6 + a // 4, (a % 4) * P:(a % 4) * P + r], h[i % 2][0:r, a * P:(a + 1) * P], k.ident[0:r, 0:r])
                ins.then_inc(s["t"], 1)

            turn(0)
            for n, (j, i) in enumerate(groups):
                r, wd = ROWS[i], jobs[j][1]
                if j == 0:
                    if i + 1 < NT:
                        turn(i + 1)
                    pe.wait_ge(s["hT"], i + 1)
                if i == 0:
                    pe.wait_ge(s_w[j % 3], 16 * (j // 3 + 1))
                if n >= NBK:
                    pe.wait_ge(s["ev"], n - NBK + 1)
                for a in range(KD):
                    ins = pe.matmul(ps[0:r, n % NBK, 0:wd], hT[:, a, i * P:i * P + r], w[j % 3][:, a, 0:wd], start=(a == 0), stop=(a == KD - 1))
                ins.then_inc(s["mm"], 1)

        @block.scalar
        def _(act):
            def columns(i):
                r = ROWS[i]
                act.wait_ge(s["t"], i + 1)
                act.activation(hT[:, :, i * P:i * P + r], ps[:, 6:8, :].rearrange("p b (a n) -> p (b a) n", n=P)[:, :, 0:r], ACT.Copy).then_inc(s["hT"], 1)

            columns(0)
            for n, (j, i) in enumerate(groups):
                r, (c, wd) = ROWS[i], jobs[j]
                if j == 0 and i + 1 < NT:
                    columns(i + 1)
                act.wait_ge(s["mm"], n + 1)
                act.activation(z[0:r, i, c:c + wd], ps[0:r, n % NBK, 0:wd], ACT.Copy).then_inc(s["ev"], 1)


def hgrn(k):
    nc, t, ar, ps = k.nc, k.t, k.ar, k.ps
    NCH = SEQ // C
    Q, F = ar.view(O_HQ, GH, T), ar.view(O_HF, GH, T)
    K, B = ar.view(O_K, GH, T), ar.view(O_K + GH * T, GH, T)
    o = O_K + 2 * GH * T
    reset = ar.view(o, T); o += T
    mask = ar.view(o, 2, 4 * C, dt=I32); o += 8 * C
    kst = [ar.view(o + b * 512, 512) for b in range(2)]; o += 1024
    BL, EBL = ar.view(o, GH, NCH + DB), ar.view(o + 96, GH, NCH + DB); o += 192
    lbl, lb, oml = ar.view(o, GH, 2), ar.view(o + 8, GH), ar.view(o + 12, GH); o += 16
    lbm, lbe, lbs = ar.view(o, GH), ar.view(o + 4, GH, 2), ar.view(o + 12, GH); o += 16
    ssq, rs, tmp, sd = (ar.view(o + 36 * j, NT * GH) for j in range(4)); o += 144
    A, ga = ar.view(O_A, NT, 512), ar.view(o, 512); o += 512
    ssa, rsa, sda, tma = (ar.view(o + 16 * j, NT) for j in range(4)); o += 64
    parts = ((P, 0, NT - 1), (NS, NT - 1, NT))
    assert o <= O_HQ
    V, G, R = ar.view(O_V, NT, 512), ar.view(O_G, NT, 512), ar.view(O_R, NT, 512)
    o = O_END
    att = [ar.view(o + b * 256, 4 * C) for b in range(2)]; o += 512
    S = [ar.view(o + b * 512, GH, DK) for b in range(2)]; o += 1024
    sq = ar.view(o, 512); o += 512
    gn = ar.view(o, 512); o += 512
    o_s0 = o
    S0 = ar.view(o, DB, GH * DK); o += DB * GH * DK
    vm = ar.view(o, DB, DK); o += DB * DK
    qp = ar.view(o, DB * NS); o += DB * NS
    assert o <= k.end, (o, k.end)
    qmk = ar.view(o_s0 - 512, DB * NS)
    ada = modulation_chunks(t)[ADA3:]
    wa = [ar.view(a, KD, 512) for a in (o_s0, o)]
    assert o + KD * 512 <= k.end
    ba = [ar.view(o_s0 + 4096 + b * 512, 512, p=1) for b in range(2)]
    row = ar.view(o_s0 + 4096 + 1024, 512, p=NC)
    s_wa, s_ba = ([k.sem(f"hg_{n}{b}") for b in range(2)] for n in ("wa", "ba"))

    names = ("const lb lbd lbe sig f k ln b eb q enb kin d est kst ebl g gate zero att attm tr trc ds s1 s2 o oc red"
             " ch out s0 qm vm qp sds st so soc fin zf zq zv ap ae ao ga sqa msa sda an").split()
    s = {n: k.sem("hg_" + n) for n in names}
    SB = slice(SEQ, T)

    with nc.Block() as block:
        @block.sync
        def _(sp):
            with nc.allow_non_contiguous_dma(reason="1024 values"):
                for j in range(2):
                    sp.dma_start(lbl[:, :, j], t["hg_lb_logits"][j, :].rearrange("(h p) -> p h", p=P)).then_inc(s["lb"], 16)
            sp.dma_start(ga, t["attn_out_g"].broadcast_to([P, 512])).then_inc(s["ga"], 16)

            def load_ada(n):
                w, b, c = ada[n]
                sp.dma_start(ba[n % 2], b[:, c * 512:(c + 1) * 512]).then_inc(s_ba[n % 2], 16)
                sp.dma_start(wa[n % 2], w[:, :, c * 512:(c + 1) * 512]).then_inc(s_wa[n % 2], 16)

            sp.dma_start(F, t["hf"]).then_inc(s["zf"], 16)
            load_ada(0)
            sp.dma_start(reset, t["k_reset"].broadcast_to([P, T])).then_inc(s["const"], 16)
            sp.dma_start(mask.rearrange("p a b -> p (a b)"), t["k_masks"].bitcast(I32)).then_inc(s["const"], 16)
            sp.dma_start(gn, t["hg_out_g"].broadcast_to([P, 512])).then_inc(s["g"], 16)
            sp.dma_start(Q, t["hq"]).then_inc(s["zq"], 16)
            load_ada(1)
            for dst, src in ((V, t["hv"]), (G, t["hg"])):
                sp.dma_start(dst[:, 0:NT - 1, :], src[:, 0:NT - 1, :]).then_inc(s["zv"], 16)
                sp.dma_start(dst[0:NS, NT - 1, :], src[0:NS, NT - 1, :]).then_inc(s["zv"], 16)
            for n in range(2, len(ada)):
                sp.wait_ge(s["ap"], n - 1)
                load_ada(n)
            sp.wait_ge(s["ap"], len(ada))
            sp.dma_start(S0.rearrange("p s (h e) -> p s h e", e=DK), t["state_hgrn"].rearrange("o s h p e -> p (o s) h e")).then_inc(s["s0"], 16)
            sp.wait_ge(s["gate"], 2)
            sp.dma_start(qmk, t["k_qmask"].broadcast_to([P, DB * NS])).then_inc(s["qm"], 16)
            sp.wait_ge(s["s2"], 4 * (NT - 1))
            sp.dma_start(t["hgrn_prompt"].rearrange("a b h p e -> p (a b h) e"), S[0]).then_inc(s["out"], 16)
            sp.wait_ge(s["st"], 2 * GH)
            sp.dma_start(t["hgrn_sample"].rearrange("o s h p e -> p (o s) h e"), S0.rearrange("p s (h e) -> p s h e", e=DK)).then_inc(s["out"], 16)
            sp.wait_ge(s["out"], 32)
            sp.wait_ge(s["ao"], 16 * len(ada))

        @block.scalar
        def _(act):
            def root(i):
                r, hs = ROWS[i], slice(i * GH, (i + 1) * GH)
                act.wait_ge(s["soc"], i + 1)
                act.activation(sd[0:r, hs], ssq[0:r, hs], ACT.Sqrt).then_inc(s["so"], 1)

            def ada_row(n):
                act.wait_ge(s["ap"], n + 1)
                if n:
                    act.wait_ge(s["ao"], 16 * n)
                act.activation(row, ps[0:NC, 4 + n, :], ACT.Copy).then_inc(s["ae"], 1)
                act.wait_ge(s["ae"], n + 1)
                act.dma_start(t["mod"][:, (ADA3 + n) * 512:(ADA3 + n + 1) * 512], row).then_inc(s["ao"], 16)

            for n, a, b in parts:
                for i in range(a, b):
                    if i >= 1:
                        act.wait_ge(s["sqa"], i)
                    act.activation(sq[0:n, :], A[0:n, i, :], ACT.Square, accum_out=ssa[0:n, i:i + 1]).then_inc(s["sqa"], 1)
            for m, (n, a, b) in enumerate(parts):
                act.wait_ge(s["msa"], m + 1)
                act.activation(sda[0:n, a:b], ssa[0:n, a:b], ACT.Sqrt).then_inc(s["sda"], 1)
            act.wait_ge(s["zf"], 16)
            for h in range(GH):
                act.activation(F[:, h, :], F[:, h, :], ACT.Sigmoid).then_inc(s["sig"], 1)
            act.wait_ge(s["lbd"], 1)
            act.activation(lbe.rearrange("p a b -> p (a b)"), lbl.rearrange("p a b -> p (a b)"), ACT.Exp).then_inc(s["lbe"], 1)
            for h in range(GH):
                act.wait_ge(s["k"], h + 1)
                act.activation(F[:, h, :], F[:, h, :], ACT.Ln).then_inc(s["ln"], 1)
            for h in range(GH):
                act.wait_ge(s["b"], h + 1)
                act.activation(F[:, h, :], B[:, h, :], ACT.Exp).then_inc(s["eb"], 1)
            act.activation(EBL, BL, ACT.Exp).then_inc(s["ebl"], 1)
            for h in range(GH):
                act.wait_ge(s["q"], h + 1)
                act.activation(F[:, h, :], B[:, h, :], ACT.Exp, scale=-1.0).then_inc(s["enb"], 1)
            for h in range(GH):
                act.wait_ge(s["d"], h + 1)
                act.activation(B[:, h, :], B[:, h, :], ACT.Exp).then_inc(s["est"], 1)
            for n in range(len(ada)):
                ada_row(n)
            act.wait_ge(s["zv"], 64)
            act.activation(G[:, 0:NT - 1, :], G[:, 0:NT - 1, :], ACT.Silu).then_inc(s["fin"], 1)
            act.activation(G[0:NS, NT - 1, :], G[0:NS, NT - 1, :], ACT.Silu).then_inc(s["fin"], 1)
            for i in range(NT):
                r = ROWS[i]
                act.wait_ge(s["tr"], i + 1)
                if i >= 2:
                    act.wait_ge(s["ds"], 2 * (i - 1))
                act.activation(kst[i % 2][0:r, :], ps[0:r, 2 + i % 2, :], ACT.Copy).then_inc(s["trc"], 1)
                act.wait_ge(s["o"], i + 1)
                act.activation(R[0:r, i, :], ps[0:r, 6 + i % 2, :], ACT.Copy).then_inc(s["oc"], 1)
                if i >= 1:
                    act.wait_ge(s["red"], i)
                act.activation(sq[0:r, :], ps[0:r, 6 + i % 2, :], ACT.Square).then_inc(s["oc"], 1)
                if i >= 1:
                    root(i - 1)
            root(NT - 1)

        @block.tensor
        def _(pe):
            for n in range(len(ada)):
                pe.wait_ge(s_wa[n % 2], 16 * (n // 2 + 1))
                pe.wait_ge(s_ba[n % 2], 16 * (n // 2 + 1))
                for a in range(KD):
                    pe.matmul(ps[0:NC, 4 + n, :], k.cT[:, a, :], wa[n % 2][:, a, :], start=(a == 0), stop=False)
                pe.matmul(ps[0:NC, 4 + n, :], k.ones, ba[n % 2], start=False, stop=True).then_inc(s["ap"], 1)
            pe.wait_ge(s["ae"], len(ada))
            pe.wait_ge(s["zv"], 64)
            pe.wait_ge(s["kin"], GH)
            pe.wait_ge(s["kst"], GH)
            for i in range(NT - 1):
                for h in range(GH):
                    for j in range(2):
                        cs = slice(i * P + j * C, i * P + (j + 1) * C)
                        ins = pe.matmul(ps[j * C:(j + 1) * C, i % 2, h * C:(h + 1) * C], F[:, h, cs], Q[:, h, cs], start=True, stop=True)
                ins.then_inc(s["att"], 1)
                if i >= 2:
                    pe.wait_ge(s["trc"], i - 1)
                for h in range(GH):
                    ins = pe.transpose(ps[:, 2 + i % 2, h * DK:(h + 1) * DK], K[:, h, i * P:(i + 1) * P], k.ident)
                ins.then_inc(s["tr"], 1)
                pe.wait_ge(s["trc"], i + 1)
                for j in range(2):
                    if i >= 1:
                        pe.wait_ge(s[("s1", "s2")[j]], 4 * i)
                    for h in range(GH):
                        hs = slice(h * DK, (h + 1) * DK)
                        ins = pe.matmul(ps[:, 4 + j, hs], kst[i % 2][j * C:(j + 1) * C, hs], V[j * C:(j + 1) * C, i, hs], start=True, stop=True)
                    ins.then_inc(s["ds"], 1)
                pe.wait_ge(s["attm"], i + 1)
                if i >= 2:
                    pe.wait_ge(s["oc"], 2 * (i - 1))
                pe.wait_ge(s["zero"], 5)
                for j in range(2):
                    if j == 1:
                        pe.wait_ge(s["s1"], 4 * (i + 1))
                    elif i >= 1:
                        pe.wait_ge(s["s2"], 4 * i)
                    for h in range(GH):
                        hs, cs = slice(h * DK, (h + 1) * DK), slice(i * P + j * C, i * P + (j + 1) * C)
                        js = slice(j * C, (j + 1) * C)
                        pe.matmul(ps[js, 6 + i % 2, hs], att[i % 2][js, h * C:(h + 1) * C], V[js, i, hs], start=True, stop=False)
                        ins = pe.matmul(ps[js, 6 + i % 2, hs], Q[:, h, cs], S[j][:, h, :], start=False, stop=True)
                ins.then_inc(s["o"], 1)
            i = NT - 1
            for h in range(GH):
                ins = pe.matmul(ps[0:NS, 0, h * NS:(h + 1) * NS], F[:, h, SB], Q[:, h, SB], start=True, stop=True)
            ins.then_inc(s["att"], 1)
            pe.wait_ge(s["trc"], i - 1)
            for h in range(GH):
                ins = pe.transpose(ps[0:NS, 2, h * DK:(h + 1) * DK], K[:, h, SB], k.ident)
            ins.then_inc(s["tr"], 1)
            pe.wait_ge(s["trc"], i + 1)
            pe.wait_ge(s["s2"], 4 * i)
            pe.wait_ge(s["attm"], i + 1)
            pe.wait_ge(s["oc"], 2 * (i - 1))
            for h in range(GH):
                hs = slice(h * DK, (h + 1) * DK)
                pe.wait_ge(s["vm"], h + 1)
                if h >= 1:
                    pe.wait_ge(s["st"], 2 * h)
                for j in range(2):
                    ins = pe.matmul(ps[:, 4 + j, :], kst[0][0:NS, hs], vm[0:NS, 4 * j:4 * j + 4, :], start=True, stop=True)
                ins.then_inc(s["sds"], 1)
                pe.matmul(ps[0:NS, 6, hs], att[0][0:NS, h * NS:(h + 1) * NS], V[0:NS, i, hs], start=True, stop=False)
                pe.wait_ge(s["qp"], h + 1)
                if h == 0:
                    pe.wait_ge(s["s0"], 16)
                for b in range(DB):
                    ins = pe.matmul(ps[0:NS, 6, hs], qp[:, b * NS:(b + 1) * NS], S0[:, b, hs], start=False, stop=(b == DB - 1))
                ins.then_inc(s["sds"], 1)
            pe.wait_ge(s["sds"], 2 * GH)
            pe.sem_inc(s["o"], 1)

        @block.vector
        def _(ve):
            ch = Chain(ve, s["ch"])
            for a in att:
                ve.memset(a, 0.0).then_inc(s["zero"], 1)
            for a in S:
                ve.memset(a, 0.0).then_inc(s["zero"], 1)
            ve.memset(ssq, 0.0).then_inc(s["zero"], 1)
            for m, (n, a, b) in enumerate(parts):
                ve.wait_ge(s["sqa"], b)
                ve.tensor_scalar(ssa[0:n, a:b], ssa[0:n, a:b], 1.0 / 512, EPS, ALU.mult, ALU.add).then_inc(s["msa"], 1)
                ve.wait_ge(s["msa"], m + 1)
            ve.wait_ge(s["ga"], 16)
            for m, (n, a, b) in enumerate(parts):
                rstd_steps(ch, ve, lambda: ve.wait_ge(s["sda"], m + 1), ssa[0:n, a:b], rsa[0:n, a:b], sda[0:n, a:b], tma[0:n, a:b])
                for i in range(a, b):
                    ve.scalar_tensor_tensor(A[0:n, i, :], A[0:n, i, :], rsa[0:n, i:i + 1], ga[0:n, :], ALU.mult, ALU.mult).then_inc(s["an"], 1)
            ve.wait_ge(s["lb"], 32)
            ch.step(ve.tensor_tensor(lbm, lbl[:, :, 0], lbl[:, :, 1], ALU.max))
            ch.mark(ve.tensor_tensor(lbl[:, :, 0], lbl[:, :, 0], lbm, ALU.subtract))
            ve.tensor_tensor(lbl[:, :, 1], lbl[:, :, 1], lbm, ALU.subtract).then_inc(s["lbd"], 1)
            ve.wait_ge(s["lbe"], 1)
            ch.step(ve.tensor_tensor(lbs, lbe[:, :, 0], lbe[:, :, 1], ALU.add))
            ch.step(ve.reciprocal(lbm, lbs))
            ch.step(ve.tensor_tensor(lb, lbe[:, :, 0], lbm, ALU.mult))
            ch.step(ve.tensor_scalar(oml, lb, -1.0, 1.0, ALU.mult, ALU.add))
            for h in range(GH):
                ve.wait_ge(s["sig"], h + 1)
                ve.tensor_scalar(F[:, h, :], F[:, h, :], oml[:, h:h + 1], lb[:, h:h + 1], ALU.mult, ALU.add).then_inc(s["f"], 1)
                ve.wait_ge(s["f"], h + 1)
                ve.tensor_scalar(K[:, h, :], F[:, h, :], -1.0, 1.0, ALU.mult, ALU.add).then_inc(s["k"], 1)
            ve.wait_ge(s["const"], 32)
            for h in range(GH):
                ve.wait_ge(s["ln"], h + 1)
                ch.step(ve.tensor_tensor_scan(B[:, h, :], reset, F[:, h, :], 0.0, ALU.mult, ALU.add))
                ch.mark(ve.tensor_copy(BL[:, h, 0:NCH], B[:, h, C - 1:SEQ:C]))
                ve.tensor_copy(BL[:, h, NCH:NCH + DB], B[:, h, SEQ + DS - 1:T:DS]).then_inc(s["b"], 1)
            ve.wait_ge(s["zq"], 16)
            for h in range(GH):
                ve.wait_ge(s["eb"], h + 1)
                ve.scalar_tensor_tensor(Q[:, h, :], Q[:, h, :], float(DK) ** -0.5, F[:, h, :], ALU.mult, ALU.mult).then_inc(s["q"], 1)
            ch.join()
            ve.wait_ge(s["b"], GH)
            for h in range(GH):
                ve.wait_ge(s["enb"], h + 1)
                ve.tensor_tensor(F[:, h, :], K[:, h, :], F[:, h, :], ALU.mult).then_inc(s["kin"], 1)
                ch.mark(ve.tensor_tensor(B[:, h, 0:SEQ].rearrange("p (a c) -> p a c", c=C), BL[:, h, 0:NCH].unsqueeze(2).broadcast_to([P, NCH, C]),
                                         B[:, h, 0:SEQ].rearrange("p (a c) -> p a c", c=C), ALU.subtract))
                ve.tensor_tensor(B[:, h, SB].rearrange("p (a c) -> p a c", c=DS), BL[:, h, NCH:NCH + DB].unsqueeze(2).broadcast_to([P, DB, DS]),
                                 B[:, h, SB].rearrange("p (a c) -> p a c", c=DS), ALU.subtract).then_inc(s["d"], 1)
            for h in range(GH):
                ve.wait_ge(s["est"], h + 1)
                ve.tensor_tensor(K[:, h, :], K[:, h, :], B[:, h, :], ALU.mult).then_inc(s["kst"], 1)
            ve.wait_ge(s["fin"], 2)
            ve.wait_ge(s["g"], 16)
            ve.tensor_tensor(G[:, 0:NT - 1, :], G[:, 0:NT - 1, :], gn.unsqueeze(1).broadcast_to([P, NT - 1, 512]), ALU.mult).then_inc(s["gate"], 1)
            ve.tensor_tensor(G[0:NS, NT - 1, :], G[0:NS, NT - 1, :], gn[0:NS, :], ALU.mult).then_inc(s["gate"], 1)
            ve.wait_ge(s["zero"], 5)
            ve.wait_ge(s["ebl"], 1)

            def sums(i):
                r = ROWS[i]
                ve.wait_ge(s["oc"], 2 * (i + 1))
                ve.tensor_reduce(ssq[0:r, i * GH:(i + 1) * GH], sq[0:r, :].rearrange("p (h e) -> p h e", e=DK), AX.X, ALU.add).then_inc(s["red"], 1)
                hs = slice(i * GH, (i + 1) * GH)
                ve.wait_ge(s["red"], i + 1)
                ve.tensor_scalar(ssq[0:r, hs], ssq[0:r, hs], 1.0 / DK, EPS, ALU.mult, ALU.add).then_inc(s["soc"], 1)

            def gated(i):
                r, hs = ROWS[i], slice(i * GH, (i + 1) * GH)
                ve.wait_ge(s["soc"], i + 1)
                rstd_steps(ch, ve, lambda: ve.wait_ge(s["so"], i + 1), ssq[0:r, hs], rs[0:r, hs], sd[0:r, hs], tmp[0:r, hs])
                Rv = R[0:r, i, :].rearrange("p (h e) -> p h e", e=DK)
                ch.step(ve.tensor_tensor(Rv, Rv, rs[0:r, hs].unsqueeze(2).broadcast_to([r, GH, DK]), ALU.mult))
                ch.step(ve.tensor_tensor(R[0:r, i, :], R[0:r, i, :], G[0:r, i, :], ALU.mult))

            for i in range(NT - 1):
                ve.wait_ge(s["att"], i + 1)
                if i >= 2:
                    ve.wait_ge(s["o"], i - 1)
                ve.copy_predicated(att[i % 2], mask[:, 0, :], ps[:, i % 2, 0:4 * C]).then_inc(s["attm"], 1)
                for j in range(2):
                    ve.wait_ge(s["ds"], 2 * i + j + 1)
                    if j == 0 and i >= 1:
                        ve.wait_ge(s["s2"], 4 * i)
                        ve.wait_ge(s["o"], i)
                    if j == 1:
                        ve.wait_ge(s["s1"], 4 * (i + 1))
                        ve.wait_ge(s["o"], i + 1)
                    for h in range(GH):
                        hs = slice(h * DK, (h + 1) * DK)
                        dst = S[1] if j == 0 else S[0]
                        ve.scalar_tensor_tensor(dst[:, h, :], S[j][:, h, :], EBL[:, h, 2 * i + j:2 * i + j + 1], ps[:, 4 + j, hs], ALU.mult, ALU.add).then_inc(s[("s1", "s2")[j]], 1)
                sums(i)
                if i >= 1:
                    gated(i - 1)
            i = NT - 1
            ve.wait_ge(s["att"], i + 1)
            ch.step(ve.memset(att[0][0:NS, :], 0.0))
            ve.copy_predicated(att[0][0:NS, :], mask[0:NS, 1, :], ps[0:NS, 0, 0:4 * NS]).then_inc(s["attm"], 1)
            ve.wait_ge(s["qm"], 16)
            ve.wait_ge(s["s0"], 16)
            ve.wait_ge(s["zv"], 64)
            ve.wait_ge(s["ao"], 16 * len(ada))
            for h in range(GH):
                hs = slice(h * DK, (h + 1) * DK)
                if h >= 1:
                    ve.wait_ge(s["sds"], 2 * h)
                ve.tensor_tensor(vm[0:NS, :, :], V[0:NS, i, hs].unsqueeze(1).broadcast_to([NS, DB, DK]),
                                 k.small[0:NS, 10:18].unsqueeze(2).broadcast_to([NS, DB, DK]), ALU.mult).then_inc(s["vm"], 1)
                ve.tensor_tensor(qp.rearrange("p (a b) -> p a b", b=NS), Q[:, h, SB].unsqueeze(1).broadcast_to([P, DB, NS]),
                                 qmk.rearrange("p (a b) -> p a b", b=NS), ALU.mult).then_inc(s["qp"], 1)
                ve.wait_ge(s["sds"], 2 * h + 2)
                ch.step(ve.tensor_tensor(S0[:, :, hs], S0[:, :, hs], EBL[:, h, NCH:NCH + DB].unsqueeze(2).broadcast_to([P, DB, DK]), ALU.mult))
                for j in range(2):
                    ve.tensor_tensor(S0[:, 4 * j:4 * j + 4, hs], S0[:, 4 * j:4 * j + 4, hs], ps[:, 4 + j, :].rearrange("p (a b) -> p a b", b=DK), ALU.add).then_inc(s["st"], 1)
            sums(i)
            gated(NT - 2)
            gated(NT - 1)


def gather_index(ve, ch, k, raw, idx):
    ch.step(ve.tensor_scalar(idx, raw, 8.0, k.small[:, 8:9], ALU.mult, ALU.add))


EARLY = 6


def recurrence_groups(k, wp):
    t, hT = k.t, k.ar.view(HT, KD, T)
    w_v = t["w_in"].rearrange("o (a p) n -> p (o a) n", p=P)
    chunks = ((HF0, "feat", t["hf"]), (HQ0, "feat", t["hq"]), (HI0, "tok", t["hv"]), (HG0, "tok", t["hg"]))
    groups = []
    for j, (c0, kind, dst) in enumerate(chunks):
        if kind == "tok":
            for i in range(NT):
                groups.append((j, ROWS[i], 512, (lambda a, i=i: hT[:, a, i * P:i * P + ROWS[i]]),
                               (lambda a, j=j: wp[j % 2][:, a, :]), dst[0:ROWS[i], i, :]))
        else:
            for f in range(GH):
                for c, n in ((0, 512), (512, 512), (1024, NS)):
                    groups.append((j, P, n, (lambda a, f=f, j=j: wp[j % 2][:, a, f * P:(f + 1) * P]),
                                   (lambda a, c=c, n=n: hT[:, a, c:c + n]), dst[:, f, c:c + n]))
    return w_v, chunks, groups


def rope(k):
    nc, t, ar, ps = k.nc, k.t, k.ar, k.ps
    z = ar.view(O_Z, NT, NA)
    kiT = ar.view(O_KIT, SEQ, p=HD)
    wp = ar.view(O_F, KD, 512)
    _, chunks, groups = recurrence_groups(k, [wp, wp])
    groups = groups[0:EARLY]
    o = O_F + KD * 512
    out = [ar.view(o + b * 512, 512) for b in range(EARLY)]; o += EARLY * 512
    s_w, s_mm, s_pe, s_out = (k.sem("rp_" + n) for n in ("w", "mm", "pe", "out"))
    gk = ar.view(o, HD); o += HD
    kk = ar.view(o, NT, HD); o += NT * HD
    ss, rs, sd, tmp = (ar.view(o + 16 * j, NT) for j in range(4)); o += 64
    tm = [ar.view(o + j * 96 * 8, 96 * 8) for j in range(4)]
    g_in, ch_s, v_out, kv_out = k.sem("rp_g"), k.sem("rp_ch"), k.sem("rp_v"), k.sem("rp_kv")
    s_ms, s_sd, s_rot, s_tr, s_ev = (k.sem("rp_" + n) for n in ("ms", "sd", "rot", "tr", "ev"))
    parts = ((P, 0, NT - 1), (NS, NT - 1, NT))

    def store(eng, sem, name, c0, w):
        a = t[name + "_prompt"]
        a = a.rearrange("a b (i p) h d -> p (a b i) (h d)", p=P) if len(a.shape) == 5 else a.rearrange("a b (i p) d -> p (a b i) d", p=P)
        eng.dma_start(a, z[:, 0:NT - 1, c0:c0 + w]).then_inc(sem, 16)
        a = t[name + "_sample"]
        a = a.rearrange("a b s h d -> (a b s) (h d)") if len(a.shape) == 5 else a.rearrange("a b s d -> (a b s) d")
        eng.dma_start(a, z[0:NS, NT - 1, c0:c0 + w]).then_inc(sem, 16)

    with nc.Block() as block:
        @block.sync
        def _(sp):
            sp.dma_start(gk, t["idx_k_g"].broadcast_to([P, HD])).then_inc(g_in, 16)
            sp.dma_start(wp, t["w_in"].rearrange("o (a p) n -> p (o a) n", p=P)[:, :, chunks[0][0]:chunks[0][0] + 512]).then_inc(s_w, 16)
            store(sp, v_out, "v", VC, HKV * HD)
            sp.wait_ge(s_rot, 1)
            store(sp, kv_out, "k", KC, HKV * HD)
            store(sp, kv_out, "kidx", KIC, HD)
            sp.dma_start(t["wi"], z[0:NS, NT - 1, WIC:WIC + IH]).then_inc(kv_out, 16)
            for n, g in enumerate(groups):
                sp.wait_ge(s_pe, n + 1)
                sp.dma_start(g[5], out[n][0:g[1], 0:g[2]]).then_inc(s_out, 16)
            sp.wait_ge(s_out, 16 * EARLY)
            sp.wait_ge(v_out, 32)
            sp.wait_ge(kv_out, 16 * 5)

        @block.vector
        def _(ve):
            ch = Chain(ve, ch_s)
            for n, a, b in parts:
                ch.step(ve.tensor_tensor(kk[0:n, a:b, :], z[0:n, a:b, KIC:KIC + HD], z[0:n, a:b, KIC:KIC + HD], ALU.mult))
                ch.step(ve.tensor_reduce(ss[0:n, a:b], kk[0:n, a:b, :], AX.X, ALU.add))
                ve.tensor_scalar(ss[0:n, a:b], ss[0:n, a:b], 1.0 / HD, EPS, ALU.mult, ALU.add).then_inc(s_ms, 1)
            for m, (n, a, b) in enumerate(parts):
                rstd_steps(ch, ve, lambda: ve.wait_ge(s_sd, m + 1), ss[0:n, a:b], rs[0:n, a:b], sd[0:n, a:b], tmp[0:n, a:b])
            ve.wait_ge(g_in, 16)
            for n, a, b in parts:
                zk = z[0:n, a:b, KIC:KIC + HD]
                ch.step(ve.tensor_tensor(zk, zk, rs[0:n, a:b].unsqueeze(2).broadcast_to([n, b - a, HD]), ALU.mult))
                ch.step(ve.tensor_tensor(zk, zk, gk[0:n, :].unsqueeze(1).broadcast_to([n, b - a, HD]), ALU.mult))
                zw = z[0:n, a:b, WIC:WIC + IH]
                ch.step(ve.tensor_scalar(zw, zw, float(IH * HD) ** -0.5, None, ALU.mult))
                for c0, nh in ((QC, H + HKV), (QIC, IH + 1)):
                    for i in range(a, b) if n == P else (a,):
                        zh = z[0:n, i, c0:c0 + nh * HD].rearrange("p (h d) -> p h d", d=HD)
                        x1, x2 = zh[:, :, 0:RH], zh[:, :, RH:ROT]
                        cos = k.rope[0:n, i, 0:1, :].broadcast_to([n, nh, RH])
                        sin = k.rope[0:n, i, 1:2, :].broadcast_to([n, nh, RH])
                        t1, t2, t3, t4 = (x[0:n, 0:nh * RH].rearrange("p (h d) -> p h d", d=RH) for x in tm)
                        ch.mark(ve.tensor_tensor(t1, x1, cos, ALU.mult))
                        ch.mark(ve.tensor_tensor(t2, x2, sin, ALU.mult))
                        ch.mark(ve.tensor_tensor(t3, x2, cos, ALU.mult))
                        ch.step(ve.tensor_tensor(t4, x1, sin, ALU.mult))
                        ch.mark(ve.tensor_tensor(x1, t1, t2, ALU.subtract))
                        ch.step(ve.tensor_tensor(x2, t3, t4, ALU.add))
            ve.sem_inc(s_rot, 1)
            for i in range(NT - 1):
                ve.wait_ge(s_tr, i + 1)
                b = 2 * (i % 2)
                ve.tensor_copy(kiT[:, i * P:(i + 1) * P], ps[0:HD, b, 0:P]).then_inc(s_ev, 1)

        @block.scalar
        def _(act):
            for m, (n, a, b) in enumerate(parts):
                act.wait_ge(s_ms, m + 1)
                act.activation(sd[0:n, a:b], ss[0:n, a:b], ACT.Sqrt).then_inc(s_sd, 1)
            for n, g in enumerate(groups):
                act.wait_ge(s_mm, n + 1)
                act.activation(out[n][0:g[1], 0:g[2]], ps[0:g[1], 4 + n % 4, 0:g[2]], ACT.Copy).then_inc(s_pe, 1)

        @block.tensor
        def _(pe):
            pe.wait_ge(s_w, 16)
            for n, (j, m, cols, lhs, rhs, dst) in enumerate(groups):
                if n >= 4:
                    pe.wait_ge(s_pe, n - 3)
                for a in range(KD):
                    ins = pe.matmul(ps[0:m, 4 + n % 4, 0:cols], lhs(a), rhs(a), start=(a == 0), stop=(a == KD - 1))
                ins.then_inc(s_mm, 1)
            pe.wait_ge(s_rot, 1)
            for i in range(NT - 1):
                b = 2 * (i % 2)
                if i >= 2:
                    pe.wait_ge(s_ev, i - 1)
                pe.transpose(ps[0:HD, b, 0:P], z[:, i, KIC:KIC + HD], k.ident).then_inc(s_tr, 1)


def index(k):
    nc, t, ar, ps = k.nc, k.t, k.ar, k.ps
    z, hT = ar.view(O_Z, NT, NA), ar.view(HT, KD, T)
    kiT = ar.view(O_KIT, SEQ, p=HD)
    o = O_F
    wp = [ar.view(o + b * KD * 512, KD, 512) for b in range(2)]; o += 2 * KD * 512
    stage = [ar.view(o + b * 512, 512) for b in range(4)]; o += 2048
    rl = [ar.view(o + b * SEQ, SEQ) for b in range(2)]; o += 2 * SEQ
    qiT = ar.view(o, IH, P, p=HD); o += IH * P
    wsel = ar.view(o, DB, NS, p=NS); o += DB * NS
    msel = ar.view(o, DB, NS, p=NS); o += DB * NS
    wiT = ar.view(o, DB, p=NS); o += 8
    raw, idx, idh = ar.view(o, DB, dt=I32), ar.view(k.o_idx, DB, dt=I32), ar.view(o + 8, 2, DB, dt=I32); o += 24
    NKI = 4
    KI = [ar.view(o + b * 512, 8, HD) for b in range(NKI)]; o += NKI * 512
    kis = [ar.view(o + b * 512, 512) for b in range(2)]; o += 1024
    rls = [ar.view(o + b * 512, 512, p=NS) for b in range(4)]; o += 2048
    qiS = ar.view(o, DB, IH * DS); o += DB * IH * DS
    kin = ar.view(o, NS, p=HD); o += NS
    top = [ar.view(o + 8 * j, 8) for j in range(2)]; o += 16
    one, spare = ar.view(o, 1), [ar.view(o + 1 + j, 1) for j in range(4)]; o += 16
    bias = [ar.view(o + b * 512, 512, p=1) for b in range(2)]; o += 1024
    assert o <= k.end, (o, k.end)
    accs = ar.view(O_ACCS, PAST + DS, p=NS)
    names = "tr ev mm rl acc diag pt idx wi ms wsel ch qd sq sqc kit kic smm srl fold done new nrl nfold top on pmm pev rlw pacc pdiag".split()
    s = {n: k.sem("ix_" + n) for n in names}
    s_ki, s_pw, s_st = [k.sem(f"ix_ki{b}") for b in range(NKI)], [k.sem(f"ix_pw{b}") for b in range(2)], [k.sem(f"ix_st{b}") for b in range(4)]
    nmm = IH * (NT - 1)
    FIRST = 4
    PB = (6, 7, 0, 1)

    w_v, chunks, groups = recurrence_groups(k, wp)
    groups = groups[EARLY:]
    ada = modulation_chunks(t)[ADA1:ADA2]
    sources = [w_v[:, :, c[0]:c[0] + 512] for c in chunks] + [w[:, :, n * 512:(n + 1) * 512] for w, b, n in ada]
    for n in range(len(ada)):
        j = len(chunks) + n
        groups.append((j, NC, 512, (lambda a: k.cT[:, a, :]), (lambda a, j=j: wp[j % 2][:, a, :]), t["mod"][:, (ADA1 + n) * 512:(ADA1 + n + 1) * 512]))
    last = {g[0]: n for n, g in enumerate(groups)}

    def weighed(n):
        if n < IH * FIRST:
            return s["acc"], n + 1
        u, h = divmod(n - IH * FIRST, IH)
        return (s["rlw"], n - IH * FIRST + 1) if h == 0 else (s["pacc"], (IH - 1) * u + h)

    def tile(i):
        return ar.view(ACC_AT[i], P * (i + 1))

    def head_weight(i, h):
        return z[:, i, WIC + h:WIC + h + 1]

    def diagonal(eng, i, sem):
        eng.wait_ge(*weighed(IH * i + IH - 1))
        dg = tile(i)[:, i * P:(i + 1) * P]
        eng.tensor_tensor(dg, dg, k.cb, ALU.add).then_inc(sem, 1)

    s_pb = [k.sem(f"ix_pb{b}") for b in range(2)]

    with nc.Block() as block:
        @block.sync
        def _(sp):
            with nc.allow_non_contiguous_dma(reason="a few hundred values"):
                for b in range(DB):
                    sp.dma_start(raw[:, b:b + 1], t["page_table"][b, :].rearrange("(g o) -> g o", o=1).unsqueeze(1).broadcast_to([16, 8, 1])).then_inc(s["pt"], 16)
                    sp.dma_start(wiT[:, b:b + 1], t["wi"][b * DS:(b + 1) * DS, :].rearrange("q (h o) -> h q o", o=1)).then_inc(s["wi"], 16)
            sp.dma_start(msel.rearrange("p a b -> p (a b)"), t["k_msel"]).then_inc(s["ms"], 16)
            sp.wait_ge(s["sqc"], 2)
            sp.dma_start(qiS[HD:P, :, :], qiS[0:HD, :, :]).then_inc(s["qd"], 16)

            def load(j):
                sp.dma_start(wp[j % 2], sources[j]).then_inc(s_pw[j % 2], 16)
                if j >= len(chunks):
                    w, b, n = ada[j - len(chunks)]
                    sp.dma_start(bias[j % 2], b[:, n * 512:(n + 1) * 512]).then_inc(s_pb[j % 2], 16)

            load(1)
            sp.wait_ge(s["qd"], 16)
            for n, g in enumerate(groups):
                if n - 1 == last.get(g[0] - 1) and g[0] + 1 < len(sources):
                    sp.wait_ge(s["pmm"], n)
                    load(g[0] + 1)
                sp.wait_ge(s["pev"], n + 1)
                sp.dma_start(g[5], stage[n % 4][0:g[1], 0:g[2]]).then_inc(s_st[n % 4], 16)
            for b in range(4):
                sp.wait_ge(s_st[b], 16 * ((len(groups) + 3 - b) // 4))

        @block.gpsimd
        def _(po):
            po.wait_ge(s["idx"], 1)
            rows = t["cache_kidx"].rearrange("o n (a b) d -> (o n a) (b d)", b=8)
            for m in range(2 * DB):
                half, b = divmod(m, DB)
                if m == NKI:
                    for i in range(FIRST, NT - 1):
                        for h in range(1, IH):
                            n = IH * i + h
                            po.wait_ge(s["rlw"], n - IH * FIRST + 1)
                            po.wait_ge(*weighed(n - 1))
                            po.tensor_tensor(tile(i), tile(i), rl[n % 2][:, 0:P * (i + 1)], ALU.add).then_inc(s["pacc"], 1)
                        diagonal(po, i, s["pdiag"])
                if m >= NKI:
                    po.wait_ge(s["kit"], m - NKI + 1)
                po.indirect_dma_start(KI[m % NKI].rearrange("p a d -> p (a d)"), None, rows,
                                      bass.IndirectOffsetOnAxis(ap=idh[:, half, b:b + 1], axis=0)).then_inc(s_ki[m % NKI], 16)

        @block.tensor
        def _(pe):
            def prompt(i):
                for g in range(2):
                    if i >= 1:
                        pe.wait_ge(s["ev"], 2 * (i - 1) + g + 1)
                    for h in range(4):
                        hh = 4 * g + h
                        ins = pe.transpose(ps[0:HD, 4 + g, h * P:(h + 1) * P], z[:, i, QIC + hh * HD:QIC + (hh + 1) * HD], k.ident)
                    ins.then_inc(s["tr"], 1)
                N = P * (i + 1)
                for h in range(IH):
                    n = IH * i + h
                    if h % 4 == 0:
                        pe.wait_ge(s["ev"], 2 * i + h // 4 + 1)
                    if n >= 2:
                        pe.wait_ge(s["rl"], n - 1)
                    b = 2 * (n % 2)
                    for c in range(0, N, 512):
                        w = min(512, N - c)
                        ins = pe.matmul(ps[:, b + c // 512, 0:w], qiT[:, h, :], kiT[:, c:c + w], start=True, stop=True)
                    ins.then_inc(s["mm"], 1)

            def fold(m, par):
                pe.wait_ge(s["srl"], 2 * m + par + 1)
                pe.matmul(ps[0:NS, 6 + par, :], wsel[:, m % DB, :], rls[(2 * m + par) % 4], start=(m % DB == 0), stop=(m % DB == DB - 1)).then_inc(s["fold"], 1)

            def sample(half):
                for n in range(DB * half, DB * half + DB):
                    b = n % DB
                    pe.wait_ge(s_ki[n % NKI], 16 * (n // NKI + 1))
                    if n >= 2:
                        pe.wait_ge(s["kic"], n - 1)
                    for jj in range(4):
                        ins = pe.transpose(ps[:, n % 2, jj * P:(jj + 1) * P], KI[n % NKI][:, 2 * jj:2 * jj + 2, :].rearrange("p a d -> p (a d)"), k.ident)
                    ins.then_inc(s["kit"], 1)
                    pe.wait_ge(s["kic"], n + 1)
                    for par in range(2):
                        if n >= 2:
                            pe.wait_ge(s["srl"], 2 * (n - 2) + par + 1)
                        rs = slice(par * HD, (par + 1) * HD)
                        pe.matmul(ps[0:NS, 2 + 2 * (n % 2) + par, :], qiS[rs, b, :], kis[n % 2][rs, :], start=True, stop=True).then_inc(s["smm"], 1)
                    if half == 1 and b == 1:
                        pe.wait_ge(s["done"], 2)
                    if b >= 1:
                        fold(n - 1, 0)
                        fold(n - 1, 1)
                fold(DB * half + DB - 1, 0)
                fold(DB * half + DB - 1, 1)
                pe.wait_ge(s["srl"], 2 * DB * (half + 1))

            for g in range(2):
                for h in range(4):
                    hh = 4 * g + h
                    ins = pe.transpose(ps[0:HD, 6 + g, h * NS:(h + 1) * NS],
                                       z[0:NS, NT - 1, QIC + hh * HD:QIC + (hh + 1) * HD], k.ident[0:NS, 0:NS])
                ins.then_inc(s["sq"], 1)
            for i in range(NT - 1):
                prompt(i)
            pe.wait_ge(s["qd"], 16)
            pe.wait_ge(s["wsel"], 1)
            pe.wait_ge(s["rl"], nmm)
            sample(0)
            sample(1)
            pe.transpose(ps[0:HD, 0, 0:NS], z[0:NS, NT - 1, KIC:KIC + HD], k.ident[0:NS, 0:NS]).then_inc(s["new"], 1)
            pe.wait_ge(s["nrl"], 1)
            for b in range(DB):
                ins = pe.matmul(ps[0:NS, 2, b * DS:(b + 1) * DS], qiS[0:HD, b, :], kin[:, b * DS:(b + 1) * DS], start=True, stop=True)
            ins.then_inc(s["new"], 1)
            pe.wait_ge(s["nrl"], 2)
            for b in range(DB):
                ins = pe.matmul(ps[0:NS, 4, 0:DS], wsel[:, b, :], rls[0][:, b * DS:(b + 1) * DS], start=(b == 0), stop=(b == DB - 1))
            ins.then_inc(s["nfold"], 1)
            for n, (j, m, cols, lhs, rhs, dst) in enumerate(groups):
                if n == 0:
                    pe.wait_ge(s["done"], 4)
                if j and groups[n - 1][0] != j:
                    pe.wait_ge(s_pw[j % 2], 16 * ((j + 1) // 2))
                if n >= 4:
                    pe.wait_ge(s["pev"], n - 3)
                for a in range(KD):
                    ins = pe.matmul(ps[0:m, PB[n % 4], 0:cols], lhs(a), rhs(a), start=(a == 0), stop=(a == KD - 1 and j < len(chunks)))
                if j >= len(chunks):
                    pe.wait_ge(s_pb[j % 2], 16 * ((j - len(chunks)) // 2 + 1))
                    ins = pe.matmul(ps[0:m, PB[n % 4], 0:cols], k.ones, bias[j % 2], start=False, stop=True)
                ins.then_inc(s["pmm"], 1)

        @block.scalar
        def _(act):
            def prompt(i):
                if i >= 1:
                    act.wait_ge(s["mm"], IH * i)
                for g in range(2):
                    act.wait_ge(s["tr"], 2 * i + g + 1)
                    act.activation(qiT[:, 4 * g:4 * g + 4, :].rearrange("p a b -> p (a b)"), ps[0:HD, 4 + g, :], ACT.Copy).then_inc(s["ev"], 1)
                N = P * (i + 1)
                for h in range(IH):
                    n = IH * i + h
                    act.wait_ge(s["mm"], n + 1)
                    if n >= 2:
                        act.wait_ge(*weighed(n - 2))
                    b = 2 * (n % 2)
                    act.activation(rl[n % 2][:, 0:N], ps[:, b:b + 2, :].rearrange("p a b -> p (a b)")[:, 0:N], ACT.Relu).then_inc(s["rl"], 1)
                    if i >= FIRST:
                        act.wait_ge(s["rl"], n + 1)
                        act.activation(tile(i) if h == 0 else rl[n % 2][:, 0:N], rl[n % 2][:, 0:N], ACT.Copy, scale=head_weight(i, h)).then_inc(s["rlw"], 1)

            def sample(half):
                for n in range(DB * half, DB * half + DB):
                    act.wait_ge(s["kit"], n + 1)
                    if n >= 2:
                        act.wait_ge(s["smm"], 2 * (n - 1))
                    act.activation(kis[n % 2], ps[:, n % 2, :], ACT.Copy).then_inc(s["kic"], 1)
                    for par in range(2):
                        act.wait_ge(s["smm"], 2 * n + par + 1)
                        if n >= 2:
                            act.wait_ge(s["fold"], 2 * (n - 2) + par + 1)
                        act.activation(rls[(2 * n + par) % 4], ps[0:NS, 2 + 2 * (n % 2) + par, :], ACT.Relu).then_inc(s["srl"], 1)
                for par in range(2):
                    act.wait_ge(s["fold"], 2 * DB * (half + 1) - 1 + par)
                    act.activation(grid[:, 8 * half + par:8 * half + 8:2, :], ps[0:NS, 6 + par, :].rearrange("q (j p) -> q j p", p=P), ACT.Copy).then_inc(s["done"], 1)

            grid = accs[:, 0:PAST].rearrange("q (p j) -> q j p", j=16)
            for g in range(2):
                act.wait_ge(s["sq"], g + 1)
                dst = qiS[0:HD, :, 4 * g * DS:4 * (g + 1) * DS].rearrange("p s (h q) -> p h s q", q=DS)
                for h in range(4):
                    ins = act.activation(dst[:, h, :, :], ps[0:HD, 6 + g, h * NS:(h + 1) * NS].rearrange("p (s q) -> p s q", q=DS), ACT.Copy)
                ins.then_inc(s["sqc"], 1)
            for i in range(NT - 1):
                prompt(i)
            sample(0)
            sample(1)
            act.wait_ge(s["new"], 1)
            act.activation(kin, ps[0:HD, 0, 0:NS], ACT.Copy).then_inc(s["nrl"], 1)
            act.wait_ge(s["new"], 2)
            act.wait_ge(s["fold"], 4 * DB)
            act.activation(rls[0][:, 0:NS], ps[0:NS, 2, 0:NS], ACT.Relu).then_inc(s["nrl"], 1)
            act.wait_ge(s["nfold"], 1)
            act.activation(rls[1][:, 0:DS], ps[0:NS, 4, 0:DS], ACT.Copy).then_inc(s["done"], 1)
            for n, (j, m, cols, lhs, rhs, dst) in enumerate(groups):
                act.wait_ge(s["pmm"], n + 1)
                if n >= 4:
                    act.wait_ge(s_st[n % 4], 16 * (n // 4))
                act.activation(stage[n % 4][0:m, 0:cols], ps[0:m, PB[n % 4], 0:cols], ACT.Copy).then_inc(s["pev"], 1)

        @block.vector
        def _(ve):
            ch = Chain(ve, s["ch"])
            ve.memset(one, 1.0).then_inc(s["on"], 1)
            ve.wait_ge(s["on"], 1)

            taken = 0

            def select(*accs_):
                nonlocal taken
                m, turns = len(accs_), 4
                rounds = TOPK // 8 // turns
                with ve.Fori(0, rounds) as j:
                    base = taken + 2 * m * turns * j
                    for v in range(turns):
                        for u, acc in enumerate(accs_):
                            if v:
                                ve.wait_ge(s["top"], base + 2 * m * v - m + u + 1)
                                ve.tensor_copy(spare[2 + u], one)
                            ve.max(top[u][0:acc.shape[0], :], acc).then_inc(s["top"], 1)
                        for u, acc in enumerate(accs_):
                            ve.wait_ge(s["top"], base + 2 * m * v + u + 1)
                            ve.tensor_copy(spare[u], one)
                            ve.match_replace(acc, top[u][0:acc.shape[0], :], acc, TAKEN).then_inc(s["top"], 1)
                    ve.wait_ge(s["top"], base + 2 * m * turns)
                taken += 2 * m * turns * rounds
                for acc in accs_:
                    ve.tensor_scalar(acc, acc, TAKEN, OFF, ALU.not_equal, ALU.mult)


            def sample_operands():
                ve.wait_ge(s["pt"], 16 * DB)
                gather_index(ve, ch, k, raw, idx)
                for half in range(2):
                    ch.step(ve.tensor_scalar(idh[:, half, :], idx, 2.0, float(half), ALU.mult, ALU.add))
                ve.sem_inc(s["idx"], 1)
                ve.wait_ge(s["wi"], 16 * DB)
                ve.wait_ge(s["ms"], 16)
                ve.tensor_tensor(wsel, msel, wiT.unsqueeze(2).broadcast_to([NS, DB, NS]), ALU.mult).then_inc(s["wsel"], 1)

            for i in range(FIRST):
                if i == 1:
                    sample_operands()
                for h in range(IH):
                    n = IH * i + h
                    x = rl[n % 2][:, 0:P * (i + 1)]
                    ve.wait_ge(s["rl"], n + 1)
                    if h == 0:
                        ve.tensor_scalar(tile(i), x, head_weight(i, h), None, ALU.mult).then_inc(s["acc"], 1)
                    else:
                        ve.wait_ge(*weighed(n - 1))
                        ve.scalar_tensor_tensor(tile(i), x, head_weight(i, h), tile(i), ALU.mult, ALU.add).then_inc(s["acc"], 1)
                diagonal(ve, i, s["diag"])
                ve.wait_ge(s["diag"], i + 1)
                if P * (i + 1) <= TOPK:
                    ve.tensor_scalar(tile(i), tile(i), 0.5 * NEG, OFF, ALU.is_lt, ALU.mult)
            select(tile(2), tile(3))
            ve.wait_ge(s["pdiag"], 2)
            select(tile(4), tile(5))
            ve.wait_ge(s["pdiag"], 4)
            select(tile(6), tile(7))
            ve.wait_ge(s["done"], 5)
            ch.step(ve.tensor_tensor(accs[:, PAST:PAST + DS], rls[1][:, 0:DS], k.small[0:NS, 0:DS], ALU.add))
            select(accs)


O_K0 = 40272
O_V0 = O_K0 + 16 * HKV * HD


def gather_past(po, k, dst, name, b, sem):
    rows = k.t[name].rearrange("o n (a b) h d -> (o n a) (b h d)", b=16)
    idx = k.ar.view(k.o_idx, DB, dt=I32)
    po.indirect_dma_start(dst.rearrange("p a d -> p (a d)"), None, rows, bass.IndirectOffsetOnAxis(ap=idx[:, b:b + 1], axis=0)).then_inc(sem, 16)


def prompt_attention(k):
    nc, t, ar, ps = k.nc, k.t, k.ar, k.ps
    z = ar.view(O_Z, NT, NA)
    kT, A = ar.view(O_KT, HKV, SEQ, p=HD), ar.view(O_A, NT, 512)
    o = O_F
    qT = [ar.view(o + b * H * P, H, P, p=HD) for b in range(2)]; o += 2 * H * P
    L = [ar.view(o + b * SEQ, SEQ) for b in range(2)]; o += 2 * SEQ
    E = [ar.view(o + b * SEQ, SEQ) for b in range(2)]; o += 2 * SEQ
    PT = [ar.view(o + b * 512, 4, P) for b in range(4)]; o += 2048
    nmx, den, rden = (ar.view(o + 64 * j, H * (NT - 1)) for j in range(3)); o += 192
    ada = modulation_chunks(t)[ADA2:ADA3]
    wb, bias = ar.view(o, 512), ar.view(o + 512, 512, p=1); o += 1024
    assert o <= O_K0
    wa = ar.view(O_V0 + 16 * HKV * HD, KD - 1, 512)
    row = A[0:NC, NT - 1, :]
    ADA_EVERY = 10
    assert ADA_EVERY * (len(ada) - 1) + KD + 2 < 4 * H
    names = "past aw ap ae ao ks kc tr ev mm l mx e pt ptc pv rd o".split()
    s = {n: k.sem("at_" + n) for n in names}
    chunks = [(i, h, c) for i in range(NT - 1) for h in range(H) for c in range(0, i + 1, 4)]
    first = {}
    for m, (i, h, c) in enumerate(chunks):
        first.setdefault((i, h), m)

    with nc.Block() as block:
        @block.sync
        def _(sp):
            for q, (w, b, n) in enumerate(ada):
                if q:
                    sp.wait_ge(s["ap"], q)
                cs = slice(n * 512, (n + 1) * 512)
                sp.dma_start(wa, w[:, 0:KD - 1, cs]).then_inc(s["aw"], 16)
                sp.dma_start(wb, w[:, KD - 1, cs]).then_inc(s["aw"], 16)
                sp.dma_start(bias, b[:, cs]).then_inc(s["aw"], 16)
                sp.wait_ge(s["ae"], q + 1)
                sp.dma_start(t["mod"][:, (ADA2 + q) * 512:(ADA2 + q + 1) * 512], row).then_inc(s["ao"], 16)
            sp.wait_ge(s["ao"], 16 * len(ada))

        @block.gpsimd
        def _(po):
            for at, name in ((O_K0, "cache_k"), (O_V0, "cache_v")):
                gather_past(po, k, ar.view(at, 16, HKV * HD), name, 0, s["past"])
            po.wait_ge(s["past"], 32)

        @block.tensor
        def _(pe):
            def queries(i):
                if i >= 2:
                    pe.wait_ge(s["o"], i - 1)
                for g in range(2):
                    if g == 1:
                        pe.wait_ge(s["ev"], 2 * i + 1)
                    for h in range(4):
                        hh = 4 * g + h
                        ins = pe.transpose(ps[0:HD, 6 + i % 2, h * P:(h + 1) * P], z[:, i, QC + hh * HD:QC + (hh + 1) * HD], k.ident)
                    ins.then_inc(s["tr"], 1)

            def logits(i, h):
                n = H * i + h
                if h % 4 == 0:
                    pe.wait_ge(s["ev"], 2 * i + h // 4 + 1)
                if n >= 2:
                    pe.wait_ge(s["l"], n - 1)
                b, N = 2 * (n % 2), P * (i + 1)
                for c in range(0, N, 512):
                    w = min(512, N - c)
                    ins = pe.matmul(ps[:, b + c // 512, 0:w], qT[i % 2][:, h, :], kT[:, h // 2, c:c + w], start=True, stop=True)
                ins.then_inc(s["mm"], 1)

            def turn(i, h):
                n = H * i + h
                m = first[i, h]
                pe.wait_ge(s["e"], n + 1)
                for c in range(0, i + 1, 4):
                    if m >= 2:
                        pe.wait_ge(s["ptc"], m - 1)
                    for u in range(min(4, i + 1 - c)):
                        ins = pe.transpose(ps[:, 4 + m % 2, u * P:(u + 1) * P], E[n % 2][:, (c + u) * P:(c + u + 1) * P], k.ident)
                    ins.then_inc(s["pt"], 1)
                    m += 1

            def weigh(i, h):
                m = first[i, h]
                if h == 0:
                    pe.wait_ge(s["ev"], 2 * i + 2)
                for c in range(0, i + 1, 4):
                    pe.wait_ge(s["ptc"], m + 1)
                    for u in range(min(4, i + 1 - c)):
                        ins = pe.matmul(ps[:, 6 + i % 2, h * HD:(h + 1) * HD], PT[m % 4][:, u, :], z[:, c + u, VC + (h // 2) * HD:VC + (h // 2 + 1) * HD],
                                        start=(c + u == 0), stop=(c + u == i))
                    m += 1
                ins.then_inc(s["pv"], 1)

            for i in range(NT - 1):
                if i >= 4:
                    pe.wait_ge(s["kc"], i - 3)
                for h in range(HKV):
                    ins = pe.transpose(ps[0:HD, i % 4, h * P:(h + 1) * P], z[:, i, KC + h * HD:KC + (h + 1) * HD], k.ident)
                ins.then_inc(s["ks"], 1)
            queries(0)
            pe.wait_ge(s["kc"], NT - 1)
            for n in range(H * (NT - 1) + 2):
                i, h = divmod(n, H)
                if n >= 2:
                    turn(*divmod(n - 2, H))
                chunk, u = divmod(n - 2, ADA_EVERY)
                if n >= 2 and chunk < len(ada) and u < KD:
                    if u == 0:
                        pe.wait_ge(s["aw"], 48 * (chunk + 1))
                        if chunk:
                            pe.wait_ge(s["ae"], chunk)
                    pe.matmul(ps[0:NC, 1, :], k.cT[:, u, :], wa[:, u, :] if u < KD - 1 else wb, start=(u == 0), stop=False)
                    if u == KD - 1:
                        pe.matmul(ps[0:NC, 1, :], k.ones, bias, start=False, stop=True).then_inc(s["ap"], 1)
                if n == 4 * H:
                    pe.wait_ge(s["ae"], len(ada))
                if n < H * (NT - 1):
                    logits(i, h)
                    if h == 4 and i + 1 < NT - 1:
                        queries(i + 1)
                if n >= 2:
                    weigh(*divmod(n - 2, H))

        @block.vector
        def _(ve):
            def mask(i, h):
                n, N = H * i + h, P * (i + 1)
                b = 2 * (n % 2)
                ve.wait_ge(s["mm"], n + 1)
                if n >= 2:
                    ve.wait_ge(s["e"], n - 1)
                ve.scalar_tensor_tensor(L[n % 2][:, 0:N], ps[:, b:b + 2, :].rearrange("p a b -> p (a b)")[:, 0:N], float(HD) ** -0.5,
                                        ar.view(ACC_AT[i], N), ALU.mult, ALU.add).then_inc(s["l"], 1)
                ve.wait_ge(s["l"], n + 1)
                ve.tensor_reduce(nmx[:, n:n + 1], L[n % 2][:, 0:N], AX.X, ALU.max, negate=True).then_inc(s["mx"], 1)

            def out(i):
                n = slice(H * i, H * i + H)
                ve.wait_ge(s["e"], n.stop)
                ve.reciprocal(rden[:, n], den[:, n]).then_inc(s["rd"], 1)
                ve.wait_ge(s["rd"], i + 1)
                ve.wait_ge(s["pv"], n.stop)
                ve.tensor_tensor(A[:, i, :].rearrange("p (h d) -> p h d", d=HD), ps[:, 6 + i % 2, :].rearrange("p (h d) -> p h d", d=HD),
                                 rden[:, n].unsqueeze(2).broadcast_to([P, H, HD]), ALU.mult).then_inc(s["o"], 1)

            for i in range(NT - 1):
                ve.wait_ge(s["ks"], i + 1)
                ve.tensor_copy(kT[:, :, i * P:(i + 1) * P], ps[0:HD, i % 4, :].rearrange("p (h n) -> p h n", n=P)).then_inc(s["kc"], 1)
            for n in range(H * (NT - 1) + 3):
                if n < H * (NT - 1):
                    mask(*divmod(n, H))
                if n >= H and n % H == 2:
                    out(n // H - 1)

        @block.scalar
        def _(act):
            def queries(i):
                for g in range(2):
                    if i >= 2 and g == 0:
                        act.wait_ge(s["mm"], H * (i - 1))
                    act.wait_ge(s["tr"], 2 * i + g + 1)
                    act.activation(qT[i % 2][:, 4 * g:4 * g + 4, :].rearrange("p a b -> p (a b)"), ps[0:HD, 6 + i % 2, :], ACT.Copy).then_inc(s["ev"], 1)

            queries(0)
            for n in range(H * (NT - 1) + 2):
                i, h = divmod(n, H)
                if h == 4 and i + 1 < NT - 1:
                    queries(i + 1)
                chunk, u = divmod(n - 3, ADA_EVERY)
                if n >= 3 and chunk < len(ada) and u == KD - 1:
                    act.wait_ge(s["ap"], chunk + 1)
                    if chunk:
                        act.wait_ge(s["ao"], 16 * chunk)
                    act.activation(row, ps[0:NC, 1, :], ACT.Copy).then_inc(s["ae"], 1)
                if 1 <= n <= H * (NT - 1):
                    N, m = P * ((n - 1) // H + 1), n - 1
                    act.wait_ge(s["mx"], m + 1)
                    if m >= 2:
                        act.wait_ge(s["pt"], first[divmod(m - 1, H)])
                    act.activation(E[m % 2][:, 0:N], L[m % 2][:, 0:N], ACT.Exp, bias=nmx[:, m:m + 1], accum_out=den[:, m:m + 1]).then_inc(s["e"], 1)
                if n >= 2:
                    i, h = divmod(n - 2, H)
                    m = first[i, h]
                    for c in range(0, i + 1, 4):
                        act.wait_ge(s["pt"], m + 1)
                        if m >= 4:
                            ii, hh, _ = chunks[m - 4]
                            act.wait_ge(s["pv"], H * ii + hh + 1)
                        w = P * min(4, i + 1 - c)
                        act.activation(PT[m % 4].rearrange("p a b -> p (a b)")[:, 0:w], ps[:, 4 + m % 2, 0:w], ACT.Copy).then_inc(s["ptc"], 1)
                        m += 1


def sample_attention(k):
    nc, t, ar, ps = k.nc, k.t, k.ar, k.ps
    z, A = ar.view(O_Z, NT, NA), ar.view(O_A, NT, 512)
    mb = ar.view(O_ACCS, PAST + DS, p=NS)
    NL = PAST + NS
    Kc = [ar.view(a, 16, HKV * HD) for a in (O_K0, O_KT)]
    Vc = [ar.view(a, 16, HKV * HD) for a in (O_V0, O_ACC)]
    o = O_F
    L = [ar.view(o + b * NL, NL) for b in range(2)]; o += 2 * NL
    QB = ar.view(o, DB, 2, NS); o += 2 * DB * NS
    mbn = ar.view(o, DB, DS, p=NS); o += NS
    kTn = ar.view(o, 2, NS); o += 2 * NS
    idx = ar.view(k.o_idx, DB, dt=I32)
    nmx, den, rden = (ar.view(o + 4 * j, 4) for j in range(3)); o += 12
    kT = [ar.view(o + b * 1024, 2, 512) for b in range(2)]; o += 2048
    PT = [ar.view(o + b * 512, 512) for b in range(2)]; o += 1024
    qr = ar.view(o - 512, 2, 2, P, p=NS)
    rsel = ar.view(o, DB, NS, p=NS); o += DB * NS
    ob = ar.view(o, 256); o += 256
    assert o <= O_K0, (o, O_K0)
    names = "qr kc0 kc1 vc0 vc1 rs ch qt qc kn knc zero mbn kt ktc mm lc mx e ptt ptc pv rd ob out0 in".split()
    s = {n: k.sem("sa_" + n) for n in names}
    NCK = 5

    with nc.Block() as block:
        @block.sync
        def _(sp):
            sp.dma_start(rsel.rearrange("p a b -> p (a b)"), t["k_rsel"]).then_inc(s["rs"], 16)
            for pr in range(DB // 2):
                sp.wait_ge(s["ob"], pr + 1)
                for j in range(2):
                    for g in range(HKV):
                        dst = t["att"][(2 * pr + j) * DS:(2 * pr + j + 1) * DS, g * 2 * HD:(g + 1) * 2 * HD].rearrange("q (g d) -> g q d", d=HD)
                        sp.dma_start(dst, ob[j * HD + 16 * g:j * HD + 16 * g + 16, g * HD:(g + 1) * HD]).then_inc(s["out0"], 16)
            sp.wait_ge(s["out0"], 16 * DB * HKV)
            sp.dma_start(A[0:NS, NT - 1, :], t["att"]).then_inc(s["in"], 16)
            sp.wait_ge(s["in"], 16)

        @block.gpsimd
        def _(po):
            for b in range(1, DB):
                if b >= 2:
                    po.wait_ge(s["kt"], 4 * (b - 1))
                gather_past(po, k, Kc[b % 2], "cache_k", b, s[f"kc{b % 2}"])
                if b >= 2:
                    po.wait_ge(s["pv"], b - 1)
                gather_past(po, k, Vc[b % 2], "cache_v", b, s[f"vc{b % 2}"])

        @block.tensor
        def _(pe):
            pe.wait_ge(s["qr"], 2)
            for pp in range(2):
                for g in range(2):
                    ins = pe.transpose(ps[:, 6, (2 * pp + g) * NS:(2 * pp + g + 1) * NS], qr[:, pp, g, :], k.ident[0:NS, 0:NS])
            ins.then_inc(s["qt"], 1)
            for pp in range(2):
                ins = pe.transpose(ps[:, 7, pp * NS:(pp + 1) * NS], z[0:NS, NT - 1, KC + pp * P:KC + (pp + 1) * P], k.ident[0:NS, 0:NS])
            ins.then_inc(s["kn"], 1)
            pe.wait_ge(s["qc"], 8)
            pe.wait_ge(s["knc"], 1)
            pe.wait_ge(s["mbn"], 1)
            pe.wait_ge(s["rs"], 16)
            grid = mb[:, 0:PAST].rearrange("q (p j) -> q j p", j=16)

            def keys(b, c):
                m = 4 * b + c
                if c == 0 and b >= 1:
                    pe.wait_ge(s[f"kc{b % 2}"], 16 * ((b + 1) // 2))
                if m >= 2:
                    pe.wait_ge(s["ktc"], m - 1)
                for pp in range(2):
                    for u in range(4):
                        ins = pe.transpose(ps[:, 2 * (m % 2) + pp, u * P:(u + 1) * P], Kc[b % 2][:, 4 * c + u, pp * P:(pp + 1) * P], k.ident)
                ins.then_inc(s["kt"], 1)

            def logits(b, c):
                m = NCK * b + c
                if m >= 2:
                    pe.wait_ge(s["lc"], m - 1)
                rs = slice(HD * (b % 2), HD * (b % 2) + HD)
                if c < 4:
                    pe.wait_ge(s["ktc"], 4 * b + c + 1)
                    out = ps[rs, 4 + m % 2, :]
                    for pp in range(2):
                        pe.matmul(out, QB[:, b, pp, :], kT[(4 * b + c) % 2][:, pp, :], start=(pp == 0), stop=False)
                    ins = pe.matmul(out, rsel[:, b, :], grid[:, 4 * c:4 * c + 4, :], start=False, stop=True)
                else:
                    out = ps[rs, 4 + m % 2, 0:NS]
                    for pp in range(2):
                        pe.matmul(out, QB[:, b, pp, :], kTn[:, pp, :], start=(pp == 0), stop=False)
                    ins = pe.matmul(out, rsel[:, b, :], mbn.rearrange("q a b -> q (a b)"), start=False, stop=True)
                ins.then_inc(s["mm"], 1)

            def weigh(pr):
                pe.wait_ge(s["e"], pr + 1)
                if pr >= 1:
                    pe.wait_ge(s["ob"], pr)

                def turn(c):
                    m, w = NCK * pr + c, (P if c < 4 else NS)
                    if m >= 2:
                        pe.wait_ge(s["ptc"], m - 1)
                    for u in range(4 if c < 4 else 1):
                        at = c * 512 + u * P
                        ins = pe.transpose(ps[0:w, 6 - c % 2, u * P:(u + 1) * P], L[pr % 2][:, at:at + w], k.ident)
                    ins.then_inc(s["ptt"], 1)

                turn(0)
                for c in range(NCK):
                    m = NCK * pr + c
                    if c + 1 < NCK:
                        turn(c + 1)
                    pe.wait_ge(s["ptc"], m + 1)
                    for j in range(2):
                        b = 2 * pr + j
                        if c == 0 and b >= 1:
                            pe.wait_ge(s[f"vc{j}"], 16 * ((b + 1) // 2))
                        rs = slice(HD * j, HD * j + HD)
                        for u in range(4 if c < 4 else 1):
                            if c < 4:
                                ins = pe.matmul(ps[rs, 7, 0:256], PT[m % 2][:, u * P + j * HD:u * P + (j + 1) * HD], Vc[j][:, 4 * c + u, :],
                                                start=(c == 0 and u == 0), stop=False)
                            else:
                                ins = pe.matmul(ps[rs, 7, 0:256], PT[m % 2][0:NS, j * HD:(j + 1) * HD], z[0:NS, NT - 1, VC:VC + 256],
                                                start=False, stop=True)
                                ins.then_inc(s["pv"], 1)

            keys(0, 0)
            keys(0, 1)
            for b in range(DB):
                for c in range(NCK):
                    if c >= 1 and c + 1 < 4:
                        keys(b, c + 1)
                    elif c >= 3 and b % 2 == 0:
                        keys(b + 1, c - 3)
                    logits(b, c)
                if b % 2 == 1:
                    if b + 1 < DB:
                        keys(b + 1, 0)
                        keys(b + 1, 1)
                    weigh(b // 2)

        @block.vector
        def _(ve):
            ch = Chain(ve, s["ch"])
            for pp in range(2):
                ve.tensor_copy(qr[:, pp, :, :].rearrange("p g (c d) -> p g c d", d=HD), z[0:NS, NT - 1, QC + 4 * pp * HD:QC + (4 * pp + 4) * HD]
                               .rearrange("p (c g d) -> p g c d", g=2, d=HD)).then_inc(s["qr"], 1)
            ve.memset(QB, 0.0).then_inc(s["zero"], 1)
            ch.step(ve.tensor_scalar(mbn, k.small[0:NS, 10:18].unsqueeze(2).broadcast_to([NS, DB, DS]), -OFF, OFF, ALU.mult, ALU.add))
            ve.tensor_tensor(mbn, mbn, mb[:, PAST:PAST + DS].unsqueeze(1).broadcast_to([NS, DB, DS]), ALU.add).then_inc(s["mbn"], 1)
            ve.wait_ge(s["kn"], 1)
            ve.tensor_copy(kTn.rearrange("p a b -> p (a b)"), ps[:, 7, 0:2 * NS]).then_inc(s["knc"], 1)
            ve.wait_ge(s["zero"], 1)
            ve.wait_ge(s["qt"], 1)
            for pp in range(2):
                for g in range(2):
                    for par in range(2):
                        rs = slice(par * HD, (par + 1) * HD)
                        row = ((2 * pp + par) * 2 + g) * DS
                        ve.tensor_scalar(QB[rs, :, pp, row:row + DS], ps[rs, 6, (2 * pp + g) * NS:(2 * pp + g + 1) * NS].rearrange("p (s q) -> p s q", q=DS),
                                         float(HD) ** -0.5, None, ALU.mult).then_inc(s["qc"], 1)

            def copy_keys(m):
                ve.wait_ge(s["kt"], m + 1)
                if m >= 2:
                    b, c = divmod(m - 2, 4)
                    ve.wait_ge(s["mm"], NCK * b + c + 1)
                ve.tensor_copy(kT[m % 2].rearrange("p a b -> p (a b)"), ps[:, 2 * (m % 2):2 * (m % 2) + 2, :].rearrange("p a b -> p (a b)")).then_inc(s["ktc"], 1)

            for pr in range(DB // 2):
                for m in range(8 * pr, 8 * pr + 8):
                    copy_keys(m)
                ve.wait_ge(s["lc"], 2 * NCK * (pr + 1))
                ve.tensor_reduce(nmx[:, pr:pr + 1], L[pr % 2], AX.X, ALU.max, negate=True).then_inc(s["mx"], 1)
                ve.wait_ge(s["e"], pr + 1)
                ve.reciprocal(rden[:, pr:pr + 1], den[:, pr:pr + 1]).then_inc(s["rd"], 1)
                ve.wait_ge(s["rd"], pr + 1)
                ve.wait_ge(s["pv"], 2 * pr + 2)
                if pr >= 1:
                    ve.wait_ge(s["out0"], 16 * 8 * pr)
                ve.tensor_scalar(ob, ps[:, 7, 0:256], rden[:, pr:pr + 1], None, ALU.mult).then_inc(s["ob"], 1)

        @block.scalar
        def _(act):
            for pr in range(DB // 2):
                for m in range(2 * NCK * pr, 2 * NCK * (pr + 1)):
                    b, c = divmod(m, NCK)
                    rs = slice(HD * (b % 2), HD * (b % 2) + HD)
                    w = 512 if c < 4 else NS
                    act.wait_ge(s["mm"], m + 1)
                    if pr >= 2 and m == 2 * NCK * pr:
                        act.wait_ge(s["ptt"], NCK * (pr - 1))
                    act.activation(L[pr % 2][rs, c * 512:c * 512 + w], ps[rs, 4 + m % 2, 0:w], ACT.Copy).then_inc(s["lc"], 1)
                act.wait_ge(s["mx"], pr + 1)
                act.wait_ge(s["lc"], 2 * NCK * (pr + 1))
                act.activation(L[pr % 2], L[pr % 2], ACT.Exp, bias=nmx[:, pr:pr + 1], accum_out=den[:, pr:pr + 1]).then_inc(s["e"], 1)
                for c in range(NCK):
                    m = NCK * pr + c
                    act.wait_ge(s["ptt"], m + 1)
                    w, n = (P, 512) if c < 4 else (NS, P)
                    act.activation(PT[m % 2][0:w, 0:n], ps[0:w, 6 - c % 2, 0:n], ACT.Copy).then_inc(s["ptc"], 1)


NR = 4 + NE
O_RT = 46000
R_W1, R_W2, R_D1, R_D2, R_BE, R_TOK, R_CH, R_BUF, R_NU, R_LG = (O_RT + n for n in (0, 16, 32, 48, 64, 96, 128, 160, 192, 208))


def project_out(k):
    nc, t, ar, ps = k.nc, k.t, k.ar, k.ps
    A, R = ar.view(O_A, NT, 512), ar.view(O_R, NT, 512)
    o = O_R + NT * 512
    wo = ar.view(o, KD, D); o += KD * D
    gt, sc, sh = (ar.view(o + j * 2 * D, 2, D) for j in range(3)); o += 6 * D
    g2 = ar.view(o, D); o += D
    x = [ar.view(o + j * D, D) for j in range(2)]; o += 2 * D
    x1 = [ar.view(o + j * D, D) for j in range(2)]; o += 2 * D
    h2 = [ar.view(o + j * D, D) for j in range(2)]; o += 2 * D
    mT = [ar.view(o + j * D, KD, P) for j in range(2)]; o += 2 * D
    hT = [ar.view(o + j * D, KD, P) for j in range(2)]; o += 2 * D
    sq = ar.view(o, D); o += D
    wr = ar.view(o, KD, NR); o += KD * NR
    ss, rs, sd, tm = (ar.view(o + 16 * j, NT) for j in range(4)); o += 64
    assert o <= O_RT, o
    lg = ar.view(R_LG, NT, NR)
    names = "w0 w1 wr mod x0 x1 t1 m1 mm gx xo h t2 h2 rt ch ss ms sd".split()
    s = {n: k.sem("po_" + n) for n in names}
    s_x1o, s_h2o = [k.sem(f"po_x1o{b}") for b in range(2)], [k.sem(f"po_h2o{b}") for b in range(2)]
    OUT = (2, 3, 7)

    with nc.Block() as block:
        @block.sync
        def _(sp):
            for c in range(2):
                sp.dma_start(wo[:, :, c * 512:(c + 1) * 512], t["w_out"].rearrange("o (a p) n -> p (o a) n", p=P)[:, :, c * 512:(c + 1) * 512]).then_inc(s[f"w{c}"], 16)
            sp.dma_start(x[0], x_rows(t, 0)).then_inc(s["x0"], 16)
            sp.dma_start(x[1], x_rows(t, 1)).then_inc(s["x1"], 16)
            load_scale_shift(sp, k, s["mod"], (g2, t["norm2_g"]), [(gt, 2), (sc, 4), (sh, 3)])
            sp.dma_start(wr[:, :, 0:4], t["w_group"].rearrange("o (a p) n -> p (o a) n", p=P)).then_inc(s["wr"], 16)
            sp.dma_start(wr[:, :, 4:NR], t["w_expert_router"].rearrange("o (a p) n -> p (o a) n", p=P)).then_inc(s["wr"], 16)
            for i in range(2, NT):
                sp.wait_ge(s["xo"], i - 1)
                sp.dma_start(x[i % 2][0:ROWS[i], :], x_rows(t, i)).then_inc(s[f"x{i % 2}"], 16)
            sp.wait_ge(s["wr"], 32)

        @block.gpsimd
        def _(po):
            for i in range(NT):
                po.wait_ge(s["xo"], i + 1)
                po.dma_start(tile_rows(t["x1"], i), x1[i % 2][0:ROWS[i], :]).then_inc(s_x1o[i % 2], 16)
                po.wait_ge(s["h"], i + 1)
                po.dma_start(tile_rows(t["h2"], i), h2[i % 2][0:ROWS[i], :]).then_inc(s_h2o[i % 2], 16)
            for b in range(2):
                po.wait_ge(s_x1o[b], 16 * ((NT + 1 - b) // 2))
                po.wait_ge(s_h2o[b], 16 * ((NT + 1 - b) // 2))

        @block.scalar
        def _(act):
            def columns(i):
                r = ROWS[i]
                act.wait_ge(s["t1"], i + 1)
                if i >= 2:
                    act.wait_ge(s["mm"], 2 * (i - 1))
                act.activation(mT[i % 2][:, :, 0:r], ps[:, 0:2, :].rearrange("p b (a n) -> p (b a) n", n=P)[:, :, 0:r], ACT.Copy).then_inc(s["m1"], 1)

            columns(0)
            for i in range(NT + 1):
                if i + 1 < NT:
                    columns(i + 1)
                if i < NT:
                    r = ROWS[i]
                    act.wait_ge(s["xo"], i + 1)
                    if i >= 1:
                        act.wait_ge(s["ss"], i)
                    act.activation(sq[0:r, :], x1[i % 2][0:r, :], ACT.Square, accum_out=ss[0:r, i:i + 1]).then_inc(s["ss"], 1)
                    act.wait_ge(s["ms"], i + 1)
                    act.activation(sd[0:r, i:i + 1], ss[0:r, i:i + 1], ACT.Sqrt).then_inc(s["sd"], 1)
                if i >= 1:
                    j, r = i - 1, ROWS[i - 1]
                    act.wait_ge(s["t2"], j + 1)
                    if j >= 2:
                        act.wait_ge(s["rt"], j - 1)
                    act.activation(hT[j % 2][:, :, 0:r], ps[:, 4:6, :].rearrange("p b (a n) -> p (b a) n", n=P)[:, :, 0:r], ACT.Copy).then_inc(s["h2"], 1)

        @block.tensor
        def _(pe):
            def turn(i):
                r = ROWS[i]
                if i >= 1:
                    pe.wait_ge(s["m1"], i)
                for a in range(KD):
                    src = A if a < 4 else R
                    ins = pe.transpose(ps[:, a // 4, (a % 4) * P:(a % 4) * P + r], src[0:r, i, (a % 4) * P:(a % 4 + 1) * P], k.ident[0:r, 0:r])
                ins.then_inc(s["t1"], 1)

            def router(i):
                r = ROWS[i]
                pe.wait_ge(s["h2"], i + 1)
                for a in range(KD):
                    ins = pe.matmul(ps[0:r, 6, i * NR:(i + 1) * NR], hT[i % 2][:, a, 0:r], wr[:, a, :], start=(a == 0), stop=(a == KD - 1))
                ins.then_inc(s["rt"], 1)

            turn(0)
            for i in range(NT + 1):
                if i + 1 < NT:
                    turn(i + 1)
                if i < NT:
                    r = ROWS[i]
                    pe.wait_ge(s["m1"], i + 1)
                    for c in range(2):
                        n = 2 * i + c
                        if i == 0:
                            pe.wait_ge(s[f"w{c}"], 16)
                        if n >= 3:
                            pe.wait_ge(s["gx"], n - 2)
                        for a in range(KD):
                            ins = pe.matmul(ps[0:r, OUT[n % 3], :], mT[i % 2][:, a, 0:r], wo[:, a, c * 512:(c + 1) * 512], start=(a == 0), stop=(a == KD - 1))
                        ins.then_inc(s["mm"], 1)
                if i >= 1:
                    j, r = i - 1, ROWS[i - 1]
                    pe.wait_ge(s["h"], j + 1)
                    if j >= 1:
                        pe.wait_ge(s["h2"], j)
                    for a in range(KD):
                        ins = pe.transpose(ps[:, 4 + a // 4, (a % 4) * P:(a % 4) * P + r], h2[j % 2][0:r, a * P:(a + 1) * P], k.ident[0:r, 0:r])
                    ins.then_inc(s["t2"], 1)
                if i >= 2:
                    if i == 2:
                        pe.wait_ge(s["wr"], 32)
                    router(i - 2)
            router(NT - 1)

        @block.vector
        def _(ve):
            ch = Chain(ve, s["ch"])
            ve.wait_ge(s["mod"], 16 * 7)
            ch.step(ve.scalar_tensor_tensor(sc[:, 0, :], sc[:, 0, :], 1.0, g2, ALU.add, ALU.mult))
            ch.step(ve.scalar_tensor_tensor(sc[0:NS, 1, :], sc[0:NS, 1, :], 1.0, g2[0:NS, :], ALU.add, ALU.mult))
            for i in range(NT):
                r, m = ROWS[i], int(i == NT - 1)
                col = slice(i, i + 1)
                if i >= 2:
                    ve.wait_ge(s_x1o[i % 2], 16 * (i // 2))
                    ve.wait_ge(s["ss"], i - 1)
                for c in range(2):
                    n, cs = 2 * i + c, slice(c * 512, (c + 1) * 512)
                    ve.wait_ge(s["mm"], n + 1)
                    ve.tensor_tensor(x1[i % 2][0:r, cs], ps[0:r, OUT[n % 3], :], gt[0:r, m, cs], ALU.mult).then_inc(s["gx"], 1)
                ve.wait_ge(s["gx"], 2 * i + 2)
                ve.wait_ge(s[f"x{i % 2}"], 16 * (i // 2 + 1))
                ve.tensor_tensor(x1[i % 2][0:r, :], x1[i % 2][0:r, :], x[i % 2][0:r, :], ALU.add).then_inc(s["xo"], 1)
                ve.wait_ge(s["ss"], i + 1)
                ve.tensor_scalar(ss[0:r, col], ss[0:r, col], 1.0 / D, EPS, ALU.mult, ALU.add).then_inc(s["ms"], 1)
                ve.wait_ge(s["ms"], i + 1)
                rstd_steps(ch, ve, lambda: ve.wait_ge(s["sd"], i + 1), ss[0:r, col], rs[0:r, col], sd[0:r, col], tm[0:r, col])
                if i >= 2:
                    ve.wait_ge(s["t2"], i - 1)
                    ve.wait_ge(s_h2o[i % 2], 16 * (i // 2))
                ch.step(ve.scalar_tensor_tensor(h2[i % 2][0:r, :], x1[i % 2][0:r, :], rs[0:r, col], sc[0:r, m, :], ALU.mult, ALU.mult))
                ve.tensor_tensor(h2[i % 2][0:r, :], h2[i % 2][0:r, :], sh[0:r, m, :], ALU.add).then_inc(s["h"], 1)
            ch.step(ve.memset(lg, 0.0))
            ve.wait_ge(s["rt"], NT)
            ch.mark(ve.tensor_copy(lg[:, 0:NT - 1, :].rearrange("p a b -> p (a b)"), ps[:, 6, 0:(NT - 1) * NR]))
            ch.step(ve.tensor_copy(lg[0:NS, NT - 1, :], ps[0:NS, 6, (NT - 1) * NR:NT * NR]))


W_E = KD * FE
EX_END = 2 * 3 * W_E + 6 * D + 3 * FE


def expert_weights(t):
    w1, w3 = (t[n].rearrange("o e (a p) f -> p (o e) a f", p=P) for n in ("w1", "w3"))
    return (w1, FE), (w3, FE), (t["w2"].rearrange("o e (a p) d -> p (o e) a d", p=P), D)


def load_expert(sp, k, n, sem):
    be, chg, buf = (k.ar.view(a, NB, p=1, dt=I32) for a in (R_BE, R_CH, R_BUF))
    e = sp.value_load(be[0:1, bass.ds(n, 1)], min_val=0, max_val=NE - 1)
    at = sp.value_load(buf[0:1, bass.ds(n, 1)], min_val=0, max_val=1)
    new = sp.value_load(chg[0:1, bass.ds(n, 1)], min_val=0, max_val=1)
    Wt = k.ar.view(0, 2, 3 * W_E)
    for j, (src, wd) in enumerate(expert_weights(k.t)):
        dst = Wt[:, bass.ds(at, 1), j * W_E:(j + 1) * W_E].rearrange("p o (a f) -> p (o a) f", f=wd)
        sp.dma_start(dst, src[:, bass.ds(e, 1), :, :].rearrange("p o a f -> p (o a) f"), cond=new).then_inc(sem, 16)


def route(k):
    nc, t, ar, ps = k.nc, k.t, k.ar, k.ps
    lg = ar.view(R_LG, NT, NR)
    W = [ar.view(R_W1, NT), ar.view(R_W2, NT)]
    Dst = [ar.view(R_D1, NT, dt=I32), ar.view(R_D2, NT, dt=I32)]
    be, tok = ar.view(R_BE, NB, p=1, dt=I32), ar.view(R_TOK, NB, dt=I32)
    o = EX_END
    def new(*d, **kw):
        nonlocal o
        v = ar.view(o, *d, **kw)
        o += (int(np.prod(d)) + 15) // 16 * 16
        return v
    bias, cst = new(NR), new(256)
    pref, thr, iota_b, iota_p = cst[:, 0:4], cst[:, 16:16 + NT], cst[:, 32:32 + NB], cst[:, 128:256]
    gm, gs, gw, m1, m2, d21, den = (new(NT) for _ in range(7))
    ge, goh, eg, oh1, oh2, key = (new(NT, 4) for _ in range(6))
    tmp4 = new(NT, 4, 4)
    M1, M2 = new(NT, 4, 4), new(NT, 4, 4)
    M, Cs, rk, pr = new(NT, NE), new(NT + 1, NE), new(NT, NE), new(NT, NE)
    cnt, nb, ends, base, onesr = new(NE), new(NE), new(NE), new(NE), new(NE)
    cmpb, cmpe = new(NE, NT), new(NB, NE, p=1)
    bef, chf, flip, buff = (new(NB, p=1) for _ in range(4))
    chg, buf, used = ar.view(R_CH, NB, p=1, dt=I32), ar.view(R_BUF, NB, p=1, dt=I32), ar.view(R_NU, 1, p=1, dt=I32)
    df = [new(NT), new(NT)]
    ones = new(P)
    tid = new(NT)
    ends_b, past = new(NB), new(NT, NB)
    place, block_f = new(2, NT), new(2, NT)
    oh_place, oh_block = [new(NT, P) for _ in range(2)], [new(NT, NB) for _ in range(2)]
    names = "c ch a1 a2 m rk tok oh tables w".split()
    s = {n: k.sem("ro_" + n) for n in names}

    with nc.Block() as block:
        @block.sync
        def _(sp):
            sp.dma_start(cst, t["k_route"].broadcast_to([P, 256])).then_inc(s["c"], 16)
            sp.dma_start(bias[:, 0:4], t["b_group"].broadcast_to([P, 4])).then_inc(s["c"], 16)
            sp.dma_start(bias[:, 4:NR], t["b_expert_router"].broadcast_to([P, NE])).then_inc(s["c"], 16)
            sp.dma_start(tid, t["k_tid"]).then_inc(s["c"], 16)
            sp.wait_ge(s["tables"], 1)
            load_expert(sp, k, 0, s["w"])
            sp.wait_ge(s["w"], 48)

        @block.scalar
        def _(act):
            act.wait_ge(s["a1"], 1)
            act.activation(ge, ge, ACT.Exp).then_inc(s["a2"], 1)
            act.wait_ge(s["a1"], 2)
            act.activation(d21, d21, ACT.Exp).then_inc(s["a2"], 1)

        @block.tensor
        def _(pe):
            pe.wait_ge(s["m"], 1)
            pe.matmul(ps[:, 0, 0:NT * NE], k.tri, M.rearrange("p a b -> p (a b)"), start=True, stop=False)
            pe.matmul(ps[:, 0, 0:NT * NE], ones, Cs[:, 0:NT, :].rearrange("p a b -> p (a b)"), start=False, stop=True)
            pe.matmul(ps[:, 1, 0:NE], ones, Cs[:, NT, :], start=True, stop=True).then_inc(s["rk"], 1)
            for j in range(2):
                pe.wait_ge(s["oh"], j + 1)
                for i in range(NT):
                    r = ROWS[i]
                    ins = pe.matmul(ps[:, 2, 0:NB], oh_place[j][0:r, i, :], oh_block[j][0:r, i, :], start=(j == 0 and i == 0), stop=(j == 1 and i == NT - 1))
            ins.then_inc(s["tok"], 1)

        @block.vector
        def _(ve):
            ch = Chain(ve, s["ch"])
            tt, ts = ve.tensor_tensor, ve.tensor_scalar
            ch.mark(ve.memset(ones, 1.0))
            ch.mark(ve.memset(onesr, 1.0))
            ch.mark(ve.memset(Cs, 0.0))
            ch.mark(ve.memset(chf, 1.0))
            ve.wait_ge(s["c"], 64)
            ch.mark(ts(ends_b, iota_b, float(P), float(P), ALU.mult, ALU.add))
            ch.step(tt(lg, lg, bias.unsqueeze(1).broadcast_to([P, NT, NR]), ALU.add))

            def wide(v):
                return v.unsqueeze(2).broadcast_to([P, NT, 4])

            def first_max(x, mx, oh):
                ch.step(ve.tensor_reduce(mx, x, AX.X, ALU.max))
                ch.step(tt(key, x, wide(mx), ALU.is_equal))
                ch.step(tt(key, key, pref.unsqueeze(1).broadcast_to([P, NT, 4]), ALU.mult))
                ch.step(ve.tensor_reduce(gs, key, AX.X, ALU.max))
                ch.step(tt(oh, key, wide(gs), ALU.is_equal))

            gl = lg[:, :, 0:4]
            el = lg[:, :, 4:NR].rearrange("p a (g e) -> p a g e", e=4)
            first_max(gl, gm, goh)
            tt(ge, gl, wide(gm), ALU.subtract).then_inc(s["a1"], 1)
            ch.step(tt(tmp4, el, goh.unsqueeze(3).broadcast_to([P, NT, 4, 4]), ALU.mult))
            ch.step(ve.tensor_reduce(eg, tmp4.rearrange("p a g e -> p a e g"), AX.X, ALU.add))
            first_max(eg, m1, oh1)
            ch.step(ve.scalar_tensor_tensor(eg, oh1, OFF, eg, ALU.mult, ALU.add))
            first_max(eg, m2, oh2)
            tt(d21, m2, m1, ALU.subtract).then_inc(s["a1"], 1)
            for Mj, oh in ((M1, oh1), (M2, oh2)):
                ch.step(tt(Mj, goh.unsqueeze(3).broadcast_to([P, NT, 4, 4]), oh.unsqueeze(2).broadcast_to([P, NT, 4, 4]), ALU.mult))
                ch.step(ve.memset(Mj[NS:P, NT - 1, :, :], 0.0))
            f1, f2 = (x.rearrange("p a g e -> p a (g e)") for x in (M1, M2))
            ch.step(tt(M, f1, f2, ALU.add))
            for i in range(NT):
                ch.step(tt(Cs[:, i + 1, :], Cs[:, i, :], M[:, i, :], ALU.add))
            ve.sem_inc(s["m"], 1)
            ve.wait_ge(s["a2"], 2)
            ch.step(ve.tensor_reduce(gs, ge, AX.X, ALU.add))
            ch.step(ve.reciprocal(gw, gs))
            ch.step(ts(den, d21, 1.0, None, ALU.add))
            ch.step(ve.reciprocal(gs, den))
            ch.step(tt(W[0], gw, gs, ALU.mult))
            ch.step(tt(W[1], W[0], d21, ALU.mult))
            ve.wait_ge(s["rk"], 1)
            ch.mark(ve.tensor_copy(rk.rearrange("p a b -> p (a b)"), ps[:, 0, 0:NT * NE]))
            ch.step(ve.tensor_copy(cnt, ps[:, 1, 0:NE]))
            ch.step(tt(cmpb, cnt.unsqueeze(2).broadcast_to([P, NE, NT]), thr.unsqueeze(1).broadcast_to([P, NE, NT]), ALU.is_gt))
            ch.step(ve.tensor_reduce(nb, cmpb, AX.X, ALU.add))
            ch.step(ve.tensor_tensor_scan(ends, onesr, nb, 0.0, ALU.mult, ALU.add))
            ch.step(tt(cmpe, iota_b[0:1, :].unsqueeze(2).broadcast_to([1, NB, NE]), ends[0:1, :].unsqueeze(1).broadcast_to([1, NB, NE]), ALU.is_ge))
            ch.step(ve.tensor_reduce(bef, cmpe, AX.X, ALU.add))
            ch.step(ts(bef, bef, float(NE - 1), None, ALU.min))
            ch.step(ve.tensor_copy(be, bef))
            ch.step(tt(chf[:, 1:NB], bef[:, 1:NB], bef[:, 0:NB - 1], ALU.not_equal))
            ch.step(ts(flip, chf, -2.0, 1.0, ALU.mult, ALU.add))
            ch.step(ve.tensor_tensor_scan(buff, flip, chf, 1.0, ALU.mult, ALU.add))
            ch.mark(ve.tensor_copy(chg, chf))
            ch.mark(ve.tensor_copy(buf, buff))
            ch.step(ve.tensor_copy(used, ends[0:1, NE - 1:NE]))
            ve.sem_inc(s["tables"], 1)
            ch.step(tt(base, ends, nb, ALU.subtract))
            ch.step(ts(base, base, float(P), None, ALU.mult))
            ch.step(tt(rk, rk, base.unsqueeze(1).broadcast_to([P, NT, NE]), ALU.add))
            for j, f in enumerate((f1, f2)):
                ch.step(tt(pr, rk, f, ALU.mult))
                ch.step(ve.tensor_reduce(df[j], pr, AX.X, ALU.add))
                ch.step(ve.tensor_copy(Dst[j], df[j]))
                ch.step(tt(past, df[j].unsqueeze(2).broadcast_to([P, NT, NB]), ends_b.unsqueeze(1).broadcast_to([P, NT, NB]), ALU.is_ge))
                ch.step(ve.tensor_reduce(block_f[:, j, :], past, AX.X, ALU.add))
                ch.step(ve.scalar_tensor_tensor(place[:, j, :], block_f[:, j, :], -float(P), df[j], ALU.mult, ALU.add))
                ch.mark(tt(oh_place[j], iota_p.unsqueeze(1).broadcast_to([P, NT, P]), place[:, j, :].unsqueeze(2).broadcast_to([P, NT, P]), ALU.is_equal))
                ch.step(tt(oh_block[j], iota_b.unsqueeze(1).broadcast_to([P, NT, NB]), block_f[:, j, :].unsqueeze(2).broadcast_to([P, NT, NB]), ALU.is_equal))
                tt(oh_block[j], oh_block[j], tid.unsqueeze(2).broadcast_to([P, NT, NB]), ALU.mult).then_inc(s["oh"], 1)
            ve.wait_ge(s["tok"], 1)
            ch.step(ve.tensor_copy(tok, ps[:, 2, 0:NB]))


def combine_inputs(k):
    o = EX_END
    gt, sc, sh = (k.ar.view(o + j * 2 * D, 2, D) for j in range(3))
    g = k.ar.view(o + 6 * D, D)
    o += 7 * D
    early = (O_RT - o) // D
    x1 = [k.ar.view(o + i * D if i < early else (i - early) * D, D) for i in range(NT)]
    return gt, sc, sh, g, x1, early


def experts(k):
    nc, t, ar, ps = k.nc, k.t, k.ar, k.ps
    tok, buf, used = ar.view(R_TOK, NB, dt=I32), ar.view(R_BUF, NB, p=1, dt=I32), ar.view(R_NU, 1, p=1, dt=I32)
    SURE = A_TOT // P // 2 * 2
    Wt = ar.view(0, 2, 3 * W_E)
    o = 2 * 3 * W_E
    X = [ar.view(o + b * D, D) for b in range(2)]; o += 2 * D
    XT = [ar.view(o + b * D, KD, P) for b in range(2)]; o += 2 * D
    sg, hh = ar.view(o, FE), ar.view(o + FE, FE); o += 2 * FE
    hT = ar.view(o, 4, P); o += 512
    Y = [ar.view(o + b * D, D) for b in range(2)]; o += 2 * D
    assert o == EX_END
    names = "t xt g u sg h ht htc y yc next".split()
    s = {n: k.sem("ex_" + n) for n in names}
    s_w, s_x, s_yo = ([k.sem(f"ex_{n}{b}") for b in range(2)] for n in ("w", "x", "yo"))

    def loops(eng, body, otherwise=None):
        count = eng.value_load(used, min_val=0, max_val=NB)
        for b in range(2):
            body(b, b, True)
        with eng.Fori(1, SURE // 2) as i:
            for b in range(2):
                body(2 * i + b, b, False)
        with eng.Fori(SURE // 2, NB // 2) as i:
            for b in range(2):
                with eng.If(count > 2 * i + b):
                    body(2 * i + b, b, False)
                if otherwise:
                    with eng.Else():
                        otherwise(2 * i + b, b)

    with nc.Block() as block:
        @block.sync
        def _(sp):
            def body(n, b, first):
                if not first:
                    sp.wait_ge(s["y"], n - 1)
                if not (isinstance(n, int) and n == 0):
                    load_expert(sp, k, n, s_w[b])
            loops(sp, body)

        @block.gpsimd
        def _(po):
            count = po.value_load(used, min_val=0, max_val=NB)

            def body(n, b, first):
                if not first:
                    po.wait_ge(s["t"], n - 1)
                po.indirect_dma_start(X[b], None, t["h2"], bass.IndirectOffsetOnAxis(ap=tok[:, n % NB:n % NB + 1], axis=0)).then_inc(s_x[b], 16)
            gt, sc, sh, g, x1, early = combine_inputs(k)
            ahead = scale_shift_parts(k, (g, t["final_g"].rearrange("(o n) -> o n", o=1)), [(gt, 5), (sc, 7), (sh, 6)])
            ahead += [(x1[i], tile_rows(t["x1"], i)) for i in range(early)]
            assert len(ahead) < SURE
            for n in range(NB + 1):
                if 2 <= n < 2 + len(ahead):
                    po.dma_start(*ahead[n - 2]).then_inc(s["next"], 16)
                if n <= SURE:
                    body(n, n % 2, n < 2)
                else:
                    with po.If(count + 1 > n):
                        body(n, n % 2, False)
            po.wait_ge(s["next"], 16 * len(ahead))

        @block.tensor
        def _(pe):
            def turn(b, half):
                for a in range(4 * half, 4 * half + 4):
                    ins = pe.transpose(ps[:, half, (a % 4) * P:(a % 4 + 1) * P], X[b][:, a * P:(a + 1) * P], k.ident)
                if half:
                    ins.then_inc(s["t"], 1)

            def body(n, i, b):
                at = pe.value_load(buf[0:1, bass.ds(n, 1)], min_val=0, max_val=1)

                def w(off, width):
                    return Wt[:, bass.ds(at, 1), off:off + width].rearrange("p o a -> p (o a)")

                if not (isinstance(n, int) and n == 0):
                    pe.wait_ge(s_w[b], (i + b) * 48)
                pe.wait_ge(s["xt"], n + 1)
                if not (isinstance(n, int) and n == 0):
                    pe.wait_ge(s["h"], n)
                for m in range(2):
                    for a in range(KD):
                        ins = pe.matmul(ps[:, 2 + m, :], XT[b][:, a, :], w(m * 4096 + a * FE, FE), start=(a == 0), stop=(a == KD - 1))
                    ins.then_inc(s["gu"[m]], 1)
                pe.wait_ge(s_x[1 - b], (i + 1 + b) * 16)
                turn(1 - b, 0)
                pe.wait_ge(s["h"], n + 1)
                for a in range(4):
                    ins = pe.transpose(ps[:, 4, a * P:(a + 1) * P], hh[:, a * P:(a + 1) * P], k.ident)
                ins.then_inc(s["ht"], 1)
                turn(1 - b, 1)
                pe.wait_ge(s["htc"], n + 1)
                if not (isinstance(n, int) and n == 0):
                    pe.wait_ge(s["yc"], n)
                for c in range(2):
                    for a in range(4):
                        ins = pe.matmul(ps[:, 5 + c, :], hT[:, a, :], w(8192 + a * D + c * 512, 512), start=(a == 0), stop=(a == 3))
                ins.then_inc(s["y"], 1)

            count = pe.value_load(used, min_val=0, max_val=NB)
            pe.wait_ge(s_x[0], 16)
            turn(0, 0)
            turn(0, 1)
            body(0, 0, 0)
            body(1, 0, 1)
            with pe.Fori(1, SURE // 2) as i:
                body(2 * i, i, 0)
                body(2 * i + 1, i, 1)
            with pe.Fori(SURE // 2, NB // 2) as i:
                for b in range(2):
                    with pe.If(count > 2 * i + b):
                        body(2 * i + b, i, b)

        @block.scalar
        def _(act):
            def body(n, b, first):
                act.wait_ge(s["g"], n + 1)
                if not (isinstance(n, int) and n == 0):
                    act.wait_ge(s["h"], n)
                act.activation(sg, ps[:, 2, :], ACT.Silu).then_inc(s["sg"], 1)
                act.wait_ge(s["y"], n + 1)
                if not first:
                    act.wait_ge(s_yo[b], (n - b) * 8)
                act.activation(Y[b], ps[:, 5:7, :].rearrange("p a b -> p (a b)"), ACT.Copy).then_inc(s["yc"], 1)
                act.wait_ge(s["yc"], n + 1)
                act.dma_start(t["yslot"][bass.ds(n * P, P), :], Y[b]).then_inc(s_yo[b], 16)
            def unused(n, b):
                act.dma_start(t["yslot"][bass.ds(n * P, P), :], Y[b]).then_inc(s_yo[b], 16)

            loops(act, body, unused)
            for b in range(2):
                act.wait_ge(s_yo[b], 16 * NB // 2)

        @block.vector
        def _(ve):
            def columns(n, b):
                ve.wait_ge(s["t"], n + 1)
                ve.tensor_copy(XT[b].rearrange("p a b -> p (a b)"), ps[:, 0:2, :].rearrange("p a b -> p (a b)")).then_inc(s["xt"], 1)

            def body(n, b, first):
                ve.wait_ge(s["sg"], n + 1)
                ve.wait_ge(s["u"], n + 1)
                if not (isinstance(n, int) and n == 0):
                    ve.wait_ge(s["ht"], n)
                ve.tensor_tensor(hh, sg, ps[:, 3, :], ALU.mult).then_inc(s["h"], 1)
                ve.wait_ge(s["ht"], n + 1)
                if not (isinstance(n, int) and n == 0):
                    ve.wait_ge(s["y"], n)
                ve.tensor_copy(hT.rearrange("p a b -> p (a b)"), ps[:, 4, :]).then_inc(s["htc"], 1)
                columns(n + 1, 1 - b)

            columns(0, 0)
            loops(ve, body)


def combine(k):
    nc, t, ar, ps = k.nc, k.t, k.ar, k.ps
    W = [ar.view(R_W1, NT), ar.view(R_W2, NT)]
    Dst = [ar.view(R_D1, NT, dt=I32), ar.view(R_D2, NT, dt=I32)]
    gt, sc, sh, g, x1, early = combine_inputs(k)
    o = (NT - early) * D
    ya, yb = (ar.view(o + j * NT * D, NT, D) for j in range(2)); o += 2 * NT * D
    NBF = 3
    out = [ar.view(o + j * D, D) for j in range(NBF)]; o += NBF * D
    sq = ar.view(o, D); o += D
    ss, rs, sd, tm = (ar.view(o + 16 * j, NT) for j in range(4)); o += 64
    s = {n: k.sem("co_" + n) for n in "ss ms sd ch done res first scaled".split()}
    assert o <= EX_END, o
    s_x, s_a, s_b = ([k.sem(f"co_{n}{b}") for b in range(NT)] for n in ("x", "a", "b"))
    s_o = [k.sem(f"co_o{b}") for b in range(NBF)]

    with nc.Block() as block:
        @block.sync
        def _(sp):
            for i in range(early, NT):
                sp.dma_start(x1[i][0:ROWS[i], :], tile_rows(t["x1"], i)).then_inc(s_x[i], 16)
            for j in range(NT):
                sp.wait_ge(s["done"], j + 1)
                dst = t["y_prompt"].rearrange("o s d -> (o s) d")[j * P:(j + 1) * P, :] if j < NT - 1 else t["y_sample"].rearrange("b s d -> (b s) d")
                sp.dma_start(dst, out[j % NBF][0:ROWS[j], :]).then_inc(s_o[j % NBF], 16)
            for b in range(NBF):
                sp.wait_ge(s_o[b], 16 * ((NT + NBF - 1 - b) // NBF))

        @block.gpsimd
        def _(po):
            for i in range(NT):
                r = ROWS[i]
                for y, sm, d in ((ya, s_a, Dst[0]), (yb, s_b, Dst[1])):
                    po.indirect_dma_start(y[0:r, i, :], None, t["yslot"], bass.IndirectOffsetOnAxis(ap=d[0:r, i:i + 1], axis=0)).then_inc(sm[i], 16)
            for i in range(NT):
                r, m, b = ROWS[i], int(i == NT - 1), i % NBF
                po.wait_ge(s["scaled"], i + 1)
                po.tensor_tensor(out[b][0:r, :], out[b][0:r, :], sh[0:r, m, :], ALU.add).then_inc(s["done"], 1)

        @block.scalar
        def _(act):
            def first(i):
                r = ROWS[i]
                act.wait_ge(s_a[i], 16)
                act.activation(ya[0:r, i, :], ya[0:r, i, :], ACT.Copy, scale=W[0][0:r, i:i + 1]).then_inc(s["first"], 1)

            first(0)
            for i in range(NT):
                r = ROWS[i]
                if i + 1 < NT:
                    first(i + 1)
                act.wait_ge(s["res"], i + 1)
                if i >= 1:
                    act.wait_ge(s["ss"], i)
                act.activation(sq[0:r, :], x1[i][0:r, :], ACT.Square, accum_out=ss[0:r, i:i + 1]).then_inc(s["ss"], 1)
                act.wait_ge(s["ms"], i + 1)
                act.activation(sd[0:r, i:i + 1], ss[0:r, i:i + 1], ACT.Sqrt).then_inc(s["sd"], 1)

        @block.vector
        def _(ve):
            ch = Chain(ve, s["ch"])
            ch.step(ve.scalar_tensor_tensor(sc[:, 0, :], sc[:, 0, :], 1.0, g, ALU.add, ALU.mult))
            ch.step(ve.scalar_tensor_tensor(sc[0:NS, 1, :], sc[0:NS, 1, :], 1.0, g[0:NS, :], ALU.add, ALU.mult))

            def residual(i):
                r, m, col = ROWS[i], int(i == NT - 1), slice(i, i + 1)
                a_, b_, x_ = ya[0:r, i, :], yb[0:r, i, :], x1[i][0:r, :]
                ve.wait_ge(s["first"], i + 1)
                ve.wait_ge(s_b[i], 16)
                ch.step(ve.scalar_tensor_tensor(a_, b_, W[1][0:r, col], a_, ALU.mult, ALU.add))
                ch.step(ve.tensor_tensor(a_, a_, gt[0:r, m, :], ALU.mult))
                if i >= early:
                    ve.wait_ge(s_x[i], 16)
                ve.tensor_tensor(x_, x_, a_, ALU.add).then_inc(s["res"], 1)

            def norm(i):
                r, m, b, col = ROWS[i], int(i == NT - 1), i % NBF, slice(i, i + 1)
                ve.wait_ge(s["ss"], i + 1)
                ve.tensor_scalar(ss[0:r, col], ss[0:r, col], 1.0 / D, EPS, ALU.mult, ALU.add).then_inc(s["ms"], 1)
                ve.wait_ge(s["ms"], i + 1)
                rstd_steps(ch, ve, lambda: ve.wait_ge(s["sd"], i + 1), ss[0:r, col], rs[0:r, col], sd[0:r, col], tm[0:r, col])
                if i >= NBF:
                    ve.wait_ge(s_o[b], 16 * (i // NBF))
                ve.scalar_tensor_tensor(out[b][0:r, :], x1[i][0:r, :], rs[0:r, col], sc[0:r, m, :], ALU.mult, ALU.mult).then_inc(s["scaled"], 1)

            residual(0)
            for i in range(NT):
                if i + 1 < NT:
                    residual(i + 1)
                norm(i)


_INS = ["x_prompt", "x_sample", "cache_k", "cache_v", "cache_kidx", "state_hgrn", "page_table", "c_prompt",
        "c_sample", "ada_w", "ada_b", "norm1_g", "norm2_g", "w_in", "idx_k_g", "hg_lb_logits", "attn_out_g",
        "hg_out_g", "w_out", "w_group", "b_group", "w_expert_router", "b_expert_router", "w1", "w3", "w2",
        "final_g", "ada_final_w", "ada_final_b"]
_OUTS = [("y_prompt", (1, SEQ, D)), ("y_sample", (DB, DS, D)),
         ("k_prompt", (1, 1, SEQ, HKV, HD)), ("v_prompt", (1, 1, SEQ, HKV, HD)), ("kidx_prompt", (1, 1, SEQ, HD)),
         ("hgrn_prompt", (1, 1, GH, DK, DK)),
         ("k_sample", (1, DB, DS, HKV, HD)), ("v_sample", (1, DB, DS, HKV, HD)), ("kidx_sample", (1, DB, DS, HD)),
         ("hgrn_sample", (1, DB, GH, DK, DK))]
_SCRATCH = [("mod", (1 + DB, 8 * D), F32), ("wi", (NS, IH), F32), ("att", (NS, 512), F32),
            ("x1", (T, D), F32), ("h2", (T, D), F32), ("hq", (P, GH, T), F32), ("hf", (P, GH, T), F32), ("hv", (P, NT, 512), F32), ("hg", (P, NT, 512), F32),
            ("yslot", (NB * P, D), F32)]


def constants():
    p = np.arange(P)
    half = ROT // 2
    inv = (np.float32(THETA) ** (-np.arange(half, dtype=np.float32) * np.float32(2.0 / ROT))).astype(np.float32)
    pos = np.concatenate([np.arange(SEQ), PAST + p % DS]).astype(np.float32).reshape(NT, P)
    ang = (pos[:, :, None] * inv).astype(np.float32)
    rope = np.stack([np.cos(ang), np.sin(ang)], 2).transpose(1, 0, 2, 3)
    tri = (p[:, None] < p[None, :])
    causal = np.where(p[None, :] <= p[:, None], 0.0, NEG)
    small = np.zeros((P, 64))
    for j in range(DS):
        small[:, j] = np.where(j <= p % DS, 0.0, NEG)
    small[:, 8] = p % 8
    small[:, 9] = p
    small[:, 10:18] = (p[:, None] // DS == np.arange(DB)[None, :])
    cols = np.arange(T)
    reset = np.where(cols < SEQ, cols % C != 0, cols % DS != 0)[None, :]
    q = np.arange(C)
    m0 = np.tile(p[:, None] % C <= q[None, :], (1, 4))
    m1 = np.tile((p[:, None] <= q) & (p[:, None] // DS == q // DS), (1, 4))
    qmask = (np.arange(DB)[:, None] == np.arange(NS)[None, :] // DS).reshape(1, -1)
    r = np.arange(NS)
    sq = np.arange(DB)[:, None] * DS
    rsel = r[:, None, None] == (sq + (r % DS)[None, :])[None]
    msel = np.stack([(r[None, :] == (b * DS + r % DS)[:, None]) for b in range(DB)], 1)
    rt = np.zeros((1, 256))
    rt[0, 0:4] = [4, 3, 2, 1]
    rt[0, 16:16 + NT] = np.arange(NT) * P
    rt[0, 32:32 + NB] = np.arange(NB)
    rt[0, 128:] = p
    tid = np.arange(NT)[None, :] * P + p[:, None]
    return {"k_route": rt, "k_tid": tid, "k_rsel": rsel.reshape(NS, -1), "k_msel": msel.reshape(NS, -1), "k_reset": reset, "k_masks": np.concatenate([m0, m1], 1), "k_qmask": qmask, "k_ident": np.eye(P), "k_rope": rope.reshape(P, -1), "k_tri": tri, "k_causal": causal, "k_small": small}


def kernel(**inputs):
    import concourse.bacc as _bacc
    from concourse.bass_utils import run_bass_kernel_spmd as _run

    nc = _bacc.Bacc("TRN2", target_bir_lowering=False, num_devices=1)
    arrays, t = {}, {}
    for name in _INS:
        a = np.ascontiguousarray(inputs[name])
        arrays["in_" + name] = a
        t[name] = nc.dram_tensor("in_" + name, a.shape, mybir.dt.from_np(a.dtype), kind="ExternalInput").ap()
    for name, a in constants().items():
        a = np.ascontiguousarray(a, np.float32)
        arrays[name] = a
        t[name] = nc.dram_tensor(name, a.shape, F32, kind="ExternalInput").ap()
    for name, shape in _OUTS:
        t[name] = nc.dram_tensor("out_" + name, shape, F32, kind="ExternalOutput").ap()
    for name, shape, dt in _SCRATCH:
        t[name] = nc.dram_tensor("tmp_" + name, shape, dt, kind="Internal").ap()
    build(nc, t)
    r = _run(nc, [arrays], core_ids=[0])
    return tuple(r.results[0]["out_" + name] for name, _ in _OUTS)
```
